# Optimizing a Trainium2 kernel written in Bass

```python
import math
import jax, jax.numpy as jnp
from jax import lax
import numpy as np

D_MODEL = 2048
BATCH = 1
SEQ = 256
DEPTH = 1

HEAD_DIM = 128
MOBA_HEADS = 8
MOBA_WIDTH = MOBA_HEADS * HEAD_DIM
MOBA_BLOCK = 256
MOBA_TOPK = 3
MOBA_Q_CHUNK = 16
DN_HEADS = 8
DN_WIDTH = DN_HEADS * HEAD_DIM
DN_CONV = 4
DN_CHUNK = 64
NORM_EPS = 1e-6
IN_SPLITS = (MOBA_WIDTH, MOBA_WIDTH, MOBA_WIDTH, MOBA_WIDTH,
             3 * DN_WIDTH, DN_WIDTH,
             DN_HEADS, DN_HEADS,
             D_MODEL, D_MODEL)
IN_WIDTH = sum(IN_SPLITS)

kernel_name = "moba_gated_deltanet_hybrid"

def rms_norm(x, gain):
    xf = x.astype(jnp.float32)
    y = xf * lax.rsqrt(jnp.mean(xf * xf, axis=-1, keepdims=True) + NORM_EPS)
    return (y * gain.astype(jnp.float32)).astype(x.dtype)

def l2_normalize(x):
    return x * lax.rsqrt(jnp.sum(x * x, axis=-1, keepdims=True) + NORM_EPS)

def alibi_slopes(n_heads):
    return jnp.exp2(-8.0 * jnp.arange(1, n_heads + 1, dtype=jnp.float32) / n_heads)

def moba_attention(q, k, v):
    b, s, nh, dh = q.shape
    q = jnp.swapaxes(q, 1, 2) * dh ** -0.5
    k = jnp.swapaxes(k, 1, 2)
    v = jnp.swapaxes(v, 1, 2)
    n_blk = -(-s // MOBA_BLOCK)
    pad = n_blk * MOBA_BLOCK - s
    k = jnp.pad(k, ((0, 0), (0, 0), (0, pad), (0, 0)))
    v = jnp.pad(v, ((0, 0), (0, 0), (0, pad), (0, 0)))
    kb = k.reshape(b, nh, n_blk, MOBA_BLOCK, dh)
    vb = v.reshape(b, nh, n_blk, MOBA_BLOCK, dh)
    slopes = alibi_slopes(nh)[None, :, None, None]
    n_top = min(MOBA_TOPK, n_blk - 1)
    n_chunk = s // MOBA_Q_CHUNK
    cq = MOBA_Q_CHUNK
    qc = q.reshape(b, nh, n_chunk, cq, dh).transpose(2, 0, 1, 3, 4)
    starts = jnp.arange(n_chunk, dtype=jnp.int32) * cq
    offs_blk = jnp.arange(MOBA_BLOCK, dtype=jnp.int32)
    bi = jnp.arange(b)[:, None, None]
    hi = jnp.arange(nh)[None, :, None]

    if n_top > 0:
        k_mean = jnp.mean(kb.astype(jnp.float32), axis=3)
        gate = jnp.einsum('bhsd,bhnd->bhsn', q.astype(jnp.float32), k_mean)
        q_blk = jnp.arange(s, dtype=jnp.int32) // MOBA_BLOCK
        past = jnp.arange(n_blk, dtype=jnp.int32)[None, :] < q_blk[:, None]
        gate = jnp.where(past, gate, -jnp.inf)
        _, top_idx = lax.top_k(gate, n_top)
        top_valid = top_idx < q_blk[:, None]
        idx_c = top_idx.reshape(b, nh, n_chunk, cq, n_top).transpose(2, 0, 1, 3, 4)
        valid_c = top_valid.reshape(b, nh, n_chunk, cq, n_top).transpose(2, 0, 1, 3, 4)
        xs = (qc, starts, idx_c, valid_c)
    else:
        xs = (qc, starts)

    def chunk_fn(args):
        qi, start = args[0], args[1]
        t = start + jnp.arange(cq, dtype=jnp.int32)
        blk = start // MOBA_BLOCK
        ko = lax.dynamic_index_in_dim(kb, blk, axis=2, keepdims=False)
        vo = lax.dynamic_index_in_dim(vb, blk, axis=2, keepdims=False)
        pos_o = blk * MOBA_BLOCK + offs_blk
        dist_o = (t[:, None] - pos_o[None, :]).astype(jnp.float32)
        lo = jnp.einsum('bhqd,bhkd->bhqk', qi, ko).astype(jnp.float32) - slopes * dist_o
        lo = jnp.where((pos_o[None, :] <= t[:, None])[None, None], lo, -jnp.inf)
        if n_top > 0:
            idx, valid = args[2], args[3]
            gidx = idx.reshape(b, nh, cq * n_top)
            kp = kb[bi, hi, gidx].reshape(b, nh, cq, n_top * MOBA_BLOCK, dh)
            vp = vb[bi, hi, gidx].reshape(b, nh, cq, n_top * MOBA_BLOCK, dh)
            pos_p = (idx[..., None] * MOBA_BLOCK + offs_blk).reshape(b, nh, cq, n_top * MOBA_BLOCK)
            dist_p = (t[None, None, :, None] - pos_p).astype(jnp.float32)
            lp = jnp.einsum('bhqd,bhqkd->bhqk', qi, kp).astype(jnp.float32) - slopes * dist_p
            lp = jnp.where(jnp.repeat(valid, MOBA_BLOCK, axis=-1), lp, -jnp.inf)
            p = jax.nn.softmax(jnp.concatenate([lp, lo], axis=-1), axis=-1).astype(vb.dtype)
            n_p = n_top * MOBA_BLOCK
            out = (jnp.einsum('bhqk,bhqkd->bhqd', p[..., :n_p], vp)
                   + jnp.einsum('bhqk,bhkd->bhqd', p[..., n_p:], vo))
        else:
            p = jax.nn.softmax(lo, axis=-1).astype(vb.dtype)
            out = jnp.einsum('bhqk,bhkd->bhqd', p, vo)
        return out

    out = lax.map(chunk_fn, xs)
    return out.transpose(1, 0, 3, 2, 4).reshape(b, s, nh * dh)

def short_conv(u, w):
    c = u.shape[-1]
    y = lax.conv_general_dilated(u, w[:, None, :].astype(u.dtype), window_strides=(1,),
                                 padding=[(DN_CONV - 1, 0)],
                                 dimension_numbers=('NWC', 'WIO', 'NWC'),
                                 feature_group_count=c)
    return jax.nn.silu(y)

def gated_delta_rule(q, k, v, g, beta):
    b, nh, s, dk = q.shape
    dv = v.shape[-1]
    c = DN_CHUNK
    n = s // c
    q = l2_normalize(q) * dk ** -0.5
    k = l2_normalize(k)
    q = q.reshape(b, nh, n, c, dk)
    k = k.reshape(b, nh, n, c, dk)
    v = v.reshape(b, nh, n, c, dv)
    g = jnp.cumsum(g.reshape(b, nh, n, c), axis=-1)
    beta = beta.reshape(b, nh, n, c)[..., None]
    kb = k * beta
    vb = v * beta
    causal = jnp.tril(jnp.ones((c, c), dtype=bool))
    strict = jnp.tril(jnp.ones((c, c), dtype=bool), -1)
    decay = jnp.exp(jnp.where(causal, g[..., :, None] - g[..., None, :], -jnp.inf))
    lower = jnp.where(strict, jnp.einsum('bhnid,bhnjd->bhnij', kb, k) * decay, 0.0)
    eye = jnp.eye(c, dtype=jnp.float32)
    tmat = lax.linalg.triangular_solve(eye + lower, jnp.broadcast_to(eye, lower.shape),
                                       left_side=True, lower=True, unit_diagonal=True)
    u = tmat @ vb
    w = tmat @ (kb * jnp.exp(g)[..., None])
    intra = jnp.where(causal, jnp.einsum('bhnid,bhnjd->bhnij', q, k) * decay, 0.0)

    def step(state, xs):
        qi, ki, ui, wi, gi, ai = xs
        v_new = ui - wi @ state
        out = (qi * jnp.exp(gi)[..., None]) @ state + ai @ v_new
        g_last = gi[..., -1:]
        state = (state * jnp.exp(g_last)[..., None]
                 + jnp.einsum('bhck,bhcv->bhkv', ki * jnp.exp(g_last - gi)[..., None], v_new))
        return state, out

    xs = tuple(jnp.moveaxis(t, 2, 0) for t in (q, k, u, w, g, intra))
    state0 = jnp.zeros((b, nh, dk, dv), jnp.float32)
    _, out = lax.scan(step, state0, xs)
    return jnp.moveaxis(out, 0, 2).reshape(b, nh, s, dv)

def hybrid_layer(x, norm_gain, w_in, conv_w, a_log, dt_bias, dn_norm_gain,
                 w_branch_a, w_branch_b, w_out):
    b, s, _ = x.shape
    f32 = jnp.float32
    h = rms_norm(x, norm_gain)
    cuts = np.cumsum(IN_SPLITS)[:-1].tolist()
    aq, ak, av, az, bqkv, bz, bbeta, balpha, gate_a, gate_b = jnp.split(h @ w_in, cuts, axis=-1)

    to_heads = lambda t: t.reshape(b, s, -1, HEAD_DIM)
    ya = moba_attention(to_heads(aq), to_heads(ak), to_heads(av)) * jax.nn.silu(az)

    bqkv = short_conv(bqkv, conv_w)
    bq, bk, bv = jnp.split(bqkv, 3, axis=-1)
    to_bhsd = lambda t: t.reshape(b, s, DN_HEADS, HEAD_DIM).transpose(0, 2, 1, 3).astype(f32)
    g = -jnp.exp(a_log.astype(f32)) * jax.nn.softplus(balpha.astype(f32) + dt_bias.astype(f32))
    beta = jax.nn.sigmoid(bbeta.astype(f32))
    o = gated_delta_rule(to_bhsd(bq), to_bhsd(bk), to_bhsd(bv),
                         jnp.swapaxes(g, 1, 2), jnp.swapaxes(beta, 1, 2))
    o = rms_norm(o.transpose(0, 2, 1, 3), dn_norm_gain).astype(x.dtype) * jax.nn.silu(to_heads(bz))
    yb = o.reshape(b, s, DN_WIDTH)

    merged = (jax.nn.sigmoid(gate_a) * (ya @ w_branch_a)
              + jax.nn.sigmoid(gate_b) * (yb @ w_branch_b))
    return x + merged @ w_out

def setup_inputs(seed: int = 0) -> dict:
    key = jax.random.key(seed)
    ks = jax.random.split(key, 12)
    f32 = jnp.float32
    nrm = lambda k, shape, scale: jax.random.normal(k, shape, f32) * scale
    x = jax.random.normal(ks[0], (BATCH, SEQ, D_MODEL), f32)
    norm_gain = 1.0 + nrm(ks[1], (DEPTH, D_MODEL), 0.02)
    w_in = nrm(ks[2], (DEPTH, D_MODEL, IN_WIDTH), D_MODEL ** -0.5)
    conv_w = nrm(ks[3], (DEPTH, DN_CONV, 3 * DN_WIDTH), DN_CONV ** -0.5)
    a_log = jnp.log(jax.random.uniform(ks[4], (DEPTH, DN_HEADS), f32, 1.0, 16.0))
    dt = jnp.exp(jax.random.uniform(ks[5], (DEPTH, DN_HEADS), f32, math.log(1e-3), math.log(1e-1)))
    dt_bias = dt + jnp.log(-jnp.expm1(-dt))
    dn_norm_gain = 1.0 + nrm(ks[6], (DEPTH, HEAD_DIM), 0.02)
    w_branch_a = nrm(ks[7], (DEPTH, MOBA_WIDTH, D_MODEL), MOBA_WIDTH ** -0.5)
    w_branch_b = nrm(ks[8], (DEPTH, DN_WIDTH, D_MODEL), DN_WIDTH ** -0.5)
    w_out = nrm(ks[9], (DEPTH, D_MODEL, D_MODEL), D_MODEL ** -0.5)
    final_norm_gain = 1.0 + nrm(ks[10], (D_MODEL,), 0.02)
    return {"x": x, "norm_gain": norm_gain, "w_in": w_in, "conv_w": conv_w,
            "a_log": a_log, "dt_bias": dt_bias, "dn_norm_gain": dn_norm_gain,
            "w_branch_a": w_branch_a, "w_branch_b": w_branch_b, "w_out": w_out,
            "final_norm_gain": final_norm_gain}

def reference(x, norm_gain, w_in, conv_w, a_log, dt_bias, dn_norm_gain,
              w_branch_a, w_branch_b, w_out, final_norm_gain):
    for layer in range(DEPTH):
        x = hybrid_layer(x, norm_gain[layer], w_in[layer], conv_w[layer], a_log[layer],
                         dt_bias[layer], dn_norm_gain[layer], w_branch_a[layer],
                         w_branch_b[layer], w_out[layer])
    return rms_norm(x, final_norm_gain)


_drawn_inputs = setup_inputs


def setup_inputs(seed=0):
    import zlib

    import numpy as np

    out = dict(_drawn_inputs(seed))
    spreads = {}
    factors = {'norm_gain': 4.98, 'dn_norm_gain': 8.0, 'final_norm_gain': 2.866}
    for name, (base, spread) in spreads.items():
        noise = np.random.default_rng([zlib.crc32(name.encode()), seed]).standard_normal(out[name].shape)
        drawn = base * np.exp(spread * noise) if base else spread * noise
        out[name] = __import__('jax').numpy.asarray(drawn.astype(out[name].dtype))
    for name, factor in factors.items():
        out[name] = (out[name] * factor).astype(out[name].dtype)
    return out
```

```python
from contextlib import ExitStack

import concourse.bass as bass
from concourse import mybir

ALU = mybir.AluOpType
ACT = mybir.ActivationFunctionType
AX_X = mybir.AxisListType.X
F32 = mybir.dt.float32
F32R = mybir.dt.float32r

P = 128
SEQ, D = 256, 2048
T = SEQ // P
KT = D // P
H = 8
W = H * P
CH = 512
OFF_A = 0
OFF_B = 4 * W
OFF_BETA = 8 * W
OFF_GATE = OFF_BETA + 2 * H
NG = 2 * D // CH
NC = D // CH
RING = 4
UK = 2
UNITS = 3 * KT // UK
SLOTS = 3 * KT
LEAD = 2
BU = H // UK
OU = KT // UK
FIRST_A = H * UNITS
FIRST_B = FIRST_A + NC * BU
FIRST_O = FIRST_B + NC * BU
LEVELS = 6
EPS = 1e-6
SCALE = float(P) ** -0.5
FAR = -1e30

C_CONV, C_G, C_CUM, C_BETA, C_BEG, C_EG, C_DL, C_SLOPE, C_ALL = 0, 12, 14, 16, 18, 19, 20, 21, 22

S_TURN, S_NAT, S_BACK, S_KK, S_X1 = 18, 23, 28, 30, 32
S_Y = [34 + 3 * i for i in range(LEVELS)]
S_XY = [s + 1 for s in S_Y]
S_U, S_S1, S_WS, S_O1, S_YT = 52, 54, 55, 57, 61
M_TURN, M_QK, M_PT, M_PV, M_YT = 33, 35, 39, 41, 44


def build(nc, x, norm_gain, w_in, conv_w, a_log, dt_bias, dn_norm_gain, w_a, w_b, w_out,
          final_gain, out):
    ctx = ExitStack()
    with ctx:
        def sb(name, shape, dt=F32):
            return ctx.enter_context(nc.sbuf_tensor(name, shape, dt))

        def sem(name):
            return ctx.enter_context(nc.semaphore(name))

        w_raw = sb("w_raw", [P, RING, UK * CH])
        w_hi = sb("w_hi", [P, RING, UK * CH], F32R)
        w_lo = sb("w_lo", [P, RING, UK * CH], F32R)
        xt_hi = sb("xt_hi", [P, KT, SEQ], F32R)
        xt_lo = sb("xt_lo", [P, KT, SEQ], F32R)
        ya_hi = sb("ya_hi", [P, H, SEQ], F32R)
        ya_lo = sb("ya_lo", [P, H, SEQ], F32R)
        yb_hi = sb("yb_hi", [P, H, SEQ], F32R)
        yb_lo = sb("yb_lo", [P, H, SEQ], F32R)
        gate = sb("gate", [P, NG, T, CH])
        x_sb = gate[:, 0:NC, :, :].rearrange("p c t n -> p (c t n)").rearrange("p (t d) -> p t d", t=T)
        cols = sb("cols", [P, P])
        wba_hi = sb("wba_hi", [P, KT * 2 * H], F32R)
        wba_lo = sb("wba_lo", [P, KT * 2 * H], F32R)
        dn_gain = sb("dn_gain", [P, P])
        alog = sb("alog", [P, H])
        dtb = sb("dtb", [P, H])
        ident = sb("ident", [P, P])
        ones = sb("ones", [P, P])
        causal = sb("causal", [P, P])
        neg1 = sb("neg1", [P, P])
        levels = sb("levels", [P, LEVELS, P])
        far = sb("far", [P, 3 * P])
        eps = sb("eps", [P, 1])
        rx = sb("rx", [P, 8])
        rxs = sb("rxs", [P, T])
        tabs = sb("tabs", [P, H, C_ALL])
        hs = sb("hs", [P, C_ALL])
        ba = sb("ba", [P, T, 2 * H])
        sp = sb("sp", [P, 4, T, H])
        gl = sb("gl", [P, T, H])
        cum = sb("cum", [P, 2, T, H])
        dn_nat = sb("dn_nat", [P, T, CH])
        dn_z = sb("dn_z", [P, T, P])
        dn_zg = sb("dn_zg", [P, T, P])
        conv = sb("conv", [P, 3, SEQ])
        convs = sb("convs", [P, 3 * SEQ])
        rows = convs[:, 0:P]
        wba = conv[:, 0, :]
        junk = sb("junk", [P, 1])
        ss = sb("ss", [P, 4])
        rn = sb("rn", [P, 4, 4])
        dsub = sb("dsub", [P, T, P])
        decay = sb("decay", [P, T, P])
        tin = sb("tin", [P, T, 3, P])
        qg1 = sb("qg1", [P, P])
        kbg1 = sb("kbg1", [P, P])
        kd0 = sb("kd0", [P, P])
        vb = sb("vb", [P, T, P])
        tT = sb("tT", [P, 7 * P])
        lt = sb("lt", [P, T, P])
        intra = sb("intra", [P, T, P])
        mt = sb("mt", [P, LEVELS, T, P])
        xs = sb("xs", [P, 2 * T, P])
        ysb = sb("ysb", [P, T, P])
        u = sb("u", [P, T, P])
        wT = sb("wT", [P, P])
        s1 = sb("s1", [P, P])
        vnew = sb("vnew", [P, P])
        so = sb("so", [P, 2])
        ro = sb("ro", [P, 4, 2])
        yb = sb("yb", [P, T, P])
        mo_nat = sb("mo_nat", [P, T, 3 * P])
        mo_z = sb("mo_z", [P, T, P])
        moT = sb("moT", [P, 2, SEQ])
        sm = sb("sm", [P, 3 * P])
        prob = sb("prob", [P, 3 * P])
        probT = sb("probT", [P, 3 * P])
        mx = sb("mx", [P, 8])
        ya = sb("ya", [P, T, P])
        fs = sb("fs", [P, T, NC])
        fr = sb("fr", [P, 5, T])

        pj = [ctx.enter_context(nc.psum_tensor(f"pj{i}", [P, T, CH], F32)) for i in range(2)]
        dn_ps = ctx.enter_context(nc.psum_tensor("dn_ps", [P, 2 * CH], F32))
        mo_ps = ctx.enter_context(nc.psum_tensor("mo_ps", [P, 2 * CH], F32))
        A, B = dn_ps[:, 0:CH], dn_ps[:, CH:2 * CH]
        C, E = mo_ps[:, 0:CH], mo_ps[:, CH:2 * CH]

        w_landed = [sem(f"w_landed{i}") for i in range(RING)]
        hi_ready, lo_ready = sem("hi_ready"), sem("lo_ready")
        unit_used = sem("unit_used")
        x_landed = [sem(f"x_landed{i}") for i in range(2 * T)]
        rows_landed, small_landed, wba_landed = sem("rows_landed"), sem("small_landed"), sem("wba_landed")
        const_made, ident_made, const_step = sem("const_made"), sem("ident_made"), sem("const_step")
        cols_turned, cols_ready = sem("cols_turned"), sem("cols_ready")
        x_turned, xt_hi_ready, xt_lo_ready = sem("x_turned"), sem("xt_hi_ready"), sem("xt_lo_ready")
        x_squared, rx_log, rx_exp, rx_step, rx_ready = (sem(n) for n in (
            "x_squared", "rx_log", "rx_exp", "rx_step", "rx_ready"))
        wba_hi_ready, wba_lo_ready = sem("wba_hi_ready"), sem("wba_lo_ready")
        ba_done, ba_ready, beta_ready, tab_step, tab_act, g_ready = (sem(n) for n in (
            "ba_done", "ba_ready", "beta_ready", "tab_step", "tab_act", "g_ready"))
        cum_done, cum_ready, tabs_ready, tabs_pool = (sem(n) for n in (
            "cum_done", "cum_ready", "tabs_ready", "tabs_pool"))
        tile0_done = sem("tile0_done")
        dn_nat_ready, mo_nat_ready, gate_ready = sem("dn_nat_ready"), sem("mo_nat_ready"), sem("gate_ready")
        hs_ready = sem("hs_ready")
        dn_turned, conv_step, convs_ready, nat_done = (sem(n) for n in (
            "dn_turned", "conv_step", "convs_ready", "nat_done"))
        dn_z_ready, dn_zg_ready = sem("dn_z_ready"), sem("dn_zg_ready")
        dsub_ready, dexp_ready, decay_ready = sem("dsub_ready"), sem("dexp_ready"), sem("decay_ready")
        norm_squared, norm_log, norm_exp, norm_step = (sem(n) for n in (
            "norm_squared", "norm_log", "norm_exp", "norm_step"))
        scaled_dve, scaled_act, scaled_pool = sem("scaled_dve"), sem("scaled_act"), sem("scaled_pool")
        back_done, tT_act, tT_dve, kk_done = sem("back_done"), sem("tT_act"), sem("tT_dve"), sem("kk_done")
        lt_ready, intra_ready, mt_ready = sem("lt_ready"), sem("intra_ready"), sem("mt_ready")
        x1_step, x1_done, x1_ready = sem("x1_step"), sem("x1_done"), sem("x1_ready")
        y_done, y_ready, xy_done, xs_ready = sem("y_done"), sem("y_ready"), sem("xy_done"), sem("xs_ready")
        u_done, u_ready, wT_ready, s1_done, s1_ready = (sem(n) for n in (
            "u_done", "u_ready", "wT_ready", "s1_done", "s1_ready"))
        ws_done, vnew_ready, o_done = sem("ws_done"), sem("vnew_ready"), sem("o_done")
        o_squared, o_log, o_exp, o_step, yb_ready = (sem(n) for n in (
            "o_squared", "o_log", "o_exp", "o_step", "yb_ready"))
        ybT_done, yb_hi_ready, yb_lo_ready = sem("ybT_done"), sem("yb_hi_ready"), sem("yb_lo_ready")
        mo_z_ready, mo_turned, moT_ready, qk_done = (sem(n) for n in (
            "mo_z_ready", "mo_turned", "moT_ready", "qk_done"))
        sm_ready, mx_ready, prob_ready, rsum_ready = (sem(n) for n in (
            "sm_ready", "mx_ready", "prob_ready", "rsum_ready"))
        max_step, ro_ready = sem("max_step"), sem("ro_ready")
        pt_done, pt_ready, pv_done, ya_ready = sem("pt_done"), sem("pt_ready"), sem("pv_done"), sem("ya_ready")
        yaT_done, ya_hi_ready, ya_lo_ready = sem("yaT_done"), sem("ya_hi_ready"), sem("ya_lo_ready")
        sig_ready, a_gated, b_gated, merged = sem("sig_ready"), sem("a_gated"), sem("b_gated"), sem("merged")
        mT_done, mT_hi_ready, mT_lo_ready = sem("mT_done"), sem("mT_hi_ready"), sem("mT_lo_ready")
        x_again = [sem(f"x_again{i}") for i in range(NC)]
        gain_landed, sum_ready, f_squared = sem("gain_landed"), sem("sum_ready"), sem("f_squared")
        f_total, f_log, f_exp, f_step, fr_ready = (sem(n) for n in (
            "f_total", "f_log", "f_exp", "f_step", "fr_ready"))
        y_scaled, stored = sem("y_scaled"), sem("stored")

        block = ctx.enter_context(nc.Block())

        def wait_chunk(eng, t, chunk, last_unit):
            if t == 0:
                eng.wait_ge(tile0_done, chunk + 1)
            else:
                eng.wait_ge(unit_used, last_unit + 1)

        @block.sync
        def _(sp):
            for i in range(2 * T):
                t, hf = i // 2, i % 2
                sp.dma_start(x_sb[:, t, hf * D // 2:(hf + 1) * D // 2],
                             x[t * P:(t + 1) * P, hf * D // 2:(hf + 1) * D // 2]).then_inc(x_landed[i], 16)
                if i == 0:
                    sp.dma_start(rows[0:96, :], conv_w.rearrange("j (b c) -> (j b) c", c=P)).then_inc(rows_landed, 16)
                    sp.dma_start(rows[96:96 + KT, :], norm_gain.rearrange("(k c) -> k c", c=P)).then_inc(rows_landed, 16)

            def iteration(h, first):
                head_col = h * P if first else sp.snap(h * P)
                gate_col = OFF_GATE if first else sp.snap(h * CH + OFF_GATE)
                for j in range(UNITS):
                    slot = j % RING
                    used = None if first and j < RING else h * UNITS + j - RING + 1
                    k = (j % (KT // UK)) * UK
                    if used is not None:
                        sp.wait_ge(lo_ready, used)
                    for i in reversed(range(UK)):
                        r = slice((k + i) * P, (k + i + 1) * P)
                        dst = w_raw[:, slot, i * CH:(i + 1) * CH]
                        if j < UNITS // 3 * 2:
                            branch = 1 if j < UNITS // 3 else 0
                            dst = dst.rearrange("p (a n) -> p a n", a=4)
                            src = w_in[r, branch * 4 * W:(branch + 1) * 4 * W].rearrange(
                                "p (a w) -> p a w", a=4)[:, :, bass.ds(head_col, P)]
                        else:
                            src = w_in[r, bass.ds(gate_col, CH)]
                        sp.dma_start(dst, src).then_inc(w_landed[slot], 16)
                    if first and j == RING - 1:
                        sp.dma_start(wba[:, :].rearrange("p (k n) -> p k n", k=KT),
                                     w_in[:, OFF_BETA:OFF_GATE].rearrange("(k p) n -> p k n", p=P)
                                     ).then_inc(wba_landed, 16)
                        sp.dma_start(dn_gain[:, :], dn_norm_gain.rearrange("(a n) -> a n", a=1).to_broadcast([P, P])
                                     ).then_inc(small_landed, 16)
                        sp.dma_start(alog[:, :], a_log.rearrange("(a n) -> a n", a=1).to_broadcast([P, H])
                                     ).then_inc(small_landed, 16)
                        sp.dma_start(dtb[:, :], dt_bias.rearrange("(a n) -> a n", a=1).to_broadcast([P, H])
                                     ).then_inc(small_landed, 16)

            iteration(0, True)
            with sp.Fori(1, H) as h:
                iteration(h, False)

            def chunk(wmat, c, units, first_unit):
                col = c * CH if isinstance(c, int) else sp.snap(c * CH)
                for j in range(units):
                    slot = j % RING
                    sp.wait_ge(lo_ready, c * units + (first_unit + j - RING + 1))
                    for i in reversed(range(UK)):
                        k = UK * j + i
                        sp.dma_start(w_raw[:, slot, i * CH:(i + 1) * CH],
                                     wmat[k * P:(k + 1) * P, bass.ds(col, CH)]).then_inc(w_landed[slot], 16)

            with sp.Fori(0, NC) as c:
                chunk(w_a, c, BU, FIRST_A)
            with sp.Fori(0, NC) as c:
                chunk(w_b, c, BU, FIRST_B)
            for c in range(NC):
                chunk(w_out, c, OU, FIRST_O)
                if c == 0:
                    sp.wait_ge(merged, T * NC)
                    for j in range(NC):
                        sp.dma_start(gate[:, j, :, :], x[:, j * CH:(j + 1) * CH].rearrange("(t p) n -> p t n", p=P)
                                     ).then_inc(x_again[j], 16)
                    sp.wait_ge(mT_done, 2 * NC)
                    sp.dma_start(gate[:, NC:NC + NC // 2, :, :].rearrange("p c t n -> p (c t n)"),
                                 final_gain.rearrange("(a n) -> a n", a=1).to_broadcast([P, D])
                                 ).then_inc(gain_landed, 16)
            for t in range(T):
                for c in range(NC):
                    sp.wait_ge(y_scaled, t * NC + c + 1)
                    sp.dma_start(out[t * P:(t + 1) * P, c * CH:(c + 1) * CH], gate[:, c, t, :]).then_inc(stored, 16)
            sp.wait_ge(stored, 16 * T * NC)

        @block.gpsimd
        def _(pool):
            pool.memset(ident[:, :], 0.0).then_inc(const_step, 1)
            pool.wait_ge(const_step, 1)
            pool.affine_select(out=ident[:, :], in_=ident[:, :], compare_op=ALU.not_equal, fill=1.0, base=0,
                               pattern=[[-1, P]], channel_multiplier=1).then_inc(ident_made, 1)
            pool.memset(ones[:, :], 1.0).then_inc(const_step, 1)
            pool.memset(eps[:, :], EPS).then_inc(const_step, 1)
            pool.wait_ge(const_step, 3)
            pool.affine_select(out=causal[:, :], in_=ones[:, :], compare_op=ALU.is_ge, fill=0.0, base=0,
                               pattern=[[1, P]], channel_multiplier=-1).then_inc(const_step, 1)
            pool.iota(sm[:, 0:P], pattern=[[1, P]], base=0, channel_multiplier=-1,
                      allow_small_or_imprecise_dtypes=True).then_inc(const_step, 1)
            pool.iota(sm[:, P:3 * P], pattern=[[1, 2 * P]], base=-P, channel_multiplier=-1,
                      allow_small_or_imprecise_dtypes=True).then_inc(const_step, 1)
            pool.wait_ge(const_step, 6)
            pool.affine_select(out=far[:, 0:P], in_=sm[:, 0:P], compare_op=ALU.is_ge, fill=FAR, base=0,
                               pattern=[[-1, P]], channel_multiplier=1).then_inc(const_step, 1)
            pool.affine_select(out=far[:, P:3 * P], in_=sm[:, P:3 * P], compare_op=ALU.is_ge, fill=FAR, base=P,
                               pattern=[[-1, 2 * P]], channel_multiplier=1).then_inc(const_step, 1)
            done = 8
            for n in range(LEVELS + 1):
                s = 1 << n
                m = neg1[:, :] if n == 0 else levels[:, n - 1, :]
                blocks = m.rearrange("p (b e c) -> p b e c", e=2, c=s)
                pool.memset(m, -1.0 if n == 0 else 1.0).then_inc(const_step, 1)
                done += 1
                pool.wait_ge(const_step, done)
                pool.affine_select(out=blocks, in_=blocks, compare_op=ALU.is_ge, fill=0.0, base=-1,
                                   pattern=[[0, P // (2 * s)], [1, 2], [0, s]], channel_multiplier=0).then_inc(const_step, 1)
                pool.wait_ge(const_step, done + 1)
                pool.affine_select(out=blocks, in_=blocks, compare_op=ALU.is_ge, fill=0.0, base=0,
                                   pattern=[[-2 * s, P // (2 * s)], [0, 2], [0, s]], channel_multiplier=1).then_inc(const_step, 1)
                pool.wait_ge(const_step, done + 2)
                pool.affine_select(out=blocks, in_=blocks, compare_op=ALU.is_ge, fill=0.0, base=s - 1,
                                   pattern=[[2 * s, P // (2 * s)], [0, 2], [0, s]], channel_multiplier=-1).then_inc(const_step, 1)
                done += 3
            for h in range(H):
                pool.memset(tabs[:, h, C_SLOPE:C_SLOPE + 1], 2.0 ** (-8.0 * (h + 1) / H)).then_inc(tabs_pool, 1)
            pool.wait_ge(const_step, done)
            pool.memset(junk[:, 0:1], 0.0).then_inc(const_made, 1)

            def head(h, first):
                if not first:
                    pool.wait_ge(sm_ready, h)
                    pool.wait_ge(scaled_act, 3 * h)
                    pool.wait_ge(scaled_dve, 3 * h)
                    pool.wait_ge(nat_done, h)
                pool.tensor_copy(hs[:, :], tabs[:, bass.ds(h, 1), :].rearrange("p a c -> p (a c)")).then_inc(hs_ready, 1)
                pool.wait_ge(dn_z_ready, h + 1)
                if not first:
                    pool.wait_ge(yb_ready, T * h)
                pool.tensor_tensor(dn_zg[:, :, :], dn_z[:, :, :],
                                   dn_gain[:, None, :].to_broadcast([P, T, P]), ALU.mult).then_inc(dn_zg_ready, 1)
                pool.wait_ge(scaled_dve, 3 * h + 1)
                if not first:
                    pool.wait_ge(s1_done, h)
                for dst, t, col in ((kd0, 0, C_DL), (kbg1, 1, C_BEG)):
                    pool.tensor_tensor(dst[:, :], tin[:, t, 0, :], hs[:, col:col + 1].to_broadcast([P, P]),
                                       ALU.mult).then_inc(scaled_pool, 1)
                pool.wait_ge(lt_ready, h + 1)
                for n in range(LEVELS):
                    pool.tensor_tensor(mt[:, n, :, :], lt[:, :, :],
                                       levels[:, n, None, :].to_broadcast([P, T, P]), ALU.mult).then_inc(mt_ready, 1)

            pool.wait_ge(tabs_pool, H)
            pool.wait_ge(tabs_ready, 8)
            pool.wait_ge(small_landed, 48)
            head(0, True)
            with pool.Fori(1, H) as h:
                head(h, False)

        @block.tensor
        def _(pe):
            pe.wait_ge(ident_made, 1)
            pe.wait_ge(rows_landed, 32)
            pe.transpose(E[:, 0:96 + KT], rows[0:96 + KT, :], ident[0:96 + KT, 0:96 + KT]).then_inc(cols_turned, 1)
            banks = [pj[0][:, 0, :], pj[0][:, 1, :], pj[1][:, 0, :], pj[1][:, 1, :]]
            for g in range(KT // 2):
                if g == 0:
                    pe.wait_ge(x_landed[0], 16)
                    pe.wait_ge(x_landed[2], 16)
                if g == KT // 4:
                    pe.wait_ge(x_landed[1], 16)
                    pe.wait_ge(x_landed[3], 16)
                if g >= 4:
                    pe.wait_ge(xt_lo_ready, 2 * (g - 3))
                for q in range(4):
                    k, t = 2 * g + q // 2, q % 2
                    mm = pe.transpose(banks[g % 4][:, q * P:(q + 1) * P], x_sb[:, t, k * P:(k + 1) * P], ident[:, :])
                mm.then_inc(x_turned, 1)

            def unit(slot, number, hi, lo, k0, bank, kt_all, free=None, after=None):
                pe.wait_ge(hi_ready, number + 1)
                pe.wait_ge(lo_ready, number + 1)
                for t in range(T):
                    if free is not None and k0 == 0:
                        free(t)
                    for i in range(UK):
                        k = k0 + i
                        tok = slice(t * P, (t + 1) * P)
                        cs = slice(i * CH, (i + 1) * CH)
                        pe.matmul(bank[:, t, :], hi[:, k, tok], w_hi[:, slot, cs], start=(k == 0), stop=False)
                        pe.matmul(bank[:, t, :], hi[:, k, tok], w_lo[:, slot, cs], start=False, stop=False)
                        mm = pe.matmul(bank[:, t, :], lo[:, k, tok], w_hi[:, slot, cs], start=False,
                                       stop=(k == kt_all - 1))
                    if t == T - 1:
                        mm.then_inc(unit_used, 1)
                    elif k == kt_all - 1:
                        mm.then_inc(tile0_done, 1)

            def dn_step(s, h, first=False):
                if s == S_TURN:
                    pe.wait_ge(dn_nat_ready, T * h + T)
                    if not first:
                        pe.wait_ge(yb_lo_ready, h)
                    for p in range(3):
                        for t in range(T):
                            mm = pe.transpose(dn_ps[:, (p * T + t) * P:(p * T + t + 1) * P],
                                              dn_nat[:, t, p * P:(p + 1) * P], ident[:, :])
                    mm.then_inc(dn_turned, 1)
                if s == S_NAT:
                    pe.wait_ge(convs_ready, h + 1)
                    pe.wait_ge(hs_ready, h + 1)
                    for i in range(3 * T):
                        pe.transpose(dn_ps[:, i * P:(i + 1) * P], convs[:, i * P:(i + 1) * P], ident[:, :])
                    for t in range(T):
                        mm = pe.matmul(dn_ps[:, (6 + t) * P:(7 + t) * P], hs[:, C_G + t:C_G + t + 1].to_broadcast([P, P]),
                                       causal[:, :], start=True, stop=True)
                    mm.then_inc(nat_done, 1)
                if s == S_BACK:
                    pe.wait_ge(scaled_dve, 3 * h + 3)
                    pe.wait_ge(scaled_act, 3 * h + 3)
                    pe.wait_ge(dsub_ready, T * h + T)
                    for t in range(T):
                        for p in range(3):
                            i = 3 * t + p
                            pe.transpose(dn_ps[:, i * P:(i + 1) * P], tin[:, t, p, :], ident[:, :])
                    pe.transpose(dn_ps[:, 6 * P:7 * P], qg1[:, :], ident[:, :]).then_inc(back_done, 1)
                if s == S_KK:
                    pe.wait_ge(tT_act, h + 1)
                    pe.wait_ge(tT_dve, h + 1)
                    for t in range(T):
                        o = 3 * P * t
                        mm = pe.matmul(A[:, 2 * P * t:2 * P * (t + 1)], tT[:, o:o + P], tT[:, o + P:o + 3 * P],
                                       start=True, stop=True)
                    mm.then_inc(kk_done, 1)
                if s == S_X1:
                    pe.wait_ge(x1_step, 2 * h + 2)
                    for t in range(T):
                        mm = pe.transpose(B[:, t * P:(t + 1) * P], xs[:, T + t, :], ident[:, :])
                    mm.then_inc(x1_done, 1)
                if s in S_Y:
                    n = S_Y.index(s)
                    if n == 0:
                        pe.wait_ge(x1_ready, h + 1)
                        pe.wait_ge(lt_ready, h + 1)
                        pe.wait_ge(intra_ready, h + 1)
                    else:
                        pe.wait_ge(xs_ready, LEVELS * h + n)
                    pe.wait_ge(mt_ready, LEVELS * h + n + 1)
                    for t in range(T):
                        mm = pe.matmul(A[:, t * P:(t + 1) * P], mt[:, n, t, :], xs[:, t, :], start=True, stop=True)
                    mm.then_inc(y_done, 1)
                if s in S_XY:
                    n = S_XY.index(s)
                    pe.wait_ge(y_ready, LEVELS * h + n + 1)
                    for t in range(T):
                        mm = pe.matmul(B[:, (T + t) * P:(T + t + 1) * P], ysb[:, t, :], xs[:, T + t, :],
                                       start=True, stop=True)
                    if n < LEVELS - 1:
                        for t in range(T):
                            mm = pe.matmul(B[:, t * P:(t + 1) * P], xs[:, T + t, :], ysb[:, t, :],
                                           start=True, stop=True)
                    mm.then_inc(xy_done, 1)
                if s == S_U:
                    pe.wait_ge(xs_ready, LEVELS * h + LEVELS)
                    pe.wait_ge(scaled_pool, 2 * h + 2)
                    for t in range(T):
                        pe.matmul(A[:, t * P:(t + 1) * P], xs[:, T + t, :], vb[:, t, :], start=True, stop=True)
                    pe.matmul(B[:, 3 * P:4 * P], kbg1[:, :], xs[:, T + 1, :], start=True, stop=True).then_inc(u_done, 1)
                if s == S_S1:
                    pe.wait_ge(u_ready, h + 1)
                    pe.wait_ge(wT_ready, h + 1)
                    pe.matmul(B[:, P:2 * P], intra[:, 0, :], u[:, 0, :], start=True, stop=True)
                    pe.matmul(B[:, 0:P], kd0[:, :], u[:, 0, :], start=True, stop=True).then_inc(s1_done, 1)
                if s == S_WS:
                    pe.wait_ge(s1_ready, h + 1)
                    pe.matmul(A[:, 3 * P:4 * P], wT[:, :], s1[:, :], start=True, stop=True).then_inc(ws_done, 1)
                if s == S_O1:
                    pe.wait_ge(vnew_ready, h + 1)
                    pe.matmul(B[:, 2 * P:3 * P], tT[:, 6 * P:7 * P], s1[:, :], start=True, stop=False)
                    pe.matmul(B[:, 2 * P:3 * P], intra[:, 1, :], vnew[:, :], start=False, stop=True).then_inc(o_done, 1)
                if s == S_YT:
                    pe.wait_ge(yb_ready, T * h + T)
                    for t in range(T):
                        mm = pe.transpose(A[:, t * P:(t + 1) * P], yb[:, t, :], ident[:, :])
                    mm.then_inc(ybT_done, 1)

            def mo_step(s, h, first=False):
                if s == M_TURN:
                    pe.wait_ge(mo_nat_ready, 2 * T * h + 2 * T)
                    if not first:
                        pe.wait_ge(ya_lo_ready, h)
                    for p in range(2):
                        for t in range(T):
                            mm = pe.transpose(C[:, (p * T + t) * P:(p * T + t + 1) * P],
                                              mo_nat[:, t, p * P:(p + 1) * P], ident[:, :])
                    mm.then_inc(mo_turned, 1)
                if s == M_QK:
                    pe.wait_ge(moT_ready, h + 1)
                    pe.matmul(E[:, 0:P], moT[:, 0, 0:P], moT[:, 1, 0:P], start=True, stop=True)
                    pe.matmul(E[:, P:3 * P], moT[:, 0, P:2 * P], moT[:, 1, :], start=True, stop=True).then_inc(qk_done, 1)
                if s == M_PT:
                    pe.wait_ge(prob_ready, T * h + T)
                    for i in range(3):
                        mm = pe.transpose(C[:, i * P:(i + 1) * P], prob[:, i * P:(i + 1) * P], ident[:, :])
                    mm.then_inc(pt_done, 1)
                if s == M_PV:
                    pe.wait_ge(pt_ready, h + 1)
                    v = [mo_nat[:, t, 2 * P:3 * P] for t in range(T)]
                    pe.matmul(E[:, 0:P], probT[:, 0:P], v[0], start=True, stop=True)
                    pe.matmul(E[:, P:2 * P], probT[:, P:2 * P], v[0], start=True, stop=False)
                    pe.matmul(E[:, P:2 * P], probT[:, 2 * P:3 * P], v[1], start=False, stop=True).then_inc(pv_done, 1)
                if s == M_YT:
                    pe.wait_ge(ya_ready, T * h + T)
                    for t in range(T):
                        mm = pe.transpose(C[:, t * P:(t + 1) * P], ya[:, t, :], ident[:, :])
                    mm.then_inc(yaT_done, 1)

            def beta_decay_inputs():
                pe.wait_ge(const_made, 1)
                pe.wait_ge(wba_hi_ready, 1)
                pe.wait_ge(wba_lo_ready, 1)
                n = 2 * H
                for t in range(T):
                    tok = slice(t * P, (t + 1) * P)
                    for k in range(KT):
                        cs = slice(k * n, (k + 1) * n)
                        pe.matmul(C[:, t * n:(t + 1) * n], xt_hi[:, k, tok], wba_hi[:, cs], start=(k == 0), stop=False)
                        pe.matmul(C[:, t * n:(t + 1) * n], xt_hi[:, k, tok], wba_lo[:, cs], start=False, stop=False)
                        mm = pe.matmul(C[:, t * n:(t + 1) * n], xt_lo[:, k, tok], wba_hi[:, cs], start=False,
                                       stop=(k == KT - 1))
                mm.then_inc(ba_done, 1)

            def cumulate():
                pe.wait_ge(g_ready, 1)
                g = gl[:, :, :].rearrange("p t h -> p (t h)")
                pe.matmul(C[:, 64:64 + T * H], causal[:, :], g, start=True, stop=True)
                pe.matmul(C[:, 128:128 + T * H], ones[:, :], g, start=True, stop=True).then_inc(cum_done, 1)

            def iteration(h, first):
                for j in range(UNITS):
                    c = j // (KT // UK)
                    k0 = (j % (KT // UK)) * UK

                    def free(t, c=c):
                        if c == 0:
                            if first:
                                pe.wait_ge(xt_lo_ready, KT)
                            else:
                                pe.wait_ge(gate_ready, T * h - T + t + 1)
                        if c == 1 and not first:
                            pe.wait_ge(mo_nat_ready, 2 * T * h - 2 * T + 2 * t + 2)
                            pe.wait_ge(mo_z_ready, T * h - T + t + 1)
                        if c == 2:
                            pe.wait_ge(dn_nat_ready, T * h + t + 1)

                    unit(j % RING, h * UNITS + j, xt_hi, xt_lo, k0, pj[c % 2], KT, free)
                    for s in (2 * j, 2 * j + 1):
                        if not first:
                            dn_step(s + SLOTS, h - 1)
                        dn_step(s, h, first)
                        mo_step(s, h, first)
                    if first and j == 2:
                        beta_decay_inputs()
                    if first and j == 6:
                        cumulate()

            iteration(0, True)
            with pe.Fori(1, H) as h:
                iteration(h, False)

            def branch(c, hi, lo, first_unit, number, dn=None):
                for j in range(BU):
                    def free(t):
                        if number < 2:
                            pe.wait_ge(gate_ready, T * H)
                            pe.wait_ge(mo_nat_ready, 2 * T * H)
                        else:
                            pe.wait_ge(a_gated, T * (number - 2) + t + 1)
                    unit(j % RING, first_unit + c * BU + j, hi, lo, UK * j, pj[number % 2], H, free)
                    if dn is not None:
                        for s in (2 * j, 2 * j + 1):
                            dn_step(dn + s + SLOTS, H - 1)

            pe.wait_ge(ya_hi_ready, H)
            pe.wait_ge(ya_lo_ready, H)
            for c in range(NC):
                branch(c, ya_hi, ya_lo, FIRST_A, c, 2 * BU * c)
            pe.wait_ge(yb_hi_ready, H)
            pe.wait_ge(yb_lo_ready, H)

            def turn_merged(c):
                pe.wait_ge(merged, T * c + T)
                ps = [dn_ps, mo_ps][c % 2]
                if c >= 2:
                    pe.wait_ge(mT_lo_ready, 2 * (c - 1))
                for half in range(2):
                    for q in range(4):
                        i, t = 2 * half + q // 2, q % 2
                        mm = pe.transpose(ps[:, (4 * half + q) * P:(4 * half + q + 1) * P],
                                          gate[:, NC + c, t, i * P:(i + 1) * P], ident[:, :])
                    mm.then_inc(mT_done, 1)

            for c in range(NC):
                def free(t, c=c):
                    if c < 2:
                        pe.wait_ge(a_gated, T * (c + 2) + t + 1)
                    else:
                        pe.wait_ge(b_gated, T * (c - 2) + t + 1)
                for j in range(BU):
                    unit(j % RING, FIRST_B + c * BU + j, yb_hi, yb_lo, UK * j, pj[c % 2], H, free)
                    if j == 1 and c > 0:
                        turn_merged(c - 1)
            turn_merged(NC - 1)
            for c in range(NC):
                def free(t, c=c):
                    if c < 2:
                        pe.wait_ge(b_gated, T * (c + 2) + t + 1)
                    else:
                        pe.wait_ge(sum_ready, T * (c - 2) + t + 1)
                for j in range(OU):
                    if c == 0:
                        pe.wait_ge(mT_hi_ready, j + 1)
                        pe.wait_ge(mT_lo_ready, j + 1)
                    unit(j % RING, FIRST_O + c * OU + j, xt_hi, xt_lo, UK * j, pj[c % 2], KT, free)

        @block.scalar
        def _(act):
            def split(slot, number, landed, first=False):
                act.wait_ge(w_landed[slot], landed)
                if not first:
                    act.wait_ge(unit_used, number - RING + 1)
                act.activation(w_hi[:, slot, :], w_raw[:, slot, :], ACT.Copy).then_inc(hi_ready, 1)

            act.wait_ge(cols_ready, 1)
            for k in range(KT):
                act.wait_ge(x_turned, k // 2 + 1)
                src = pj[(k // 2 % 4) // 2][:, k // 2 % 2, (k % 2) * SEQ:(k % 2 + 1) * SEQ]
                act.activation(xt_hi[:, k, :], src, ACT.Copy, scale=cols[:, 96 + k:97 + k]).then_inc(xt_hi_ready, 1)
                if k == KT // 2 + 1:
                    split(0, 0, 32, True)
                if k == 3 * KT // 4 + 1:
                    split(1, 1, 32, True)
            act.wait_ge(wba_landed, 16)
            act.activation(wba_hi[:, :], wba[:, :], ACT.Copy).then_inc(wba_hi_ready, 1)
            act.wait_ge(const_made, 1)
            act.wait_ge(x_squared, T)
            act.activation(rx[:, 2:4], rx[:, 0:2], ACT.Ln, scale=1.0 / D, bias=eps[:, 0:1]).then_inc(rx_log, 1)
            act.wait_ge(rx_log, 1)
            act.activation(rx[:, 4:6], rx[:, 2:4], ACT.Exp, scale=-0.5).then_inc(rx_exp, 1)

            def tables():
                act.wait_ge(ba_done, 1)
                for t in range(T):
                    act.activation(ba[:, t, :], C[:, t * 2 * H:(t + 1) * 2 * H], ACT.Copy,
                                   scale=rx[:, 6 + t:7 + t]).then_inc(ba_ready, 1)
                act.wait_ge(ba_ready, T)
                act.activation(tabs[:, :, C_BETA:C_BETA + T].rearrange("p h t -> p t h"), ba[:, :, 0:H],
                               ACT.Sigmoid).then_inc(beta_ready, 1)
                act.wait_ge(tab_step, 2)
                act.activation(sp[:, 1, :, :], sp[:, 1, :, :], ACT.Exp).then_inc(tab_act, 1)
                act.wait_ge(small_landed, 48)
                act.activation(alog[:, :], alog[:, :], ACT.Exp).then_inc(tab_act, 1)
                act.wait_ge(tab_act, 2)
                act.activation(sp[:, 2, :, :], sp[:, 1, :, :], ACT.Ln, bias=ones[:, 0:1]).then_inc(tab_act, 1)

            def tables_cumulated():
                act.wait_ge(cum_ready, 3)
                act.activation(sp[:, 0:2, :, :], cum[:, :, :, :], ACT.Exp).then_inc(tab_act, 1)

            def dn_step(s, h, first=False):
                if s == S_TURN - 2:
                    if not first:
                        act.wait_ge(dn_turned, h)
                        act.wait_ge(dn_z_ready, h)
                    for t in range(T):
                        wait_chunk(act, t, 3 * h, UNITS * h + UNITS // 3 - 1)
                        act.activation(dn_nat[:, t, :], pj[0][:, t, :], ACT.Copy,
                                       scale=rx[:, 6 + t:7 + t]).then_inc(dn_nat_ready, 1)
                if s == S_NAT - 1:
                    act.wait_ge(conv_step, 12 * h + 12)
                    if not first:
                        act.wait_ge(nat_done, h)
                    act.activation(convs[:, :], conv[:, :, :].rearrange("p a t -> p (a t)"), ACT.Silu).then_inc(convs_ready, 1)
                    if not first:
                        act.wait_ge(dn_zg_ready, h)
                    act.activation(dn_z[:, :, :], dn_nat[:, :, 3 * P:4 * P], ACT.Silu).then_inc(dn_z_ready, 1)
                if s == S_NAT:
                    act.wait_ge(nat_done, h + 1)
                    if not first:
                        act.wait_ge(norm_step, 3 * h)
                    for i in range(2 * T):
                        act.activation(mt[:, i // 2, i % 2, :], dn_ps[:, i * P:(i + 1) * P], ACT.Square,
                                       accum_out=ss[:, i:i + 1]).then_inc(norm_squared, 1)
                    act.wait_ge(norm_squared, 2 * T * (h + 1))
                    act.activation(rn[:, 0, :], ss[:, :], ACT.Ln, bias=eps[:, 0:1]).then_inc(norm_log, 1)
                    act.wait_ge(norm_log, h + 1)
                    act.activation(rn[:, 1, :], rn[:, 0, :], ACT.Exp, scale=-0.5).then_inc(norm_exp, 1)
                    act.wait_ge(dsub_ready, T * h + T)
                    act.activation(dsub[:, :, :], dsub[:, :, :], ACT.Exp).then_inc(dexp_ready, 1)
                if s == S_NAT + 2:
                    if not first:
                        act.wait_ge(back_done, h)
                    act.wait_ge(scaled_dve, 3 * h + 1)
                    for t in range(T):
                        act.activation(tin[:, t, 1, :], tin[:, t, 0, :], ACT.Copy,
                                       scale=hs[:, C_BETA + t:C_BETA + t + 1]).then_inc(scaled_act, 1)
                    act.wait_ge(scaled_dve, 3 * h + 2)
                    act.activation(qg1[:, :], tin[:, 1, 2, :], ACT.Copy,
                                   scale=hs[:, C_EG:C_EG + 1]).then_inc(scaled_act, 1)
                if s == S_BACK:
                    act.wait_ge(back_done, h + 1)
                    act.activation(tT[:, 0:4 * P], dn_ps[:, 0:4 * P], ACT.Copy).then_inc(tT_act, 1)
                if s == S_X1:
                    act.wait_ge(x1_done, h + 1)
                    act.activation(xs[:, 0:T, :].rearrange("p t n -> p (t n)"), B[:, 0:T * P], ACT.Copy).then_inc(x1_ready, 1)
                if s in S_Y:
                    n = S_Y.index(s)
                    act.wait_ge(y_done, LEVELS * h + n + 1)
                    if n > 0 or not first:
                        act.wait_ge(xy_done, LEVELS * h + n)
                    act.activation(ysb[:, :, :].rearrange("p t n -> p (t n)"), A[:, 0:T * P], ACT.Copy).then_inc(y_ready, 1)
                if s == S_U:
                    act.wait_ge(u_done, h + 1)
                    if not first:
                        act.wait_ge(o_done, h)
                    act.activation(u[:, :, :].rearrange("p t n -> p (t n)"), A[:, 0:T * P], ACT.Copy).then_inc(u_ready, 1)
                if s == S_O1:
                    act.wait_ge(o_done, h + 1)
                    if not first:
                        act.wait_ge(o_step, 3 * h)
                    for t in range(T):
                        act.activation(mt[:, 2, t, :], B[:, (1 + t) * P:(2 + t) * P], ACT.Square,
                                       accum_out=so[:, t:t + 1]).then_inc(o_squared, 1)
                    act.wait_ge(o_squared, T * (h + 1))
                    act.activation(ro[:, 0, :], so[:, :], ACT.Ln, scale=1.0 / P, bias=eps[:, 0:1]).then_inc(o_log, 1)
                    act.wait_ge(o_log, h + 1)
                    act.activation(ro[:, 1, :], ro[:, 0, :], ACT.Exp, scale=-0.5).then_inc(o_exp, 1)
                if s == S_YT:
                    act.wait_ge(ybT_done, h + 1)
                    act.activation(yb_hi[:, bass.ds(h, 1), :].rearrange("p a n -> p (a n)"), A[:, 0:SEQ],
                                   ACT.Copy).then_inc(yb_hi_ready, 1)

            def mo_step(s, h, first=False):
                if s == M_TURN - 1:
                    if not first:
                        act.wait_ge(pv_done, h)
                        act.wait_ge(ya_ready, T * h)
                    for t in range(T):
                        wait_chunk(act, t, 3 * h + 1, UNITS * h + 2 * UNITS // 3 - 1)
                        act.activation(mo_nat[:, t, 0:P], pj[1][:, t, 0:P], ACT.Copy,
                                       scale=rxs[:, t:t + 1]).then_inc(mo_nat_ready, 1)
                        act.activation(mo_z[:, t, :], pj[1][:, t, 3 * P:4 * P], ACT.Silu,
                                       scale=rx[:, 6 + t:7 + t]).then_inc(mo_z_ready, 1)
                        act.activation(mo_nat[:, t, P:3 * P], pj[1][:, t, P:3 * P], ACT.Copy,
                                       scale=rx[:, 6 + t:7 + t]).then_inc(mo_nat_ready, 1)
                if s == M_TURN:
                    act.wait_ge(mo_turned, h + 1)
                    act.activation(moT[:, :, :].rearrange("p a t -> p (a t)"), C, ACT.Copy).then_inc(moT_ready, 1)
                if s == M_QK:
                    act.wait_ge(mx_ready, h + 1)
                    if not first:
                        act.wait_ge(rsum_ready, h)
                    act.activation(prob[:, 0:P], sm[:, 0:P], ACT.Exp, bias=mx[:, 0:1],
                                   accum_out=mx[:, 2:3]).then_inc(prob_ready, 1)
                    act.activation(prob[:, P:3 * P], sm[:, P:3 * P], ACT.Exp, bias=mx[:, 1:2],
                                   accum_out=mx[:, 3:4]).then_inc(prob_ready, 1)
                if s == M_PT:
                    act.wait_ge(pt_done, h + 1)
                    act.activation(probT[:, :], C[:, 0:3 * P], ACT.Copy).then_inc(pt_ready, 1)
                if s == M_YT:
                    act.wait_ge(yaT_done, h + 1)
                    act.activation(ya_hi[:, bass.ds(h, 1), :].rearrange("p a n -> p (a n)"), C[:, 0:SEQ],
                                   ACT.Copy).then_inc(ya_hi_ready, 1)

            def gates(h):
                for t in range(T):
                    wait_chunk(act, t, 3 * h + 2, UNITS * h + UNITS - 1)
                    act.activation(gate[:, bass.ds(h, 1), t, :].rearrange("p a n -> p (a n)"), pj[0][:, t, :],
                                   ACT.Copy, scale=rx[:, 6 + t:7 + t]).then_inc(gate_ready, 1)

            def iteration(h, first):
                for s in range(SLOTS):
                    if s % 2 == 0:
                        n = s // 2 + LEAD
                        split(n % RING, h * UNITS + n, (h * (UNITS // RING) + n // RING + 1) * 32,
                              first and n < RING)
                    if first and s == 8:
                        tables()
                    if first and s == 14:
                        tables_cumulated()
                    if not first:
                        if s == 0:
                            gates(h - 1)
                        dn_step(s + SLOTS, h - 1)
                    dn_step(s, h, first)
                    mo_step(s, h, first)

            act.wait_ge(rx_ready, 1)
            iteration(0, True)
            with act.Fori(1, H) as h:
                iteration(h, False)

            def tail_split(n):
                split(n % RING, n, (n // RING + 1) * 32)

            for c in range(NC):
                for j in range(BU):
                    tail_split(FIRST_A + BU * c + j + LEAD)
                    if c == 0 and j == 0:
                        gates(H - 1)
                    for s in (2 * j, 2 * j + 1):
                        dn_step(2 * BU * c + s + SLOTS, H - 1)
                    n = BU * c + j - 2 * BU + 1
                    if 0 <= n < NG:
                        if n == 0:
                            act.wait_ge(gate_ready, T * H)
                        act.activation(gate[:, n, :, :], gate[:, n, :, :], ACT.Sigmoid).then_inc(sig_ready, 1)

            def merged_hi(c):
                ps = [dn_ps, mo_ps][c % 2]
                for half in range(2):
                    act.wait_ge(mT_done, 2 * c + half + 1)
                    act.activation(xt_hi[:, 4 * c + 2 * half:4 * c + 2 * half + 2, :].rearrange("p k t -> p (k t)"),
                                   ps[:, half * CH:(half + 1) * CH], ACT.Copy).then_inc(mT_hi_ready, 1)

            for n in range(NC * BU):
                tail_split(FIRST_B + n + LEAD)
                if n % BU == 1 and n > BU:
                    merged_hi(n // BU - 1)
            merged_hi(NC - 1)

            def squares(c):
                for t in range(T):
                    act.wait_ge(sum_ready, T * c + t + 1)
                    if T * c + t >= 2:
                        act.wait_ge(f_squared, T * c + t - 1)
                    act.activation(sq[:, t, :], gate[:, c, t, :], ACT.Square,
                                   accum_out=fs[:, t, c:c + 1]).then_inc(f_squared, 1)

            sq = mt[:, 0:4, :, :].rearrange("p (b a) t n -> p b (a t n)", a=2)
            for n in range(NC * OU - LEAD):
                tail_split(FIRST_O + n + LEAD)
                if n % OU == 1 and n > OU:
                    squares(n // OU - 1)
            squares(NC - 1)
            act.wait_ge(f_total, 1)
            act.activation(fr[:, 1, :], fr[:, 0, :], ACT.Ln, scale=1.0 / D, bias=eps[:, 0:1]).then_inc(f_log, 1)
            act.wait_ge(f_log, 1)
            act.activation(fr[:, 2, :], fr[:, 1, :], ACT.Exp, scale=-0.5).then_inc(f_exp, 1)

        @block.vector
        def _(dve):
            def split(slot, number, first=False):
                dve.wait_ge(hi_ready, number + 1)
                dve.tensor_tensor(w_lo[:, slot, :], w_raw[:, slot, :], w_hi[:, slot, :].bitcast(F32),
                                  ALU.subtract).then_inc(lo_ready, 1)

            def newton(x_, r0, tmp1, tmp2, res, step, base, ready, scale):
                v = tmp1
                dve.tensor_scalar(v, x_, scale, EPS, ALU.mult, ALU.add).then_inc(step, 1)
                dve.wait_ge(step, base + 1)
                dve.tensor_tensor(tmp2, v, r0, ALU.mult).then_inc(step, 1)
                dve.wait_ge(step, base + 2)
                dve.scalar_tensor_tensor(out=tmp1, in0=tmp2, scalar=-0.5, in1=r0, op0=ALU.mult,
                                         op1=ALU.mult).then_inc(step, 1)
                dve.wait_ge(step, base + 3)
                dve.scalar_tensor_tensor(out=res, in0=tmp1, scalar=1.5, in1=r0, op0=ALU.add,
                                         op1=ALU.mult).then_inc(ready, 1)

            dve.wait_ge(cols_turned, 1)
            dve.tensor_copy(cols[:, 0:96 + KT], E[:, 0:96 + KT]).then_inc(cols_ready, 1)
            dve.wait_ge(cols_ready, 1)
            for k in range(KT):
                dve.wait_ge(xt_hi_ready, k // 2 * 2 + 2)
                src = pj[(k // 2 % 4) // 2][:, k // 2 % 2, (k % 2) * SEQ:(k % 2 + 1) * SEQ]
                dve.scalar_tensor_tensor(out=xt_lo[:, k, :], in0=src, scalar=cols[:, 96 + k:97 + k],
                                         in1=xt_hi[:, k, :].bitcast(F32), op0=ALU.mult,
                                         op1=ALU.subtract).then_inc(xt_lo_ready, 1)
                if k == KT // 2 + 1:
                    split(0, 0)
                if k == 3 * KT // 4 + 1:
                    split(1, 1)
            dve.wait_ge(const_made, 1)
            taps = cols[:, 0:96].rearrange("p (j a h) -> p h a j", j=4, a=3)
            for a in range(3):
                dve.tensor_copy(tabs[:, :, C_CONV + 4 * a:C_CONV + 4 * a + 4], taps[:, :, a, :]).then_inc(tabs_ready, 1)
            sq = gate[:, NC:2 * NC, :, :].rearrange("p c t n -> p (c t n)")
            for t in range(T):
                dve.tensor_tensor_reduce(sq[:, t * D:(t + 1) * D], x_sb[:, t, :], x_sb[:, t, :], 1.0, 0.0, ALU.mult,
                                         ALU.add, rx[:, t:t + 1]).then_inc(x_squared, 1)
            dve.wait_ge(wba_hi_ready, 1)
            dve.tensor_tensor(wba_lo[:, :], wba[:, :], wba_hi[:, :].bitcast(F32), ALU.subtract).then_inc(wba_lo_ready, 1)
            dve.wait_ge(x_squared, T)
            dve.wait_ge(rx_exp, 1)
            newton(rx[:, 0:2], rx[:, 4:6], rx[:, 2:4], fr[:, 4, :], rx[:, 6:8], rx_step, 0, rx_step, 1.0 / D)
            dve.wait_ge(rx_step, 4)
            dve.tensor_scalar(rxs[:, :], rx[:, 6:8], SCALE, None, ALU.mult).then_inc(rx_ready, 1)

            def tables():
                n = 0
                dve.wait_ge(ba_ready, T)
                dve.wait_ge(small_landed, 48)
                dve.tensor_tensor(sp[:, 0, :, :], ba[:, :, H:2 * H], dtb[:, None, :].to_broadcast([P, T, H]),
                                  ALU.add).then_inc(tab_step, 1)
                dve.wait_ge(tab_step, 1)
                dve.scalar_tensor_tensor(out=sp[:, 1, :, :], in0=sp[:, 0, :, :], scalar=-1.0, in1=sp[:, 0, :, :],
                                         op0=ALU.mult, op1=ALU.min).then_inc(tab_step, 1)
                dve.wait_ge(tab_act, 3)
                dve.scalar_tensor_tensor(out=sp[:, 3, :, :], in0=sp[:, 0, :, :], scalar=0.0, in1=sp[:, 2, :, :],
                                         op0=ALU.max, op1=ALU.add).then_inc(tab_step, 1)
                dve.wait_ge(tab_step, 3)
                dve.scalar_tensor_tensor(out=gl[:, :, :], in0=sp[:, 3, :, :], scalar=-1.0,
                                         in1=alog[:, None, :].to_broadcast([P, T, H]), op0=ALU.mult,
                                         op1=ALU.mult).then_inc(g_ready, 1)

            def tables_cumulated():
                dve.wait_ge(cum_done, 1)
                c0 = C[:, 64:64 + T * H].rearrange("p (t h) -> p t h", t=T)
                dve.tensor_copy(cum[:, 0, :, :], c0).then_inc(cum_ready, 1)
                dve.wait_ge(cum_ready, 1)
                dve.tensor_tensor(cum[:, 1, :, :], C[:, 128:128 + T * H].rearrange("p (t h) -> p t h", t=T),
                                  cum[:, 0, :, :], ALU.subtract).then_inc(cum_ready, 1)
                dve.wait_ge(g_ready, 1)
                dve.tensor_copy(tabs[:, :, C_G:C_G + T].rearrange("p h t -> p t h"), gl[:, :, :]).then_inc(cum_ready, 1)
                dve.tensor_copy(tabs[:, :, C_CUM:C_CUM + T].rearrange("p h t -> p t h"),
                                cum[:, 0, :, :]).then_inc(tabs_ready, 1)
                dve.wait_ge(tab_act, 4)
                dve.wait_ge(beta_ready, 1)
                dve.tensor_copy(tabs[:, :, C_EG], sp[:, 0, 1, :]).then_inc(tabs_ready, 1)
                dve.tensor_copy(tabs[:, :, C_DL], sp[:, 1, 0, :]).then_inc(tabs_ready, 1)
                dve.tensor_tensor(tabs[:, :, C_BEG], sp[:, 0, 1, :], tabs[:, :, C_BETA + 1], ALU.mult).then_inc(tabs_ready, 1)
                dve.wait_ge(cum_ready, 3)
                dve.memset(mx[:, 4:5], 0.0).then_inc(tabs_ready, 1)

            def dn_step(s, h, first=False):
                if s == S_TURN:
                    dve.wait_ge(dn_turned, h + 1)
                    dve.wait_ge(hs_ready, h + 1)
                    if not first:
                        dve.wait_ge(convs_ready, h)
                    for back in range(4):
                        for p in range(3):
                            tap = hs[:, C_CONV + 4 * p + 3 - back:C_CONV + 4 * p + 4 - back]
                            u_ = dn_ps[:, p * SEQ:(p + 1) * SEQ]
                            if back == 0:
                                dve.tensor_scalar(conv[:, p, :], u_, tap, None, ALU.mult).then_inc(conv_step, 1)
                            else:
                                dve.wait_ge(conv_step, 12 * h + 3 * (back - 1) + p + 1)
                                dve.scalar_tensor_tensor(out=conv[:, p, back:SEQ], in0=u_[:, 0:SEQ - back], scalar=tap,
                                                         in1=conv[:, p, back:SEQ], op0=ALU.mult,
                                                         op1=ALU.add).then_inc(conv_step, 1)
                if s == S_NAT:
                    dve.wait_ge(nat_done, h + 1)
                    for t in range(T):
                        dve.tensor_scalar(dsub[:, t, :], dn_ps[:, (6 + t) * P:(7 + t) * P],
                                          hs[:, C_CUM + t:C_CUM + t + 1], 0.0, ALU.subtract, ALU.min).then_inc(dsub_ready, 1)
                    dve.wait_ge(norm_exp, h + 1)
                    r0, v, r = rn[:, 1, :], rn[:, 2, :], rn[:, 3, :]
                    b = 3 * h
                    if not first:
                        dve.wait_ge(scaled_dve, 3 * h)
                    dve.scalar_tensor_tensor(out=v, in0=ss[:, :], scalar=EPS, in1=r0, op0=ALU.add,
                                             op1=ALU.mult).then_inc(norm_step, 1)
                    dve.wait_ge(norm_step, b + 1)
                    dve.scalar_tensor_tensor(out=v, in0=v, scalar=-0.5, in1=r0, op0=ALU.mult,
                                             op1=ALU.mult).then_inc(norm_step, 1)
                    dve.wait_ge(norm_step, b + 2)
                    dve.scalar_tensor_tensor(out=r, in0=v, scalar=1.5, in1=r0, op0=ALU.add,
                                             op1=ALU.mult).then_inc(norm_step, 1)
                    dve.wait_ge(norm_step, b + 3)
                    ps = dn_ps[:, 0:6 * P].rearrange("p (a t n) -> p a t n", a=3, t=T)
                    if not first:
                        dve.wait_ge(back_done, h)
                        dve.wait_ge(scaled_pool, 2 * h)
                        dve.wait_ge(u_done, h)
                    dve.tensor_tensor(tin[:, :, 0, :], ps[:, 1], r[:, 2:4, None].to_broadcast([P, T, P]),
                                      ALU.mult).then_inc(scaled_dve, 1)
                    dve.scalar_tensor_tensor(out=tin[:, :, 2, :], in0=ps[:, 0], scalar=SCALE,
                                             in1=r[:, 0:2, None].to_broadcast([P, T, P]), op0=ALU.mult,
                                             op1=ALU.mult).then_inc(scaled_dve, 1)
                    dve.tensor_tensor(vb[:, :, :], ps[:, 2], hs[:, C_BETA:C_BETA + 2, None].to_broadcast([P, T, P]),
                                      ALU.mult).then_inc(scaled_dve, 1)
                if s == S_BACK:
                    dve.wait_ge(back_done, h + 1)
                    if not first:
                        dve.wait_ge(o_done, h)
                    dve.tensor_copy(tT[:, 4 * P:7 * P], dn_ps[:, 4 * P:7 * P]).then_inc(tT_dve, 1)
                    dve.wait_ge(dexp_ready, h + 1)
                    dve.tensor_tensor(decay[:, :, :], dsub[:, :, :], causal[:, None, :].to_broadcast([P, T, P]),
                                      ALU.mult).then_inc(decay_ready, 1)
                if s == S_KK:
                    dve.wait_ge(kk_done, h + 1)
                    dve.wait_ge(decay_ready, h + 1)
                    if not first:
                        dve.wait_ge(mt_ready, LEVELS * h)
                        dve.wait_ge(u_done, h)
                    ps = A.rearrange("p (t a n) -> p t a n", t=T, a=2)
                    dve.tensor_tensor(lt[:, :, :], ps[:, :, 0, :], decay[:, :, :], ALU.mult).then_inc(lt_ready, 1)
                    dve.wait_ge(lt_ready, h + 1)
                    dve.tensor_tensor(ysb[:, :, :], lt[:, :, :], neg1[:, None, :].to_broadcast([P, T, P]),
                                      ALU.mult).then_inc(x1_step, 1)
                    dve.wait_ge(x1_step, 2 * h + 1)
                    dve.tensor_tensor(xs[:, T:2 * T, :], ysb[:, :, :], ident[:, None, :].to_broadcast([P, T, P]),
                                      ALU.add).then_inc(x1_step, 1)
                    dve.tensor_tensor(intra[:, :, :], ps[:, :, 1, :], decay[:, :, :], ALU.mult).then_inc(intra_ready, 1)
                if s in S_XY:
                    n = S_XY.index(s)
                    dve.wait_ge(xy_done, LEVELS * h + n + 1)
                    a = 0 if n < LEVELS - 1 else T
                    cur = xs[:, a:2 * T, :]
                    dve.tensor_tensor(cur, cur, B[:, a * P:2 * T * P].rearrange("p (t n) -> p t n", n=P),
                                      ALU.subtract).then_inc(xs_ready, 1)
                if s == S_U:
                    dve.wait_ge(u_done, h + 1)
                    dve.tensor_copy(wT[:, :], B[:, 3 * P:4 * P]).then_inc(wT_ready, 1)
                if s == S_S1:
                    dve.wait_ge(s1_done, h + 1)
                    dve.tensor_copy(s1[:, :], B[:, 0:P]).then_inc(s1_ready, 1)
                if s == S_WS:
                    dve.wait_ge(ws_done, h + 1)
                    dve.tensor_tensor(vnew[:, :], u[:, 1, :], A[:, 3 * P:4 * P], ALU.subtract).then_inc(vnew_ready, 1)
                if s == S_O1 + 1:
                    dve.wait_ge(o_exp, h + 1)
                    dve.wait_ge(dn_zg_ready, h + 1)
                    r0, v, r = ro[:, 1, :], ro[:, 2, :], ro[:, 3, :]
                    dve.tensor_scalar(v, so[:, :], 1.0 / P, EPS, ALU.mult, ALU.add).then_inc(o_step, 1)
                    dve.wait_ge(o_step, 3 * h + 1)
                    dve.tensor_tensor(v, v, r0, ALU.mult).then_inc(o_step, 1)
                    dve.wait_ge(o_step, 3 * h + 2)
                    dve.scalar_tensor_tensor(out=v, in0=v, scalar=-0.5, in1=r0, op0=ALU.mult,
                                             op1=ALU.mult).then_inc(o_step, 1)
                    dve.wait_ge(o_step, 3 * h + 3)
                    dve.scalar_tensor_tensor(out=r, in0=v, scalar=1.5, in1=r0, op0=ALU.add,
                                             op1=ALU.mult).then_inc(ro_ready, 1)
                    dve.wait_ge(ro_ready, h + 1)
                    for t in range(T):
                        dve.scalar_tensor_tensor(out=yb[:, t, :], in0=B[:, (1 + t) * P:(2 + t) * P], scalar=r[:, t:t + 1],
                                                 in1=dn_zg[:, t, :], op0=ALU.mult, op1=ALU.mult).then_inc(yb_ready, 1)
                if s == S_YT:
                    dve.wait_ge(yb_hi_ready, h + 1)
                    hd = bass.ds(h, 1)
                    dve.tensor_tensor(yb_lo[:, hd, :], A[:, 0:SEQ].rearrange("p (a n) -> p a n", a=1),
                                      yb_hi[:, hd, :].bitcast(F32), ALU.subtract).then_inc(yb_lo_ready, 1)

            def mo_step(s, h, first=False):
                if s == M_QK:
                    dve.wait_ge(qk_done, h + 1)
                    dve.wait_ge(hs_ready, h + 1)
                    if not first:
                        dve.wait_ge(prob_ready, T * h)
                    dve.scalar_tensor_tensor(out=sm[:, :], in0=far[:, :], scalar=hs[:, C_SLOPE:C_SLOPE + 1],
                                             in1=E[:, 0:3 * P], op0=ALU.mult, op1=ALU.add).then_inc(sm_ready, 1)
                    dve.wait_ge(sm_ready, h + 1)
                    dve.tensor_reduce(mx[:, 4:5], sm[:, 0:P], AX_X, ALU.max).then_inc(max_step, 1)
                    dve.tensor_reduce(mx[:, 5:6], sm[:, P:3 * P], AX_X, ALU.max).then_inc(max_step, 1)
                    dve.wait_ge(max_step, 2 * h + 2)
                    dve.tensor_scalar(mx[:, 0:2], mx[:, 4:6], -1.0, None, ALU.mult).then_inc(mx_ready, 1)
                if s == M_QK + 1:
                    dve.wait_ge(prob_ready, T * h + T)
                    dve.reciprocal(mx[:, 6:8], mx[:, 2:4]).then_inc(rsum_ready, 1)
                if s == M_PV:
                    dve.wait_ge(pv_done, h + 1)
                    dve.wait_ge(rsum_ready, h + 1)
                    dve.wait_ge(mo_z_ready, T * h + T)
                    if not first:
                        dve.wait_ge(yaT_done, h)
                    for t in range(T):
                        dve.scalar_tensor_tensor(out=ya[:, t, :], in0=E[:, t * P:(t + 1) * P], scalar=mx[:, 6 + t:7 + t],
                                                 in1=mo_z[:, t, :], op0=ALU.mult, op1=ALU.mult).then_inc(ya_ready, 1)
                if s == M_YT:
                    dve.wait_ge(ya_hi_ready, h + 1)
                    hd = bass.ds(h, 1)
                    dve.tensor_tensor(ya_lo[:, hd, :], C[:, 0:SEQ].rearrange("p (a n) -> p a n", a=1),
                                      ya_hi[:, hd, :].bitcast(F32), ALU.subtract).then_inc(ya_lo_ready, 1)

            def iteration(h, first):
                for s in range(SLOTS):
                    if s % 2 == 0:
                        n = s // 2 + LEAD
                        split(n % RING, h * UNITS + n)
                    if first and s == 8:
                        tables()
                    if first and s == 14:
                        tables_cumulated()
                    if not first:
                        dn_step(s + SLOTS, h - 1)
                    dn_step(s, h, first)
                    mo_step(s, h, first)

            iteration(0, True)
            with dve.Fori(1, H) as h:
                iteration(h, False)

            def tail_split(n):
                split(n % RING, n)

            def gate_a(c):
                for t in range(T):
                    wait_chunk(dve, t, 3 * H + c, FIRST_A + BU * c + BU - 1)
                    dve.wait_ge(sig_ready, c + 1)
                    dve.tensor_tensor(gate[:, c, t, :], gate[:, c, t, :], pj[c % 2][:, t, :], ALU.mult).then_inc(a_gated, 1)

            def gate_b(c):
                for t in range(T):
                    wait_chunk(dve, t, 3 * H + NC + c, FIRST_B + BU * c + BU - 1)
                    g = gate[:, NC + c, t, :]
                    dve.tensor_tensor(g, g, pj[c % 2][:, t, :], ALU.mult).then_inc(b_gated, 1)
                    dve.wait_ge(b_gated, T * c + t + 1)
                    dve.tensor_tensor(g, g, gate[:, c, t, :], ALU.add).then_inc(merged, 1)

            for c in range(NC):
                for j in range(BU):
                    tail_split(FIRST_A + BU * c + j + LEAD)
                    for s in (2 * j, 2 * j + 1):
                        dn_step(2 * BU * c + s + SLOTS, H - 1)
                    if j == BU - 1 and c == 1:
                        gate_a(0)
                    if j == 0 and c >= 2:
                        gate_a(c - 1)

            def merged_lo(c):
                ps = [dn_ps, mo_ps][c % 2]
                for half in range(2):
                    dve.wait_ge(mT_hi_ready, 2 * c + half + 1)
                    ks = slice(4 * c + 2 * half, 4 * c + 2 * half + 2)
                    dve.tensor_tensor(xt_lo[:, ks, :].rearrange("p k t -> p (k t)"), ps[:, half * CH:(half + 1) * CH],
                                      xt_hi[:, ks, :].rearrange("p k t -> p (k t)").bitcast(F32),
                                      ALU.subtract).then_inc(mT_lo_ready, 1)

            for n in range(NC * BU):
                tail_split(FIRST_B + n + LEAD)
                if n == 0:
                    gate_a(NC - 1)
                if n % BU == 0 and n > 0:
                    gate_b(n // BU - 1)
                if n % BU == 1 and n > BU:
                    merged_lo(n // BU - 1)
            gate_b(NC - 1)
            merged_lo(NC - 1)

            def residual(c):
                dve.wait_ge(x_again[c], 16)
                for t in range(T):
                    wait_chunk(dve, t, 3 * H + 2 * NC + c, FIRST_O + OU * c + OU - 1)
                    g = gate[:, c, t, :]
                    dve.tensor_tensor(g, g, pj[c % 2][:, t, :], ALU.add).then_inc(sum_ready, 1)

            for n in range(NC * OU - LEAD):
                tail_split(FIRST_O + n + LEAD)
                if n % OU == 0 and n > 0:
                    residual(n // OU - 1)
            residual(NC - 1)
            dve.wait_ge(f_squared, T * NC)
            dve.tensor_reduce(fr[:, 0, :], fs[:, :, :], AX_X, ALU.add).then_inc(f_total, 1)
            dve.wait_ge(f_exp, 1)
            newton(fr[:, 0, :], fr[:, 2, :], fr[:, 3, :], fr[:, 4, :], fr[:, 1, :], f_step, 0, fr_ready, 1.0 / D)
            dve.wait_ge(fr_ready, 1)
            dve.wait_ge(gain_landed, 16)
            fg = gate[:, NC:NC + NC // 2, :, :].rearrange("p c t n -> p (c t n)")
            for t in range(T):
                for c in range(NC):
                    g = gate[:, c, t, :]
                    dve.scalar_tensor_tensor(out=g, in0=g, scalar=fr[:, 1, t:t + 1], in1=fg[:, c * CH:(c + 1) * CH],
                                             op0=ALU.mult, op1=ALU.mult).then_inc(y_scaled, 1)


_INS = ['x', 'norm_gain', 'w_in', 'conv_w', 'a_log', 'dt_bias', 'dn_norm_gain', 'w_branch_a', 'w_branch_b',
        'w_out', 'final_norm_gain']


def kernel(**inputs):
    import numpy as _np
    import concourse.bacc as _bacc
    from concourse import mybir as _mybir
    from concourse.bass_utils import run_bass_kernel_spmd as _run

    nc = _bacc.Bacc("TRN2", target_bir_lowering=False, num_devices=1)
    arrays, args = {}, []
    for name in _INS:
        a = _np.ascontiguousarray(inputs[name])
        if name != 'final_norm_gain':
            a = a[0]
        arrays[f"in_{name}_dram"] = a
        args.append(nc.dram_tensor(f"in_{name}_dram", a.shape, _mybir.dt.from_np(a.dtype), kind="ExternalInput").ap())
    o = nc.dram_tensor("out_dram", (SEQ, D), F32, kind="ExternalOutput").ap()
    build(nc, *args, o)
    r = _run(nc, [arrays], core_ids=[0])
    return r.results[0]["out_dram"].reshape(1, SEQ, D)
```

```python
from contextlib import ExitStack

import concourse.bass as bass
from concourse import mybir

ALU = mybir.AluOpType
ACT = mybir.ActivationFunctionType
AX_X = mybir.AxisListType.X
F32 = mybir.dt.float32
F32R = mybir.dt.float32r

P = 128
SEQ, D = 256, 2048
T = SEQ // P
KT = D // P
H = 8
W = H * P
CH = 512
OFF_A = 0
OFF_B = 4 * W
OFF_BETA = 8 * W
OFF_GATE = OFF_BETA + 2 * H
NG = 2 * D // CH
NC = D // CH
RING = 4
UK = 2
UNITS = 3 * KT // UK
SLOTS = 3 * KT
LEAD = 3
BU = H // UK
OU = KT // UK
FIRST_A = H * UNITS
FIRST_B = FIRST_A + NC * BU
FIRST_O = FIRST_B + NC * BU
LEVELS = 6
EPS = 1e-6
SCALE = float(P) ** -0.5
FAR = -1e30

C_CONV, C_G, C_CUM, C_BETA, C_BEG, C_EG, C_DL, C_SLOPE, C_ALL = 0, 12, 14, 16, 18, 19, 20, 21, 22
XU = KT // UK

S_TURN, S_DEC, S_NAT, S_BACK, S_KK, S_X1 = 18, 20, 24, 29, 31, 33
S_Y = [35 + 3 * i for i in range(LEVELS)]
S_XY = [s + 1 for s in S_Y]
S_U, S_S1, S_WS, S_O1, S_YT = 52, 54, 55, 56, 60
M_TURN, M_QK, M_PT, M_PV, M_YT = 34, 36, 40, 42, 45


def build(nc, x, norm_gain, w_in, conv_w, a_log, dt_bias, dn_norm_gain, w_a, w_b, w_out,
          final_gain, out):
    ctx = ExitStack()
    with ctx:
        def sb(name, shape, dt=F32):
            return ctx.enter_context(nc.sbuf_tensor(name, shape, dt))

        def sem(name):
            return ctx.enter_context(nc.semaphore(name))

        w_raw = sb("w_raw", [P, RING, UK * CH])
        w_hi = sb("w_hi", [P, RING, UK * CH], F32R)
        w_lo = sb("w_lo", [P, RING, UK * CH], F32R)
        xt_hi = sb("xt_hi", [P, KT, SEQ], F32R)
        xt_lo = sb("xt_lo", [P, KT, SEQ], F32R)
        ya_hi = sb("ya_hi", [P, H, SEQ], F32R)
        ya_lo = sb("ya_lo", [P, H, SEQ], F32R)
        yb_hi = sb("yb_hi", [P, H, SEQ], F32R)
        yb_lo = sb("yb_lo", [P, H, SEQ], F32R)
        wba_hi, wba_lo = yb_hi[:, 0, :], yb_lo[:, 0, :]
        gate = sb("gate", [P, NG, T, CH])
        x_sb = gate[:, 0:NC, :, :].rearrange("p c t n -> p (c t n)").rearrange("p (t d) -> p t d", t=T)
        cols = sb("cols", [P, P])
        dn_gain = sb("dn_gain", [P, P])
        alog = sb("alog", [P, H])
        dtb = sb("dtb", [P, H])
        ident = sb("ident", [P, P])
        ones = sb("ones", [P, P])
        causal = sb("causal", [P, P])
        neg1 = sb("neg1", [P, P])
        levels = sb("levels", [P, LEVELS, P])
        far = sb("far", [P, 3 * P])
        rx = sb("rx", [P, 6])
        half = sb("half", [P, 4])
        tabs = sb("tabs", [P, H, C_ALL])
        hs = sb("hs", [P, C_ALL])
        ba = sb("ba", [P, T, 2 * H])
        sp = sb("sp", [P, 4, T, H])
        gl = sb("gl", [P, T, H])
        cum = sb("cum", [P, 2, T, H])
        dn_nat = sb("dn_nat", [P, T, CH])
        dn_z = sb("dn_z", [P, T, P])
        conv = sb("conv", [P, 3, SEQ])
        convs = sb("convs", [P, 3 * SEQ])
        baT = convs[0:2 * H, 2 * SEQ:3 * SEQ]
        rows = convs[:, 0:P]
        wba = conv[:, 0, :]
        ss = sb("ss", [P, 4])
        rn = sb("rn", [P, 2, 4])
        dsub = sb("dsub", [P, T, P])
        decay = sb("decay", [P, T, P])
        tin = sb("tin", [P, T, 3, P])
        qg1 = sb("qg1", [P, P])
        kbg1 = sb("kbg1", [P, P])
        kd0 = sb("kd0", [P, P])
        vb = sb("vb", [P, T, P])
        tT = sb("tT", [P, 7 * P])
        lt = sb("lt", [P, T, P])
        intra = sb("intra", [P, T, P])
        mt = sb("mt", [P, LEVELS, T, P])
        xs = sb("xs", [P, 2 * T, P])
        ysb = sb("ysb", [P, LEVELS, T, P])
        u = sb("u", [P, T, P])
        wT = sb("wT", [P, P])
        s1 = sb("s1", [P, P])
        vnew = sb("vnew", [P, P])
        so = sb("so", [P, 2])
        ro = sb("ro", [P, 2, 2])
        yb = sb("yb", [P, T, P])
        mo_nat = sb("mo_nat", [P, T, CH])
        mo_z = sb("mo_z", [P, T, P])
        moT = sb("moT", [P, 2, SEQ])
        sm = sb("sm", [P, 3 * P])
        prob = sb("prob", [P, 3 * P])
        probT = sb("probT", [P, 3 * P])
        mx = sb("mx", [P, 8])
        ya = sb("ya", [P, T, P])
        fs = sb("fs", [P, T, NC])
        fr = sb("fr", [P, 3, T])

        pj = [ctx.enter_context(nc.psum_tensor(f"pj{i}", [P, T, CH], F32)) for i in range(2)]
        dn_ps = ctx.enter_context(nc.psum_tensor("dn_ps", [P, 2 * CH], F32))
        mo_ps = ctx.enter_context(nc.psum_tensor("mo_ps", [P, 2 * CH], F32))
        A, B = dn_ps[:, 0:CH], dn_ps[:, CH:2 * CH]
        C, E = mo_ps[:, 0:CH], mo_ps[:, CH:2 * CH]

        w_landed = [sem(f"w_landed{i}") for i in range(RING)]
        hi_ready, lo_ready = sem("hi_ready"), sem("lo_ready")
        unit_used = sem("unit_used")
        x_landed = [sem(f"x_landed{i}") for i in range(NC)]
        rows_landed, small_landed, wba_landed = sem("rows_landed"), sem("small_landed"), sem("wba_landed")
        const_made, ident_made, const_step = sem("const_made"), sem("ident_made"), sem("const_step")
        cols_turned, cols_ready = sem("cols_turned"), sem("cols_ready")
        x_turned, xt_hi_ready, xt_lo_ready = sem("x_turned"), sem("xt_hi_ready"), sem("xt_lo_ready")
        x_squared, x_squared_act, rx_mean, rx_ready = (sem(n) for n in (
            "x_squared", "x_squared_act", "rx_mean", "rx_ready"))
        wba_hi_ready, wba_lo_ready = sem("wba_hi_ready"), sem("wba_lo_ready")
        ba_done, ba_ready, beta_ready, tab_step, tab_act, g_ready = (sem(n) for n in (
            "ba_done", "ba_ready", "beta_ready", "tab_step", "tab_act", "g_ready"))
        cum_done, cum_ready, tabs_ready, tabs_pool = (sem(n) for n in (
            "cum_done", "cum_ready", "tabs_ready", "tabs_pool"))
        baT_ready, ba_turned, table_loaded = sem("baT_ready"), sem("ba_turned"), sem("table_loaded")
        tile0_done = sem("tile0_done")
        dn_nat_ready, mo_nat_ready, gate_ready = sem("dn_nat_ready"), sem("mo_nat_ready"), sem("gate_ready")
        taps_ready, hs_ready, dec_done = sem("taps_ready"), sem("hs_ready"), sem("dec_done")
        dn_turned, conv_step, convs_ready, nat_done = (sem(n) for n in (
            "dn_turned", "conv_step", "convs_ready", "nat_done"))
        dn_z_ready, dn_zg_ready = sem("dn_z_ready"), sem("dn_zg_ready")
        dsub_ready, dexp_ready, decay_ready = sem("dsub_ready"), sem("dexp_ready"), sem("decay_ready")
        norm_squared, norm_eps, norm_ready = (sem(n) for n in (
            "norm_squared", "norm_eps", "norm_ready"))
        scaled_dve, scaled_act, scaled_pool = sem("scaled_dve"), sem("scaled_act"), sem("scaled_pool")
        back_done, tT_act, tT_dve, kk_done = sem("back_done"), sem("tT_act"), sem("tT_dve"), sem("kk_done")
        lt_ready, intra_ready, mt_ready = sem("lt_ready"), sem("intra_ready"), sem("mt_ready")
        x1_step, x1_done, x1_ready = sem("x1_step"), sem("x1_done"), sem("x1_ready")
        y_done, y_ready, xy_done, xs_ready, xsT_ready = (sem(n) for n in (
            "y_done", "y_ready", "xy_done", "xs_ready", "xsT_ready"))
        u_done, u_ready, wT_ready, s1_done, s1_ready = (sem(n) for n in (
            "u_done", "u_ready", "wT_ready", "s1_done", "s1_ready"))
        ws_done, vnew_ready, o_done = sem("ws_done"), sem("vnew_ready"), sem("o_done")
        o_squared, o_mean, ro_ready, yb_ready = (sem(n) for n in (
            "o_squared", "o_mean", "ro_ready", "yb_ready"))
        ybT_done, yb_hi_ready, yb_lo_ready = sem("ybT_done"), sem("yb_hi_ready"), sem("yb_lo_ready")
        mo_z_ready, mo_turned, moT_ready, qk_done = (sem(n) for n in (
            "mo_z_ready", "mo_turned", "moT_ready", "qk_done"))
        sm_ready, mx_ready, prob_ready, rsum_ready = (sem(n) for n in (
            "sm_ready", "mx_ready", "prob_ready", "rsum_ready"))
        max_step = sem("max_step")
        pt_done, pt_ready, pv_done, ya_ready = sem("pt_done"), sem("pt_ready"), sem("pv_done"), sem("ya_ready")
        yaT_done, ya_hi_ready, ya_lo_ready = sem("yaT_done"), sem("ya_hi_ready"), sem("ya_lo_ready")
        sig_ready, a_gated, b_gated, merged = sem("sig_ready"), sem("a_gated"), sem("b_gated"), sem("merged")
        mT_done, mT_hi_ready, mT_lo_ready = sem("mT_done"), sem("mT_hi_ready"), sem("mT_lo_ready")
        x_again = [sem(f"x_again{i}") for i in range(NC)]
        gain_landed, sum_ready, f_squared = sem("gain_landed"), sem("sum_ready"), sem("f_squared")
        f_total, f_mean, fr_ready, f_gained = (sem(n) for n in (
            "f_total", "f_mean", "fr_ready", "f_gained"))
        last_gained, y_act, y_dve, stored = (sem(n) for n in ("last_gained", "y_act", "y_dve", "stored"))

        block = ctx.enter_context(nc.Block())

        def halves(m, n, e):
            return m.rearrange("p t (b e c) -> p t b e c", e=2, c=2 << n)[:, :, :, e, :]

        def packed(bank, i, n):
            return bank[:, i * P:(i + 1) * P].rearrange("p (t b c) -> p t b c", t=T, c=2 << n)

        def wait_chunk(eng, t, chunk, last_unit):
            if t == 0:
                eng.wait_ge(tile0_done, chunk + 1)
            else:
                eng.wait_ge(unit_used, last_unit + 1)

        @block.sync
        def _(sp):
            sp.dma_start(rows[0:96, :], conv_w.rearrange("j (b c) -> (j b) c", c=P)).then_inc(rows_landed, 16)
            sp.dma_start(rows[96:96 + KT, :], norm_gain.rearrange("(k c) -> k c", c=P)).then_inc(rows_landed, 16)

            def iteration(h, first):
                head_col = h * P if first else sp.snap(h * P)
                gate_col = OFF_GATE if first else sp.snap(h * CH + OFF_GATE)
                for j in range(UNITS):
                    slot = j % RING
                    if first and j < NC:
                        cs = slice(j * CH, (j + 1) * CH)
                        sp.dma_start(x_sb[:, :, cs], x[:, cs].rearrange("(t p) n -> p t n", p=P)
                                     ).then_inc(x_landed[j], 16)
                    used = None if first and j < RING else h * UNITS + j - RING + 1
                    k = (j % (KT // UK)) * UK
                    if used is not None:
                        sp.wait_ge(lo_ready, used)
                    for i in reversed(range(UK)):
                        r = slice((k + i) * P, (k + i + 1) * P)
                        dst = w_raw[:, slot, i * CH:(i + 1) * CH]
                        if j < UNITS // 3 * 2:
                            branch = 1 if j < UNITS // 3 else 0
                            dst = dst.rearrange("p (a n) -> p a n", a=4)
                            src = w_in[r, branch * 4 * W:(branch + 1) * 4 * W].rearrange(
                                "p (a w) -> p a w", a=4)[:, :, bass.ds(head_col, P)]
                        else:
                            src = w_in[r, bass.ds(gate_col, CH)]
                        sp.dma_start(dst, src).then_inc(w_landed[slot], 16)
                    if first and j == RING - 1:
                        sp.dma_start(wba[:, :].rearrange("p (k n) -> p k n", k=KT),
                                     w_in[:, OFF_BETA:OFF_GATE].rearrange("(k p) n -> p k n", p=P)
                                     ).then_inc(wba_landed, 16)
                        sp.dma_start(dn_gain[:, :], dn_norm_gain.rearrange("(a n) -> a n", a=1).to_broadcast([P, P])
                                     ).then_inc(small_landed, 16)
                        sp.dma_start(alog[:, :], a_log.rearrange("(a n) -> a n", a=1).to_broadcast([P, H])
                                     ).then_inc(small_landed, 16)
                        sp.dma_start(dtb[:, :], dt_bias.rearrange("(a n) -> a n", a=1).to_broadcast([P, H])
                                     ).then_inc(small_landed, 16)

            iteration(0, True)
            with sp.Fori(1, H) as h:
                iteration(h, False)

            def chunk(wmat, c, units, first_unit):
                col = c * CH if isinstance(c, int) else sp.snap(c * CH)
                for j in range(units):
                    slot = j % RING
                    sp.wait_ge(lo_ready, c * units + (first_unit + j - RING + 1))
                    for i in reversed(range(UK)):
                        k = UK * j + i
                        sp.dma_start(w_raw[:, slot, i * CH:(i + 1) * CH],
                                     wmat[k * P:(k + 1) * P, bass.ds(col, CH)]).then_inc(w_landed[slot], 16)

            with sp.Fori(0, NC) as c:
                chunk(w_a, c, BU, FIRST_A)
            with sp.Fori(0, NC) as c:
                chunk(w_b, c, BU, FIRST_B)
            for c in range(NC):
                chunk(w_out, c, OU, FIRST_O)
                if c == 0:
                    sp.wait_ge(merged, T * NC)
                    for j in range(NC):
                        sp.dma_start(gate[:, j, :, :], x[:, j * CH:(j + 1) * CH].rearrange("(t p) n -> p t n", p=P)
                                     ).then_inc(x_again[j], 16)
                    sp.wait_ge(mT_done, 2 * NC)
                    sp.dma_start(gate[:, NC:NC + NC // 2, :, :].rearrange("p c t n -> p (c t n)"),
                                 final_gain.rearrange("(a n) -> a n", a=1).to_broadcast([P, D])
                                 ).then_inc(gain_landed, 16)
            n = (NC - 1) * CH
            for t, ready in ((1, y_dve), (0, y_act)):
                sp.wait_ge(ready, 1)
                sp.dma_start(out[t * P:(t + 1) * P, 0:n].rearrange("p (c n) -> p c n", n=CH),
                             gate[:, 0:NC - 1, t, :]).then_inc(stored, 16)
            for t in range(T):
                sp.wait_ge(y_dve, 2 + t)
                sp.dma_start(out[t * P:(t + 1) * P, n:D], gate[:, NC + NC // 2, t, :]).then_inc(stored, 16)
            sp.wait_ge(stored, 16 * 2 * T)

        @block.gpsimd
        def _(pool):
            pool.memset(ident[:, :], 0.0).then_inc(const_step, 1)
            pool.wait_ge(const_step, 1)
            pool.affine_select(out=ident[:, :], in_=ident[:, :], compare_op=ALU.not_equal, fill=1.0, base=0,
                               pattern=[[-1, P]], channel_multiplier=1).then_inc(ident_made, 1)
            pool.memset(ones[:, :], 1.0).then_inc(const_step, 1)
            pool.memset(half[:, :], -0.5).then_inc(const_step, 1)
            pool.wait_ge(const_step, 3)
            pool.affine_select(out=causal[:, :], in_=ones[:, :], compare_op=ALU.is_ge, fill=0.0, base=0,
                               pattern=[[1, P]], channel_multiplier=-1).then_inc(const_step, 1)
            pool.iota(sm[:, 0:P], pattern=[[1, P]], base=0, channel_multiplier=-1,
                      allow_small_or_imprecise_dtypes=True).then_inc(const_step, 1)
            pool.iota(sm[:, P:3 * P], pattern=[[1, 2 * P]], base=-P, channel_multiplier=-1,
                      allow_small_or_imprecise_dtypes=True).then_inc(const_step, 1)
            pool.wait_ge(const_step, 6)
            pool.affine_select(out=far[:, 0:P], in_=sm[:, 0:P], compare_op=ALU.is_ge, fill=FAR, base=0,
                               pattern=[[-1, P]], channel_multiplier=1).then_inc(const_step, 1)
            pool.affine_select(out=far[:, P:3 * P], in_=sm[:, P:3 * P], compare_op=ALU.is_ge, fill=FAR, base=P,
                               pattern=[[-1, 2 * P]], channel_multiplier=1).then_inc(const_step, 1)
            done = 8
            for n in range(LEVELS + 1):
                s = 1 << n
                m = neg1[:, :] if n == 0 else levels[:, n - 1, :]
                blocks = m.rearrange("p (b e c) -> p b e c", e=2, c=s)
                pool.memset(m, -1.0 if n == 0 else 1.0).then_inc(const_step, 1)
                done += 1
                pool.wait_ge(const_step, done)
                pool.affine_select(out=blocks, in_=blocks, compare_op=ALU.is_ge, fill=0.0, base=-1,
                                   pattern=[[0, P // (2 * s)], [1, 2], [0, s]], channel_multiplier=0).then_inc(const_step, 1)
                pool.wait_ge(const_step, done + 1)
                pool.affine_select(out=blocks, in_=blocks, compare_op=ALU.is_ge, fill=0.0, base=0,
                                   pattern=[[-2 * s, P // (2 * s)], [0, 2], [0, s]], channel_multiplier=1).then_inc(const_step, 1)
                pool.wait_ge(const_step, done + 2)
                pool.affine_select(out=blocks, in_=blocks, compare_op=ALU.is_ge, fill=0.0, base=s - 1,
                                   pattern=[[2 * s, P // (2 * s)], [0, 2], [0, s]], channel_multiplier=-1).then_inc(const_step, 1)
                done += 3
            for h in range(H):
                pool.memset(tabs[:, h, C_SLOPE:C_SLOPE + 1], 2.0 ** (-8.0 * (h + 1) / H) / SCALE).then_inc(tabs_pool, 1)
            pool.wait_ge(const_step, done)
            pool.memset(ysb[:, :, :, :], 0.0).then_inc(const_made, 1)

            def inv_sqrt(dst, src, n):
                return pool.tensor_tensor(dst, src, half[:, 0:n], ALU.pow)

            def output_norm(h):
                pool.wait_ge(o_mean, h + 1)
                inv_sqrt(ro[:, 1, :], ro[:, 0, :], T).then_inc(ro_ready, 1)

            def head(h, first):
                if not first:
                    output_norm(h - 1)
                if not first:
                    pool.wait_ge(conv_step, 12 * h)
                    pool.wait_ge(sm_ready, h)
                    pool.wait_ge(scaled_act, 3 * h)
                    pool.wait_ge(scaled_dve, 3 * h)
                row = tabs[:, bass.ds(h, 1), :]
                pool.tensor_copy(hs[:, 0:C_G], row[:, :, 0:C_G].rearrange("p a c -> p (a c)")).then_inc(taps_ready, 1)
                if first:
                    pool.wait_ge(tabs_ready, 8)
                pool.tensor_copy(hs[:, C_G:C_ALL], row[:, :, C_G:C_ALL].rearrange("p a c -> p (a c)")).then_inc(hs_ready, 1)
                pool.wait_ge(dn_z_ready, h + 1)
                pool.tensor_tensor(dn_z[:, :, :], dn_z[:, :, :],
                                   dn_gain[:, None, :].to_broadcast([P, T, P]), ALU.mult).then_inc(dn_zg_ready, 1)
                pool.wait_ge(norm_eps, h + 1)
                if not first:
                    pool.wait_ge(scaled_dve, 3 * h)
                inv_sqrt(rn[:, 1, :], rn[:, 0, :], 4).then_inc(norm_ready, 1)
                pool.wait_ge(scaled_dve, 3 * h + 1)
                if not first:
                    pool.wait_ge(s1_done, h)
                for dst, t, col in ((kd0, 0, C_DL), (kbg1, 1, C_BEG)):
                    pool.tensor_tensor(dst[:, :], tin[:, t, 0, :], hs[:, col:col + 1].to_broadcast([P, P]),
                                       ALU.mult).then_inc(scaled_pool, 1)
                pool.wait_ge(lt_ready, h + 1)
                for n in range(LEVELS):
                    pool.tensor_tensor(mt[:, n, :, :], lt[:, :, :],
                                       levels[:, n, None, :].to_broadcast([P, T, P]), ALU.mult).then_inc(mt_ready, 1)

            pool.wait_ge(rx_mean, 1)
            inv_sqrt(rx[:, 4:6], rx[:, 2:4], T).then_inc(rx_ready, 1)
            pool.wait_ge(tabs_pool, H)
            pool.wait_ge(tabs_ready, 3)
            pool.wait_ge(small_landed, 48)
            head(0, True)
            with pool.Fori(1, H) as h:
                head(h, False)
            output_norm(H - 1)
            pool.wait_ge(gain_landed, 16)
            fg = gate[:, NC:NC + NC // 2, :, :].rearrange("p c t n -> p (c t n)")
            for c in range(NC - 1):
                for t in range(T):
                    pool.wait_ge(f_squared, T * c + t + 1)
                    g = gate[:, c, t, :]
                    pool.tensor_tensor(g, g, fg[:, c * CH:(c + 1) * CH], ALU.mult).then_inc(f_gained, 1)
            pool.wait_ge(f_mean, 1)
            inv_sqrt(fr[:, 2, :], fr[:, 1, :], T).then_inc(fr_ready, 1)

        @block.tensor
        def _(pe):
            pe.wait_ge(ident_made, 1)
            pe.wait_ge(rows_landed, 32)
            pe.transpose(E[:, 0:96 + KT], rows[0:96 + KT, :], ident[0:96 + KT, 0:96 + KT]).then_inc(cols_turned, 1)
            banks = [A, B, C, E]

            def turn_x(g):
                if g % 2 == 0:
                    pe.wait_ge(x_landed[g // 2], 16)
                if g == 3:
                    pe.wait_ge(cols_ready, 1)
                if g >= 4:
                    pe.wait_ge(xt_lo_ready, 2 * (g - 3))
                for q in range(4):
                    k, t = 2 * g + q // 2, q % 2
                    mm = pe.transpose(banks[g % 4][:, q * P:(q + 1) * P], x_sb[:, t, k * P:(k + 1) * P], ident[:, :])
                mm.then_inc(x_turned, 1)

            turn_x(0)
            turn_x(1)

            def unit(slot, number, hi, lo, k0, bank, kt_all, free, between=None):
                pe.wait_ge(lo_ready, number + 1)
                for t in range(T):
                    if k0 == 0:
                        free(t)
                    for i in range(UK):
                        k = k0 + i
                        tok = slice(t * P, (t + 1) * P)
                        cs = slice(i * CH, (i + 1) * CH)
                        pe.matmul(bank[:, t, :], hi[:, k, tok], w_hi[:, slot, cs], start=(k == 0), stop=False)
                        pe.matmul(bank[:, t, :], hi[:, k, tok], w_lo[:, slot, cs], start=False, stop=False)
                        mm = pe.matmul(bank[:, t, :], lo[:, k, tok], w_hi[:, slot, cs], start=False,
                                       stop=(k == kt_all - 1))
                    if t == T - 1:
                        mm.then_inc(unit_used, 1)
                    elif k == kt_all - 1:
                        mm.then_inc(tile0_done, 1)
                    if between is not None:
                        between(t)

            def dn_step(s, h, first=False):
                if s == S_TURN:
                    pe.wait_ge(dn_nat_ready, T * h + T)
                    if not first:
                        pe.wait_ge(yb_lo_ready, h)
                    for p in range(3):
                        for t in range(T):
                            mm = pe.transpose(dn_ps[:, (p * T + t) * P:(p * T + t + 1) * P],
                                              dn_nat[:, t, p * P:(p + 1) * P], ident[:, :])
                    mm.then_inc(dn_turned, 1)
                if s == S_DEC:
                    pe.wait_ge(hs_ready, h + 1)
                    if not first:
                        pe.wait_ge(ya_ready, T * h)
                    for t in range(T):
                        mm = pe.matmul(E[:, t * P:(t + 1) * P], hs[:, C_G + t:C_G + t + 1].to_broadcast([P, P]),
                                       causal[:, :], start=True, stop=True)
                    mm.then_inc(dec_done, 1)
                if s == S_NAT:
                    pe.wait_ge(convs_ready, h + 1)
                    for i in range(3 * T):
                        mm = pe.transpose(dn_ps[:, i * P:(i + 1) * P], convs[:, i * P:(i + 1) * P], ident[:, :])
                    mm.then_inc(nat_done, 1)
                if s == S_BACK:
                    pe.wait_ge(scaled_dve, 3 * h + 3)
                    pe.wait_ge(scaled_act, 3 * h + 3)
                    for t in range(T):
                        for p in range(3):
                            i = 3 * t + p
                            pe.transpose(dn_ps[:, i * P:(i + 1) * P], tin[:, t, p, :], ident[:, :])
                    pe.transpose(dn_ps[:, 6 * P:7 * P], qg1[:, :], ident[:, :]).then_inc(back_done, 1)
                if s == S_KK:
                    pe.wait_ge(tT_act, h + 1)
                    pe.wait_ge(tT_dve, h + 1)
                    for t in range(T):
                        o = 3 * P * t
                        mm = pe.matmul(A[:, 2 * P * t:2 * P * (t + 1)], tT[:, o:o + P], tT[:, o + P:o + 3 * P],
                                       start=True, stop=True)
                    mm.then_inc(kk_done, 1)
                if s == S_X1:
                    pe.wait_ge(x1_step, 2 * h + 2)
                    for t in range(T):
                        mm = pe.transpose(B[:, t * P:(t + 1) * P], xs[:, T + t, :], ident[:, :])
                    mm.then_inc(x1_done, 1)
                if s in S_Y:
                    n = S_Y.index(s)
                    if n == 0:
                        pe.wait_ge(x1_ready, h + 1)
                        pe.wait_ge(lt_ready, h + 1)
                        pe.wait_ge(intra_ready, h + 1)
                    else:
                        pe.wait_ge(xs_ready, (LEVELS - 1) * h + n)
                    pe.wait_ge(mt_ready, LEVELS * h + n + 1)
                    x = halves(xs[:, 0:T, :], n, 0)
                    for t in range(T):
                        mm = pe.matmul(packed(A, 0, n)[:, t], mt[:, n, t, :], x[:, t], start=True, stop=True)
                    mm.then_inc(y_done, 1)
                if s in S_XY:
                    n = S_XY.index(s)
                    pe.wait_ge(y_ready, LEVELS * h + n + 1)
                    pe.wait_ge(xsT_ready, LEVELS * h + n)
                    y = halves(ysb[:, n, :, :], n, 0)
                    xT = halves(xs[:, T:2 * T, :], n, 1)
                    if n < LEVELS - 1:
                        for t in range(T):
                            pe.matmul(packed(B, 0, n)[:, t], xs[:, T + t, :], y[:, t], start=True, stop=True)
                    for t in range(T):
                        mm = pe.matmul(packed(B, 1, n)[:, t], ysb[:, n, t, :], xT[:, t], start=True, stop=True)
                    mm.then_inc(xy_done, 1)
                if s == S_U:
                    pe.wait_ge(xsT_ready, LEVELS * h + LEVELS)
                    pe.wait_ge(scaled_pool, 2 * h + 2)
                    for t in range(T):
                        pe.matmul(A[:, t * P:(t + 1) * P], xs[:, T + t, :], vb[:, t, :], start=True, stop=True)
                    pe.matmul(B[:, 3 * P:4 * P], kbg1[:, :], xs[:, T + 1, :], start=True, stop=True).then_inc(u_done, 1)
                if s == S_S1:
                    pe.wait_ge(u_ready, h + 1)
                    pe.wait_ge(wT_ready, h + 1)
                    pe.matmul(B[:, P:2 * P], intra[:, 0, :], u[:, 0, :], start=True, stop=True)
                    pe.matmul(B[:, 0:P], kd0[:, :], u[:, 0, :], start=True, stop=True).then_inc(s1_done, 1)
                if s == S_WS:
                    pe.wait_ge(s1_ready, h + 1)
                    pe.matmul(A[:, 3 * P:4 * P], wT[:, :], s1[:, :], start=True, stop=True).then_inc(ws_done, 1)
                if s == S_O1:
                    pe.wait_ge(vnew_ready, h + 1)
                    pe.matmul(B[:, 2 * P:3 * P], tT[:, 6 * P:7 * P], s1[:, :], start=True, stop=False)
                    pe.matmul(B[:, 2 * P:3 * P], intra[:, 1, :], vnew[:, :], start=False, stop=True).then_inc(o_done, 1)
                if s == S_YT:
                    pe.wait_ge(yb_ready, T * h + T)
                    for t in range(T):
                        mm = pe.transpose(A[:, t * P:(t + 1) * P], yb[:, t, :], ident[:, :])
                    mm.then_inc(ybT_done, 1)

            def mo_step(s, h, first=False):
                if s == M_TURN:
                    pe.wait_ge(mo_nat_ready, T * h + T)
                    pe.wait_ge(dsub_ready, T * h + T)
                    if not first:
                        pe.wait_ge(ya_lo_ready, h)
                    for p in range(2):
                        for t in range(T):
                            mm = pe.transpose(C[:, (p * T + t) * P:(p * T + t + 1) * P],
                                              mo_nat[:, t, p * P:(p + 1) * P], ident[:, :])
                    mm.then_inc(mo_turned, 1)
                if s == M_QK:
                    pe.wait_ge(moT_ready, h + 1)
                    pe.matmul(E[:, 0:P], moT[:, 0, 0:P], moT[:, 1, 0:P], start=True, stop=True)
                    pe.matmul(E[:, P:3 * P], moT[:, 0, P:2 * P], moT[:, 1, :], start=True, stop=True).then_inc(qk_done, 1)
                if s == M_PT:
                    pe.wait_ge(prob_ready, T * h + T)
                    for i in range(3):
                        mm = pe.transpose(C[:, i * P:(i + 1) * P], prob[:, i * P:(i + 1) * P], ident[:, :])
                    mm.then_inc(pt_done, 1)
                if s == M_PV:
                    pe.wait_ge(pt_ready, h + 1)
                    v = [mo_nat[:, t, 2 * P:3 * P] for t in range(T)]
                    pe.matmul(E[:, 0:P], probT[:, 0:P], v[0], start=True, stop=True)
                    pe.matmul(E[:, P:2 * P], probT[:, P:2 * P], v[0], start=True, stop=False)
                    pe.matmul(E[:, P:2 * P], probT[:, 2 * P:3 * P], v[1], start=False, stop=True).then_inc(pv_done, 1)
                if s == M_YT:
                    pe.wait_ge(ya_ready, T * h + T)
                    for t in range(T):
                        mm = pe.transpose(C[:, t * P:(t + 1) * P], ya[:, t, :], ident[:, :])
                    mm.then_inc(yaT_done, 1)

            def beta_decay_inputs():
                pe.wait_ge(const_made, 1)
                pe.wait_ge(wba_hi_ready, 1)
                pe.wait_ge(wba_lo_ready, 1)
                n = 2 * H
                for k in range(KT):
                    cs = slice(k * n, (k + 1) * n)
                    pe.matmul(E[0:n, 0:SEQ], wba_hi[:, cs], xt_hi[:, k, :], start=(k == 0), stop=False)
                    pe.matmul(E[0:n, 0:SEQ], wba_lo[:, cs], xt_hi[:, k, :], start=False, stop=False)
                    mm = pe.matmul(E[0:n, 0:SEQ], wba_hi[:, cs], xt_lo[:, k, :], start=False, stop=(k == KT - 1))
                mm.then_inc(ba_done, 1)

            def beta_decay_turned():
                pe.wait_ge(baT_ready, 1)
                n = 2 * H
                for t in range(T):
                    mm = pe.transpose(C[:, t * n:(t + 1) * n], baT[:, t * P:(t + 1) * P], ident[0:n, 0:n])
                mm.then_inc(ba_turned, 1)

            def cumulate():
                pe.wait_ge(g_ready, 1)
                g = gl[:, :, :].rearrange("p t h -> p (t h)")
                pe.matmul(C[:, 64:64 + T * H], causal[:, :], g, start=True, stop=True)
                pe.matmul(C[:, 128:128 + T * H], ones[:, :], g, start=True, stop=True).then_inc(cum_done, 1)

            def iteration(h, first):
                for j in range(UNITS):
                    c = j // (KT // UK)
                    k0 = (j % (KT // UK)) * UK

                    def free(t, c=c):
                        if c == 0:
                            if not first:
                                pe.wait_ge(gate_ready, T * h - T + t + 1)
                        if c == 1 and not first:
                            pe.wait_ge(mo_nat_ready, T * h - T + t + 1)
                        if c == 2:
                            pe.wait_ge(dn_nat_ready, T * h + t + 1)

                    if first and j < XU:
                        pe.wait_ge(xt_lo_ready, UK * j + UK)

                    def between(t, j=j):
                        s = T * j + t
                        if not first:
                            dn_step(s + SLOTS, h - 1)
                        dn_step(s, h, first)
                        mo_step(s, h, first)
                        if first and s == 2 * XU - 2:
                            beta_decay_turned()
                        if first and s == 2 * XU + 1:
                            cumulate()

                    unit(j % RING, h * UNITS + j, xt_hi, xt_lo, k0, pj[c % 2], KT, free, between)
                    if first:
                        for g in ((2, 3) if j == 0 else (j + 3,)):
                            if g < XU:
                                turn_x(g)
                    if first and j == XU - 2:
                        beta_decay_inputs()

            iteration(0, True)
            with pe.Fori(1, H) as h:
                iteration(h, False)

            def branch(c, hi, lo, first_unit, number, dn):
                for j in range(BU):
                    def free(t):
                        if number == 0:
                            pe.wait_ge(gate_ready, T * (H - 1) + t + 1)
                        elif number == 1:
                            pe.wait_ge(mo_nat_ready, T * H)
                        else:
                            pe.wait_ge(a_gated, T * (number - 2) + t + 1)

                    def between(t, j=j):
                        dn_step(dn + T * j + t + SLOTS, H - 1)

                    unit(j % RING, first_unit + c * BU + j, hi, lo, UK * j, pj[number % 2], H, free, between)

            pe.wait_ge(ya_hi_ready, H)
            pe.wait_ge(ya_lo_ready, H)
            for c in range(NC):
                branch(c, ya_hi, ya_lo, FIRST_A, c, 2 * BU * c)
            pe.wait_ge(yb_hi_ready, H)
            pe.wait_ge(yb_lo_ready, H)

            def turn_merged(c):
                pe.wait_ge(merged, T * c + T)
                ps = [dn_ps, mo_ps][c % 2]
                if c >= 2:
                    pe.wait_ge(mT_lo_ready, 2 * (c - 1))
                for half in range(2):
                    for q in range(4):
                        i, t = 2 * half + q // 2, q % 2
                        mm = pe.transpose(ps[:, (4 * half + q) * P:(4 * half + q + 1) * P],
                                          gate[:, NC + c, t, i * P:(i + 1) * P], ident[:, :])
                    mm.then_inc(mT_done, 1)

            for c in range(NC):
                def free(t, c=c):
                    if c < 2:
                        pe.wait_ge(a_gated, T * (c + 2) + t + 1)
                    else:
                        pe.wait_ge(b_gated, T * (c - 2) + t + 1)
                for j in range(BU):
                    unit(j % RING, FIRST_B + c * BU + j, yb_hi, yb_lo, UK * j, pj[c % 2], H, free)
                    if j == 1 and c > 0:
                        turn_merged(c - 1)
            for c in range(NC):
                def free(t, c=c):
                    if c < 2:
                        pe.wait_ge(b_gated, T * (c + 2) + t + 1)
                    else:
                        pe.wait_ge(sum_ready, T * (c - 2) + t + 1)
                for j in range(OU):
                    if c == 0:
                        pe.wait_ge(mT_hi_ready, j + 1)
                        pe.wait_ge(mT_lo_ready, j + 1)
                    unit(j % RING, FIRST_O + c * OU + j, xt_hi, xt_lo, UK * j, pj[c % 2], KT, free)
                    if c == 0 and j == 2:
                        turn_merged(NC - 1)

        @block.scalar
        def _(act):
            def split(slot, number, landed, first=False):
                act.wait_ge(w_landed[slot], landed)
                if not first:
                    act.wait_ge(unit_used, number - RING + 1)
                act.activation(w_hi[:, slot, :], w_raw[:, slot, :], ACT.Copy).then_inc(hi_ready, 1)

            act.wait_ge(ident_made, 1)
            act.activation(fr[:, 0, 0:1], ident[:, 0:1], ACT.Copy).then_inc(table_loaded, 1)
            act.wait_ge(cols_ready, 1)
            x_banks = [A, B, C, E]
            for g in range(XU):
                act.wait_ge(x_turned, g + 1)
                for k in (2 * g, 2 * g + 1):
                    act.activation(xt_hi[:, k, :], x_banks[g % 4][:, (k % 2) * SEQ:(k % 2 + 1) * SEQ], ACT.Copy,
                                   scale=cols[:, 96 + k:97 + k]).then_inc(xt_hi_ready, 1)
                split(g % RING, g, (g // RING + 1) * 32, g < RING)

            def start_stats():
                act.wait_ge(wba_landed, 16)
                act.activation(wba_hi, wba[:, :], ACT.Copy).then_inc(wba_hi_ready, 1)
                act.activation(gate[:, NC:NC + NC // 2, :, :].rearrange("p c t n -> p (c t n)"), x_sb[:, 0, :], ACT.Square,
                               accum_out=rx[:, 0:1]).then_inc(x_squared_act, 1)

            def tables():
                act.wait_ge(ba_done, 1)
                act.activation(baT[:, :], E[0:2 * H, 0:SEQ], ACT.Copy).then_inc(baT_ready, 1)
                act.wait_ge(rx_ready, 1)
                act.wait_ge(ba_turned, 1)
                for t in range(T):
                    act.activation(ba[:, t, :], C[:, t * 2 * H:(t + 1) * 2 * H], ACT.Copy,
                                   scale=rx[:, 4 + t:5 + t]).then_inc(ba_ready, 1)
                act.wait_ge(ba_ready, T)
                act.wait_ge(tab_step, 2)
                act.activation(sp[:, 1, :, :], sp[:, 1, :, :], ACT.Exp).then_inc(tab_act, 1)
                act.wait_ge(small_landed, 48)
                act.activation(alog[:, :], alog[:, :], ACT.Exp).then_inc(tab_act, 1)
                act.wait_ge(tab_act, 2)
                act.activation(sp[:, 2, :, :], sp[:, 1, :, :], ACT.Ln, bias=ones[:, 0:1]).then_inc(tab_act, 1)

            def tables_cumulated():
                act.wait_ge(cum_ready, 2)
                act.activation(sp[:, 0:2, :, :], cum[:, :, :, :], ACT.Exp).then_inc(tab_act, 1)
                act.activation(tabs[:, :, C_BETA:C_BETA + T].rearrange("p h t -> p t h"), ba[:, :, 0:H],
                               ACT.Sigmoid).then_inc(beta_ready, 1)

            def dn_step(s, h, first=False):
                if s == S_TURN - 2:
                    if first:
                        act.wait_ge(rx_ready, 1)
                    if not first:
                        act.wait_ge(dn_turned, h)
                        act.wait_ge(dn_z_ready, h)
                    for t in range(T):
                        wait_chunk(act, t, 3 * h, UNITS * h + UNITS // 3 - 1)
                        act.activation(dn_nat[:, t, :], pj[0][:, t, :], ACT.Copy,
                                       scale=rx[:, 4 + t:5 + t]).then_inc(dn_nat_ready, 1)
                if s == S_DEC + 1:
                    act.wait_ge(dsub_ready, T * h + T)
                    act.activation(dsub[:, :, :], dsub[:, :, :], ACT.Exp).then_inc(dexp_ready, 1)
                if s == S_NAT - 1:
                    act.wait_ge(conv_step, 12 * h + 12)
                    if not first:
                        act.wait_ge(nat_done, h)
                    act.activation(convs[:, :], conv[:, :, :].rearrange("p a t -> p (a t)"), ACT.Silu).then_inc(convs_ready, 1)
                    if not first:
                        act.wait_ge(yb_ready, T * h)
                    act.activation(dn_z[:, :, :], dn_nat[:, :, 3 * P:4 * P], ACT.Silu).then_inc(dn_z_ready, 1)
                if s == S_NAT:
                    act.wait_ge(nat_done, h + 1)
                    if not first:
                        act.wait_ge(norm_eps, h)
                    for i in range(2 * T):
                        act.activation(mt[:, i // 2, i % 2, :], dn_ps[:, i * P:(i + 1) * P], ACT.Square,
                                       accum_out=ss[:, i:i + 1]).then_inc(norm_squared, 1)
                if s == S_NAT + 2:
                    if not first:
                        act.wait_ge(back_done, h)
                    act.wait_ge(scaled_dve, 3 * h + 1)
                    for t in range(T):
                        act.activation(tin[:, t, 1, :], tin[:, t, 0, :], ACT.Copy,
                                       scale=hs[:, C_BETA + t:C_BETA + t + 1]).then_inc(scaled_act, 1)
                    act.wait_ge(scaled_dve, 3 * h + 2)
                    act.activation(qg1[:, :], tin[:, 1, 2, :], ACT.Copy,
                                   scale=hs[:, C_EG:C_EG + 1]).then_inc(scaled_act, 1)
                if s == S_BACK:
                    act.wait_ge(back_done, h + 1)
                    act.activation(tT[:, 0:4 * P], dn_ps[:, 0:4 * P], ACT.Copy).then_inc(tT_act, 1)
                if s == S_X1:
                    act.wait_ge(x1_done, h + 1)
                    act.activation(xs[:, 0:T, :].rearrange("p t n -> p (t n)"), B[:, 0:T * P], ACT.Copy).then_inc(x1_ready, 1)
                if s in S_Y:
                    n = S_Y.index(s)
                    act.wait_ge(y_done, LEVELS * h + n + 1)
                    act.activation(halves(ysb[:, n, :, :], n, 0), packed(A, 0, n), ACT.Copy).then_inc(y_ready, 1)
                if s == S_U:
                    act.wait_ge(u_done, h + 1)
                    if not first:
                        act.wait_ge(o_done, h)
                    act.activation(u[:, :, :].rearrange("p t n -> p (t n)"), A[:, 0:T * P], ACT.Copy).then_inc(u_ready, 1)
                if s == S_O1:
                    act.wait_ge(o_done, h + 1)
                    if not first:
                        act.wait_ge(o_mean, h)
                    for t in range(T):
                        act.activation(mt[:, 2, t, :], B[:, (1 + t) * P:(2 + t) * P], ACT.Square,
                                       accum_out=so[:, t:t + 1]).then_inc(o_squared, 1)
                if s == S_YT:
                    act.wait_ge(ybT_done, h + 1)
                    act.activation(yb_hi[:, bass.ds(h, 1), :].rearrange("p a n -> p (a n)"), A[:, 0:SEQ],
                                   ACT.Copy).then_inc(yb_hi_ready, 1)

            def mo_step(s, h, first=False):
                if s == M_TURN - 2:
                    if not first:
                        act.wait_ge(pv_done, h)
                        act.wait_ge(mo_z_ready, h)
                    for t in range(T):
                        wait_chunk(act, t, 3 * h + 1, UNITS * h + 2 * UNITS // 3 - 1)
                        act.activation(mo_nat[:, t, :], pj[1][:, t, :], ACT.Copy,
                                       scale=rx[:, 4 + t:5 + t]).then_inc(mo_nat_ready, 1)
                if s == M_TURN:
                    act.wait_ge(mo_turned, h + 1)
                    act.activation(moT[:, :, :].rearrange("p a t -> p (a t)"), C, ACT.Copy).then_inc(moT_ready, 1)
                    if not first:
                        act.wait_ge(ya_ready, T * h)
                    act.activation(mo_z[:, :, :], mo_nat[:, :, 3 * P:4 * P], ACT.Silu).then_inc(mo_z_ready, 1)
                if s == M_QK + 2:
                    act.wait_ge(mx_ready, h + 1)
                    if not first:
                        act.wait_ge(rsum_ready, h)
                    act.activation(prob[:, 0:P], sm[:, 0:P], ACT.Exp, bias=mx[:, 0:1], scale=SCALE,
                                   accum_out=mx[:, 2:3]).then_inc(prob_ready, 1)
                    act.activation(prob[:, P:3 * P], sm[:, P:3 * P], ACT.Exp, bias=mx[:, 1:2], scale=SCALE,
                                   accum_out=mx[:, 3:4]).then_inc(prob_ready, 1)
                if s == M_PT:
                    act.wait_ge(pt_done, h + 1)
                    act.activation(probT[:, :], C[:, 0:3 * P], ACT.Copy).then_inc(pt_ready, 1)
                if s == M_YT:
                    act.wait_ge(yaT_done, h + 1)
                    act.activation(ya_hi[:, bass.ds(h, 1), :].rearrange("p a n -> p (a n)"), C[:, 0:SEQ],
                                   ACT.Copy).then_inc(ya_hi_ready, 1)

            def gates(h, t):
                wait_chunk(act, t, 3 * h + 2, UNITS * h + UNITS - 1)
                act.activation(gate[:, bass.ds(h, 1), t, :].rearrange("p a n -> p (a n)"), pj[0][:, t, :],
                               ACT.Copy, scale=rx[:, 4 + t:5 + t]).then_inc(gate_ready, 1)

            def iteration(h, first):
                for s in range(SLOTS):
                    if first and s == 2 * XU - 6:
                        start_stats()
                    if first and s == 2 * XU - 1:
                        tables()
                    if first and s == 2 * XU:
                        tables_cumulated()
                    if not first:
                        dn_step(s + SLOTS, h - 1)
                    if s == SLOTS - 1:
                        gates(h, 0)
                    dn_step(s, h, first)
                    mo_step(s, h, first)
                    if s == SLOTS - 1:
                        gates(h, 1)
                    n = s // 2 + LEAD
                    if s % 2 == 0 and not (first and n < XU):
                        split(n % RING, h * UNITS + n, (h * (UNITS // RING) + n // RING + 1) * 32)

            iteration(0, True)
            with act.Fori(1, H) as h:
                iteration(h, False)

            def tail_split(n):
                split(n % RING, n, (n // RING + 1) * 32)

            for c in range(NC):
                for j in range(BU):
                    tail_split(FIRST_A + BU * c + j + LEAD)
                    for s in (2 * j, 2 * j + 1):
                        dn_step(2 * BU * c + s + SLOTS, H - 1)
                    n = BU * c + j - 2
                    if 0 <= n < NG:
                        if n == 0:
                            act.wait_ge(gate_ready, T * H)
                        act.activation(gate[:, n, :, :], gate[:, n, :, :], ACT.Sigmoid).then_inc(sig_ready, 1)

            def merged_hi(c):
                ps = [dn_ps, mo_ps][c % 2]
                for half in range(2):
                    act.wait_ge(mT_done, 2 * c + half + 1)
                    act.activation(xt_hi[:, 4 * c + 2 * half:4 * c + 2 * half + 2, :].rearrange("p k t -> p (k t)"),
                                   ps[:, half * CH:(half + 1) * CH], ACT.Copy).then_inc(mT_hi_ready, 1)

            for n in range(NC * BU):
                tail_split(FIRST_B + n + LEAD)
                if n % BU == 1 and n > BU:
                    merged_hi(n // BU - 1)

            def squares(c):
                for t in range(T):
                    act.wait_ge(sum_ready, T * c + t + 1)
                    if T * c + t >= 2:
                        act.wait_ge(f_squared, T * c + t - 1)
                    act.activation(sq[:, t, :], gate[:, c, t, :], ACT.Square,
                                   accum_out=fs[:, t, c:c + 1]).then_inc(f_squared, 1)

            sq = mt[:, 0:4, :, :].rearrange("p (b a) t n -> p b (a t n)", a=2)
            for n in range(NC * OU - LEAD):
                tail_split(FIRST_O + n + LEAD)
                if n == 3:
                    merged_hi(NC - 1)
                if n % OU == 1 and n > OU:
                    squares(n // OU - 1)
            squares(NC - 1)
            act.wait_ge(fr_ready, 1)
            act.wait_ge(f_gained, T * (NC - 1))
            act.activation(gate[:, 0:NC - 1, 0, :], gate[:, 0:NC - 1, 0, :], ACT.Copy,
                           scale=fr[:, 2, 0:1]).then_inc(y_act, 1)

        @block.vector
        def _(dve):
            def split(slot, number, first=False):
                dve.wait_ge(hi_ready, number + 1)
                dve.tensor_tensor(w_lo[:, slot, :], w_raw[:, slot, :], w_hi[:, slot, :].bitcast(F32),
                                  ALU.subtract).then_inc(lo_ready, 1)

            dve.wait_ge(cols_turned, 1)
            dve.tensor_copy(cols[:, 0:96 + KT], E[:, 0:96 + KT]).then_inc(cols_ready, 1)
            dve.wait_ge(cols_ready, 1)
            x_banks = [A, B, C, E]
            for g in range(XU):
                dve.wait_ge(xt_hi_ready, 2 * g + 2)
                for k in (2 * g, 2 * g + 1):
                    src = x_banks[g % 4][:, (k % 2) * SEQ:(k % 2 + 1) * SEQ]
                    dve.scalar_tensor_tensor(out=xt_lo[:, k, :], in0=src, scalar=cols[:, 96 + k:97 + k],
                                             in1=xt_hi[:, k, :].bitcast(F32), op0=ALU.mult,
                                             op1=ALU.subtract).then_inc(xt_lo_ready, 1)
                split(g % RING, g)

            def start_stats():
                dve.wait_ge(const_made, 1)
                taps = cols[:, 0:96].rearrange("p (j a h) -> p h a j", j=4, a=3)
                for a in range(3):
                    dve.tensor_copy(tabs[:, :, C_CONV + 4 * a:C_CONV + 4 * a + 4], taps[:, :, a, :]).then_inc(tabs_ready, 1)
                dve.wait_ge(wba_hi_ready, 1)
                dve.tensor_tensor(wba_lo, wba[:, :], wba_hi.bitcast(F32), ALU.subtract).then_inc(wba_lo_ready, 1)
                dve.tensor_tensor_reduce(gate[:, NC + NC // 2:2 * NC, :, :].rearrange("p c t n -> p (c t n)"),
                                         x_sb[:, 1, :], x_sb[:, 1, :], 1.0, 0.0, ALU.mult,
                                         ALU.add, rx[:, 1:2]).then_inc(x_squared, 1)
                dve.wait_ge(x_squared, 1)
                dve.wait_ge(x_squared_act, 1)
                dve.tensor_scalar(rx[:, 2:4], rx[:, 0:2], 1.0 / D, EPS, ALU.mult, ALU.add).then_inc(rx_mean, 1)

            def tables():
                dve.wait_ge(ba_ready, T)
                dve.wait_ge(small_landed, 48)
                dve.tensor_tensor(sp[:, 0, :, :], ba[:, :, H:2 * H], dtb[:, None, :].to_broadcast([P, T, H]),
                                  ALU.add).then_inc(tab_step, 1)
                dve.wait_ge(tab_step, 1)
                dve.scalar_tensor_tensor(out=sp[:, 1, :, :], in0=sp[:, 0, :, :], scalar=-1.0, in1=sp[:, 0, :, :],
                                         op0=ALU.mult, op1=ALU.min).then_inc(tab_step, 1)
                dve.wait_ge(tab_act, 3)
                dve.scalar_tensor_tensor(out=sp[:, 3, :, :], in0=sp[:, 0, :, :], scalar=0.0, in1=sp[:, 2, :, :],
                                         op0=ALU.max, op1=ALU.add).then_inc(tab_step, 1)
                dve.wait_ge(tab_step, 3)
                dve.scalar_tensor_tensor(out=gl[:, :, :], in0=sp[:, 3, :, :], scalar=-1.0,
                                         in1=alog[:, None, :].to_broadcast([P, T, H]), op0=ALU.mult,
                                         op1=ALU.mult).then_inc(g_ready, 1)

            def tables_cumulated():
                dve.wait_ge(cum_done, 1)
                c0 = C[:, 64:64 + T * H].rearrange("p (t h) -> p t h", t=T)
                dve.tensor_copy(cum[:, 0, :, :], c0).then_inc(cum_ready, 1)
                dve.wait_ge(cum_ready, 1)
                dve.tensor_tensor(cum[:, 1, :, :], C[:, 128:128 + T * H].rearrange("p (t h) -> p t h", t=T),
                                  cum[:, 0, :, :], ALU.subtract).then_inc(cum_ready, 1)
                dve.wait_ge(g_ready, 1)
                dve.tensor_copy(tabs[:, :, C_G:C_G + T].rearrange("p h t -> p t h"), gl[:, :, :]).then_inc(tabs_ready, 1)
                dve.tensor_copy(tabs[:, :, C_CUM:C_CUM + T].rearrange("p h t -> p t h"),
                                cum[:, 0, :, :]).then_inc(tabs_ready, 1)
                dve.wait_ge(tab_act, 4)
                dve.wait_ge(beta_ready, 1)
                dve.tensor_copy(tabs[:, :, C_EG], sp[:, 0, 1, :]).then_inc(tabs_ready, 1)
                dve.tensor_copy(tabs[:, :, C_DL], sp[:, 1, 0, :]).then_inc(tabs_ready, 1)
                dve.tensor_tensor(tabs[:, :, C_BEG], sp[:, 0, 1, :], tabs[:, :, C_BETA + 1], ALU.mult).then_inc(tabs_ready, 1)

            def dn_step(s, h, first=False):
                if s in (S_TURN, S_DEC):
                    if s == S_TURN:
                        dve.wait_ge(dn_turned, h + 1)
                        dve.wait_ge(taps_ready, h + 1)
                        if not first:
                            dve.wait_ge(convs_ready, h)
                    for back in ((0, 1) if s == S_TURN else (2, 3)):
                        if back == 2:
                            dve.wait_ge(dec_done, h + 1)
                            if not first:
                                dve.wait_ge(decay_ready, h)
                            for t in range(T):
                                dve.tensor_scalar(dsub[:, t, :], E[:, t * P:(t + 1) * P], hs[:, C_CUM + t:C_CUM + t + 1],
                                                  0.0, ALU.subtract, ALU.min).then_inc(dsub_ready, 1)
                        for p in range(3):
                            tap = hs[:, C_CONV + 4 * p + 3 - back:C_CONV + 4 * p + 4 - back]
                            u_ = dn_ps[:, p * SEQ:(p + 1) * SEQ]
                            if back == 0:
                                dve.tensor_scalar(conv[:, p, :], u_, tap, None, ALU.mult).then_inc(conv_step, 1)
                            else:
                                dve.wait_ge(conv_step, 12 * h + 3 * (back - 1) + p + 1)
                                dve.scalar_tensor_tensor(out=conv[:, p, back:SEQ], in0=u_[:, 0:SEQ - back], scalar=tap,
                                                         in1=conv[:, p, back:SEQ], op0=ALU.mult,
                                                         op1=ALU.add).then_inc(conv_step, 1)
                if s == S_NAT:
                    dve.wait_ge(norm_squared, 2 * T * (h + 1))
                    if not first:
                        dve.wait_ge(norm_ready, h)
                    dve.tensor_scalar(rn[:, 0, :], ss[:, :], EPS, None, ALU.add).then_inc(norm_eps, 1)
                    r = rn[:, 1, :]
                    dve.wait_ge(norm_ready, h + 1)
                    ps = dn_ps[:, 0:6 * P].rearrange("p (a t n) -> p a t n", a=3, t=T)
                    if not first:
                        dve.wait_ge(back_done, h)
                        dve.wait_ge(scaled_pool, 2 * h)
                        dve.wait_ge(u_done, h)
                    dve.tensor_tensor(tin[:, :, 0, :], ps[:, 1], r[:, 2:4, None].to_broadcast([P, T, P]),
                                      ALU.mult).then_inc(scaled_dve, 1)
                    dve.scalar_tensor_tensor(out=tin[:, :, 2, :], in0=ps[:, 0], scalar=SCALE,
                                             in1=r[:, 0:2, None].to_broadcast([P, T, P]), op0=ALU.mult,
                                             op1=ALU.mult).then_inc(scaled_dve, 1)
                    dve.tensor_tensor(vb[:, :, :], ps[:, 2], hs[:, C_BETA:C_BETA + 2, None].to_broadcast([P, T, P]),
                                      ALU.mult).then_inc(scaled_dve, 1)
                if s == S_BACK:
                    dve.wait_ge(back_done, h + 1)
                    if not first:
                        dve.wait_ge(o_done, h)
                    dve.tensor_copy(tT[:, 4 * P:7 * P], dn_ps[:, 4 * P:7 * P]).then_inc(tT_dve, 1)
                    dve.wait_ge(dexp_ready, h + 1)
                    dve.tensor_tensor(decay[:, :, :], dsub[:, :, :], causal[:, None, :].to_broadcast([P, T, P]),
                                      ALU.mult).then_inc(decay_ready, 1)
                if s == S_KK:
                    dve.wait_ge(kk_done, h + 1)
                    dve.wait_ge(decay_ready, h + 1)
                    if not first:
                        dve.wait_ge(mt_ready, LEVELS * h)
                        dve.wait_ge(u_done, h)
                    ps = A.rearrange("p (t a n) -> p t a n", t=T, a=2)
                    dve.tensor_tensor(lt[:, :, :], ps[:, :, 0, :], decay[:, :, :], ALU.mult).then_inc(lt_ready, 1)
                    dve.wait_ge(lt_ready, h + 1)
                    dve.tensor_tensor(u[:, :, :], lt[:, :, :], neg1[:, None, :].to_broadcast([P, T, P]),
                                      ALU.mult).then_inc(x1_step, 1)
                    dve.wait_ge(x1_step, 2 * h + 1)
                    dve.tensor_tensor(xs[:, T:2 * T, :], u[:, :, :], ident[:, None, :].to_broadcast([P, T, P]),
                                      ALU.add).then_inc(x1_step, 1)
                    dve.tensor_tensor(intra[:, :, :], ps[:, :, 1, :], decay[:, :, :], ALU.mult).then_inc(intra_ready, 1)
                if s in S_XY:
                    n = S_XY.index(s)
                    dve.wait_ge(xy_done, LEVELS * h + n + 1)
                    if n < LEVELS - 1:
                        x = halves(xs[:, 0:T, :], n, 0)
                        dve.tensor_tensor(x, x, packed(B, 0, n), ALU.subtract).then_inc(xs_ready, 1)
                    xT = halves(xs[:, T:2 * T, :], n, 1)
                    dve.tensor_tensor(xT, xT, packed(B, 1, n), ALU.subtract).then_inc(xsT_ready, 1)
                if s == S_U:
                    dve.wait_ge(u_done, h + 1)
                    dve.tensor_copy(wT[:, :], B[:, 3 * P:4 * P]).then_inc(wT_ready, 1)
                if s == S_S1:
                    dve.wait_ge(s1_done, h + 1)
                    dve.tensor_copy(s1[:, :], B[:, 0:P]).then_inc(s1_ready, 1)
                if s == S_WS:
                    dve.wait_ge(ws_done, h + 1)
                    dve.tensor_tensor(vnew[:, :], u[:, 1, :], A[:, 3 * P:4 * P], ALU.subtract).then_inc(vnew_ready, 1)
                if s == S_O1 + 1:
                    dve.wait_ge(o_squared, T * (h + 1))
                    if not first:
                        dve.wait_ge(ro_ready, h)
                    dve.tensor_scalar(ro[:, 0, :], so[:, :], 1.0 / P, EPS, ALU.mult, ALU.add).then_inc(o_mean, 1)
                    dve.wait_ge(dn_zg_ready, h + 1)
                    dve.wait_ge(ro_ready, h + 1)
                    r = ro[:, 1, :]
                    for t in range(T):
                        dve.scalar_tensor_tensor(out=yb[:, t, :], in0=B[:, (1 + t) * P:(2 + t) * P], scalar=r[:, t:t + 1],
                                                 in1=dn_z[:, t, :], op0=ALU.mult, op1=ALU.mult).then_inc(yb_ready, 1)
                if s == S_YT:
                    dve.wait_ge(yb_hi_ready, h + 1)
                    hd = bass.ds(h, 1)
                    dve.tensor_tensor(yb_lo[:, hd, :], A[:, 0:SEQ].rearrange("p (a n) -> p a n", a=1),
                                      yb_hi[:, hd, :].bitcast(F32), ALU.subtract).then_inc(yb_lo_ready, 1)

            def mo_step(s, h, first=False):
                if s == M_QK:
                    dve.wait_ge(qk_done, h + 1)
                    dve.wait_ge(hs_ready, h + 1)
                    if not first:
                        dve.wait_ge(prob_ready, T * h)
                    dve.scalar_tensor_tensor(out=sm[:, :], in0=far[:, :], scalar=hs[:, C_SLOPE:C_SLOPE + 1],
                                             in1=E[:, 0:3 * P], op0=ALU.mult, op1=ALU.add).then_inc(sm_ready, 1)
                    dve.wait_ge(sm_ready, h + 1)
                    dve.tensor_reduce(mx[:, 4:5], sm[:, 0:P], AX_X, ALU.max).then_inc(max_step, 1)
                    dve.tensor_reduce(mx[:, 5:6], sm[:, P:3 * P], AX_X, ALU.max).then_inc(max_step, 1)
                    dve.wait_ge(max_step, 2 * h + 2)
                    dve.tensor_scalar(mx[:, 0:2], mx[:, 4:6], -SCALE, None, ALU.mult).then_inc(mx_ready, 1)
                if s == M_QK + 3:
                    dve.wait_ge(prob_ready, T * h + T)
                    dve.reciprocal(mx[:, 6:8], mx[:, 2:4]).then_inc(rsum_ready, 1)
                if s == M_PV:
                    dve.wait_ge(pv_done, h + 1)
                    dve.wait_ge(rsum_ready, h + 1)
                    dve.wait_ge(mo_z_ready, h + 1)
                    if not first:
                        dve.wait_ge(yaT_done, h)
                    for t in range(T):
                        dve.scalar_tensor_tensor(out=ya[:, t, :], in0=E[:, t * P:(t + 1) * P], scalar=mx[:, 6 + t:7 + t],
                                                 in1=mo_z[:, t, :], op0=ALU.mult, op1=ALU.mult).then_inc(ya_ready, 1)
                if s == M_YT:
                    dve.wait_ge(ya_hi_ready, h + 1)
                    hd = bass.ds(h, 1)
                    dve.tensor_tensor(ya_lo[:, hd, :], C[:, 0:SEQ].rearrange("p (a n) -> p a n", a=1),
                                      ya_hi[:, hd, :].bitcast(F32), ALU.subtract).then_inc(ya_lo_ready, 1)

            def iteration(h, first):
                for s in range(SLOTS):
                    if first and s == 2 * XU - 6:
                        start_stats()
                    if first and s == 2 * XU - 1:
                        tables()
                    if first and s == 2 * XU:
                        tables_cumulated()
                    if not first:
                        dn_step(s + SLOTS, h - 1)
                    dn_step(s, h, first)
                    mo_step(s, h, first)
                    n = s // 2 + LEAD
                    if s % 2 == 0 and not (first and n < XU):
                        split(n % RING, h * UNITS + n)

            iteration(0, True)
            with dve.Fori(1, H) as h:
                iteration(h, False)

            def tail_split(n):
                split(n % RING, n)

            def gate_a(c):
                for t in range(T):
                    wait_chunk(dve, t, 3 * H + c, FIRST_A + BU * c + BU - 1)
                    dve.wait_ge(sig_ready, c + 1)
                    dve.tensor_tensor(gate[:, c, t, :], gate[:, c, t, :], pj[c % 2][:, t, :], ALU.mult).then_inc(a_gated, 1)

            def gate_b(c):
                for t in range(T):
                    wait_chunk(dve, t, 3 * H + NC + c, FIRST_B + BU * c + BU - 1)
                    g = gate[:, NC + c, t, :]
                    dve.tensor_tensor(g, g, pj[c % 2][:, t, :], ALU.mult).then_inc(b_gated, 1)
                    dve.wait_ge(b_gated, T * c + t + 1)
                    dve.tensor_tensor(g, g, gate[:, c, t, :], ALU.add).then_inc(merged, 1)

            for c in range(NC):
                for j in range(BU):
                    tail_split(FIRST_A + BU * c + j + LEAD)
                    for s in (2 * j, 2 * j + 1):
                        dn_step(2 * BU * c + s + SLOTS, H - 1)
                    if j == 0 and c > 0:
                        gate_a(c - 1)

            def merged_lo(c):
                ps = [dn_ps, mo_ps][c % 2]
                for half in range(2):
                    dve.wait_ge(mT_hi_ready, 2 * c + half + 1)
                    ks = slice(4 * c + 2 * half, 4 * c + 2 * half + 2)
                    dve.tensor_tensor(xt_lo[:, ks, :].rearrange("p k t -> p (k t)"), ps[:, half * CH:(half + 1) * CH],
                                      xt_hi[:, ks, :].rearrange("p k t -> p (k t)").bitcast(F32),
                                      ALU.subtract).then_inc(mT_lo_ready, 1)

            for n in range(NC * BU):
                tail_split(FIRST_B + n + LEAD)
                if n == 0:
                    gate_a(NC - 1)
                if n % BU == 0 and n > 0:
                    gate_b(n // BU - 1)
                if n % BU == 1 and n > BU:
                    merged_lo(n // BU - 1)

            def residual(c):
                dve.wait_ge(x_again[c], 16)
                for t in range(T):
                    wait_chunk(dve, t, 3 * H + 2 * NC + c, FIRST_O + OU * c + OU - 1)
                    g = gate[:, c, t, :]
                    dve.tensor_tensor(g, g, pj[c % 2][:, t, :], ALU.add).then_inc(sum_ready, 1)
                    if c == NC - 1:
                        dve.wait_ge(gain_landed, 16)
                        dve.wait_ge(sum_ready, T * c + t + 1)
                        dve.tensor_tensor(last[:, t, :], g, fg[:, c * CH:D], ALU.mult).then_inc(last_gained, 1)

            fg = gate[:, NC:NC + NC // 2, :, :].rearrange("p c t n -> p (c t n)")
            last = gate[:, NC + NC // 2, :, :]
            for n in range(NC * OU - LEAD):
                tail_split(FIRST_O + n + LEAD)
                if n == 0:
                    gate_b(NC - 1)
                if n == 3:
                    merged_lo(NC - 1)
                if n % OU == 0 and n > 0:
                    residual(n // OU - 1)
            residual(NC - 1)
            dve.wait_ge(f_squared, T * NC)
            dve.tensor_reduce(fr[:, 0, :], fs[:, :, :], AX_X, ALU.add).then_inc(f_total, 1)
            dve.wait_ge(f_total, 1)
            dve.tensor_scalar(fr[:, 1, :], fr[:, 0, :], 1.0 / D, EPS, ALU.mult, ALU.add).then_inc(f_mean, 1)
            dve.wait_ge(fr_ready, 1)
            dve.wait_ge(f_gained, T * (NC - 1))
            dve.tensor_scalar(gate[:, 0:NC - 1, 1, :], gate[:, 0:NC - 1, 1, :], fr[:, 2, 1:2], None,
                              ALU.mult).then_inc(y_dve, 1)
            dve.wait_ge(last_gained, T)
            for t in range(T):
                dve.tensor_scalar(last[:, t, :], last[:, t, :], fr[:, 2, t:t + 1], None, ALU.mult).then_inc(y_dve, 1)


_INS = ['x', 'norm_gain', 'w_in', 'conv_w', 'a_log', 'dt_bias', 'dn_norm_gain', 'w_branch_a', 'w_branch_b',
        'w_out', 'final_norm_gain']


def kernel(**inputs):
    import numpy as _np
    import concourse.bacc as _bacc
    from concourse import mybir as _mybir
    from concourse.bass_utils import run_bass_kernel_spmd as _run

    nc = _bacc.Bacc("TRN2", target_bir_lowering=False, num_devices=1)
    arrays, args = {}, []
    for name in _INS:
        a = _np.ascontiguousarray(inputs[name])
        if name != 'final_norm_gain':
            a = a[0]
        arrays[f"in_{name}_dram"] = a
        args.append(nc.dram_tensor(f"in_{name}_dram", a.shape, _mybir.dt.from_np(a.dtype), kind="ExternalInput").ap())
    o = nc.dram_tensor("out_dram", (SEQ, D), F32, kind="ExternalOutput").ap()
    build(nc, *args, o)
    r = _run(nc, [arrays], core_ids=[0])
    return r.results[0]["out_dram"].reshape(1, SEQ, D)
```

```python
from contextlib import ExitStack

import concourse.bass as bass
from concourse import mybir

ALU = mybir.AluOpType
ACT = mybir.ActivationFunctionType
AX_X = mybir.AxisListType.X
F32 = mybir.dt.float32
F32R = mybir.dt.float32r

P = 128
SEQ, D = 256, 2048
T = SEQ // P
KT = D // P
H = 8
W = H * P
CH = 512
OFF_A = 0
OFF_B = 4 * W
OFF_BETA = 8 * W
OFF_GATE = OFF_BETA + 2 * H
NG = 2 * D // CH
NC = D // CH
RING = 4
UK = 2
UNITS = 3 * KT // UK
SLOTS = 3 * KT
LEAD = 3
BU = H // UK
OU = KT // UK
FIRST_A = H * UNITS
FIRST_B = FIRST_A + NC * BU
FIRST_O = FIRST_B + NC * BU
LEVELS = 6
EPS = 1e-6
SCALE = float(P) ** -0.5
FAR = -1e30

C_CONV, C_G, C_CUM, C_BETA, C_BEG, C_EG, C_DL, C_SLOPE, C_ALL = 0, 12, 14, 16, 18, 19, 20, 21, 22
XU = KT // UK

S_TURN, S_DEC, S_NAT, S_BACK, S_KK = 18, 20, 24, 29, 31
S_Y = [35, 39, 43, 47, 51, 54]
S_XY = [y + 1 for y in S_Y]
S_XT = [y - 1 for y in S_Y]
S_U, S_S1, S_WS, S_O1, S_YT = 56, 58, 59, 60, 64
M_TURN, M_QK, M_EXP, M_PT, M_PV, M_YT = 34, 37, 40, 42, 44, 47


def build(nc, x, norm_gain, w_in, conv_w, a_log, dt_bias, dn_norm_gain, w_a, w_b, w_out,
          final_gain, out):
    ctx = ExitStack()
    with ctx:
        def sb(name, shape, dt=F32):
            return ctx.enter_context(nc.sbuf_tensor(name, shape, dt))

        def sem(name):
            return ctx.enter_context(nc.semaphore(name))

        w_raw = sb("w_raw", [P, RING, UK * CH])
        w_hi = sb("w_hi", [P, RING, UK * CH], F32R)
        w_lo = sb("w_lo", [P, RING, UK * CH], F32R)
        xt_hi = sb("xt_hi", [P, KT, SEQ], F32R)
        xt_lo = sb("xt_lo", [P, KT, SEQ], F32R)
        ya_hi = sb("ya_hi", [P, H, SEQ], F32R)
        ya_lo = sb("ya_lo", [P, H, SEQ], F32R)
        yb_hi = sb("yb_hi", [P, H, SEQ], F32R)
        yb_lo = sb("yb_lo", [P, H, SEQ], F32R)
        wba_parts = yb_hi[:, 0:2, :].rearrange("p a n -> p (a n)").rearrange("p (k e n) -> p k e n", k=KT, e=2)
        gate = sb("gate", [P, NG, T, CH])
        x_sb = gate[:, 0:NC, :, :].rearrange("p c t n -> p (c t n)").rearrange("p (t d) -> p t d", t=T)
        last = gate[:, NC + NC // 2, :, :]
        cols = sb("cols", [P, P])
        dn_gain = sb("dn_gain", [P, P])
        alog = sb("alog", [P, H])
        dtb = sb("dtb", [P, H])
        ident = sb("ident", [P, P])
        ones = sb("ones", [P, P])
        causal = sb("causal", [P, P])
        neg1 = sb("neg1", [P, P])
        levels = sb("levels", [P, LEVELS, P])
        far = sb("far", [P, 3 * P])
        rx = sb("rx", [P, 6])
        fold = sb("fold", [4 * H, 2 * H])
        half = sb("half", [P, 4])
        tabs = sb("tabs", [P, H, C_ALL])
        hs = sb("hs", [P, C_ALL])
        ba = sb("ba", [P, T, 2 * H])
        sp = sb("sp", [P, 4, T, H])
        gl = sb("gl", [P, T, H])
        cum = sb("cum", [P, 2, T, H])
        dn_nat = sb("dn_nat", [P, T, CH])
        dn_z = sb("dn_z", [P, T, P])
        conv = sb("conv", [P, 3, SEQ])
        convs = sb("convs", [P, 3 * SEQ])
        baT = convs[0:4 * H, 2 * SEQ:3 * SEQ]
        rows = convs[:, 0:P]
        wba = conv[:, 0, :]
        ss = sb("ss", [P, 4])
        rn = sb("rn", [P, 2, 4])
        dsub = sb("dsub", [P, T, P])
        decay = sb("decay", [P, T, P])
        tin = sb("tin", [P, T, 3, P])
        qg1 = sb("qg1", [P, P])
        kbg1 = sb("kbg1", [P, P])
        kd0 = sb("kd0", [P, P])
        vb = sb("vb", [P, T, P])
        tT = sb("tT", [P, 7 * P])
        lt = sb("lt", [P, T, P])
        intra = sb("intra", [P, T, P])
        mt = sb("mt", [P, LEVELS, T, P])
        xs = sb("xs", [P, 2 * T, P])
        ysb = sb("ysb", [P, LEVELS, T, P])
        u = sb("u", [P, T, P])
        wT = sb("wT", [P, P])
        s1 = sb("s1", [P, P])
        vnew = sb("vnew", [P, P])
        so = sb("so", [P, 2])
        ro = sb("ro", [P, 2, 2])
        yb = sb("yb", [P, T, P])
        mo_nat = sb("mo_nat", [P, T, CH])
        mo_z = sb("mo_z", [P, T, P])
        moT = sb("moT", [P, 2, SEQ])
        sm = sb("sm", [P, 3 * P])
        prob = sb("prob", [P, 3 * P])
        probT = sb("probT", [P, 3 * P])
        mx = sb("mx", [P, 8])
        ya = sb("ya", [P, T, P])
        fs = sb("fs", [P, T, NC])
        fr = sb("fr", [P, 3, T])

        pj = [ctx.enter_context(nc.psum_tensor(f"pj{i}", [P, T, CH], F32)) for i in range(2)]
        dn_ps = ctx.enter_context(nc.psum_tensor("dn_ps", [P, 2 * CH], F32))
        mo_ps = ctx.enter_context(nc.psum_tensor("mo_ps", [P, 2 * CH], F32))
        A, B = dn_ps[:, 0:CH], dn_ps[:, CH:2 * CH]
        C, E = mo_ps[:, 0:CH], mo_ps[:, CH:2 * CH]

        w_landed = [sem(f"w_landed{i}") for i in range(RING)]
        hi_ready, lo_ready = sem("hi_ready"), sem("lo_ready")
        unit_used = sem("unit_used")
        x_landed = [sem(f"x_landed{i}") for i in range(XU)]
        first_landed, first_hi, first_lo = sem("first_landed"), sem("first_hi"), sem("first_lo")
        rows_landed, small_landed, wba_landed = sem("rows_landed"), sem("small_landed"), sem("wba_landed")
        const_made, ident_made, const_step = sem("const_made"), sem("ident_made"), sem("const_step")
        cols_turned, cols_ready = sem("cols_turned"), sem("cols_ready")
        x_turned, xt_hi_ready, xt_lo_ready = sem("x_turned"), sem("xt_hi_ready"), sem("xt_lo_ready")
        x_squared, x_squared_act, rx_mean, rx_ready = (sem(n) for n in (
            "x_squared", "x_squared_act", "rx_mean", "rx_ready"))
        wba_hi_ready, wba_lo_ready = sem("wba_hi_ready"), sem("wba_lo_ready")
        ba_done, ba_ready, beta_ready, tab_step, tab_act, g_ready = (sem(n) for n in (
            "ba_done", "ba_ready", "beta_ready", "tab_step", "tab_act", "g_ready"))
        cum_done, cum_ready, tabs_ready, tabs_pool = (sem(n) for n in (
            "cum_done", "cum_ready", "tabs_ready", "tabs_pool"))
        baT_ready, ba_turned, beta_exp, table_loaded = (sem(n) for n in (
            "baT_ready", "ba_turned", "beta_exp", "table_loaded"))
        tile0_done = sem("tile0_done")
        dn_nat_ready, mo_nat_ready, gate_ready = sem("dn_nat_ready"), sem("mo_nat_ready"), sem("gate_ready")
        taps_ready, hs_ready, dec_done = sem("taps_ready"), sem("hs_ready"), sem("dec_done")
        dn_turned, conv_step, convs_ready, nat_done = (sem(n) for n in (
            "dn_turned", "conv_step", "convs_ready", "nat_done"))
        dn_z_ready, dn_zg_ready = sem("dn_z_ready"), sem("dn_zg_ready")
        dsub_ready, dexp_ready, decay_ready = sem("dsub_ready"), sem("dexp_ready"), sem("decay_ready")
        norm_squared, norm_eps, norm_ready = (sem(n) for n in (
            "norm_squared", "norm_eps", "norm_ready"))
        scaled_dve, scaled_act, scaled_pool = sem("scaled_dve"), sem("scaled_act"), sem("scaled_pool")
        back_done, tT_act, tT_dve, kk_done = sem("back_done"), sem("tT_act"), sem("tT_dve"), sem("kk_done")
        lt_ready, intra_ready, mt_ready = sem("lt_ready"), sem("intra_ready"), sem("mt_ready")
        x1_step, xT_turned = sem("x1_step"), sem("xT_turned")
        y_done, y_ready, xy_done, xs_ready, xsT_ready = (sem(n) for n in (
            "y_done", "y_ready", "xy_done", "xs_ready", "xsT_ready"))
        u_done, u_ready, wT_ready, s1_done, s1_ready = (sem(n) for n in (
            "u_done", "u_ready", "wT_ready", "s1_done", "s1_ready"))
        ws_done, vnew_ready, o_done = sem("ws_done"), sem("vnew_ready"), sem("o_done")
        o_squared, o_mean, ro_ready, yb_ready = (sem(n) for n in (
            "o_squared", "o_mean", "ro_ready", "yb_ready"))
        ybT_done, yb_hi_ready, yb_lo_ready = sem("ybT_done"), sem("yb_hi_ready"), sem("yb_lo_ready")
        mo_z_ready, mo_turned, moT_ready, qk_done = (sem(n) for n in (
            "mo_z_ready", "mo_turned", "moT_ready", "qk_done"))
        sm_ready, mx_ready, prob_ready, rsum_ready = (sem(n) for n in (
            "sm_ready", "mx_ready", "prob_ready", "rsum_ready"))
        max_step = sem("max_step")
        pt_done, pt_ready, pv_done, ya_ready = sem("pt_done"), sem("pt_ready"), sem("pv_done"), sem("ya_ready")
        yaT_done, ya_hi_ready, ya_lo_ready = sem("yaT_done"), sem("ya_hi_ready"), sem("ya_lo_ready")
        sig_ready, a_gated, b_gated, merged = sem("sig_ready"), sem("a_gated"), sem("b_gated"), sem("merged")
        mT_done, mT_hi_ready, mT_lo_ready = sem("mT_done"), sem("mT_hi_ready"), sem("mT_lo_ready")
        x_again = [sem(f"x_again{i}") for i in range(NC)]
        gain_landed, sum_ready, f_squared = sem("gain_landed"), sem("sum_ready"), sem("f_squared")
        f_total, f_mean, fr_ready, f_gained = (sem(n) for n in (
            "f_total", "f_mean", "fr_ready", "f_gained"))
        last_gained, y_act, y_dve, stored = (sem(n) for n in ("last_gained", "y_act", "y_dve", "stored"))

        block = ctx.enter_context(nc.Block())

        def halves(m, n, e):
            return m.rearrange("p t (b e c) -> p t b e c", e=2, c=2 << n)[:, :, :, e, :]

        def packed(bank, i, n):
            return bank[:, i * P:(i + 1) * P].rearrange("p (t b c) -> p t b c", t=T, c=2 << n)

        def wait_chunk(eng, t, chunk, last_unit):
            if t == 0:
                eng.wait_ge(tile0_done, chunk + 1)
            else:
                eng.wait_ge(unit_used, last_unit + 1)

        def parts(number):
            spare = number - (FIRST_O + NC * OU - RING)
            if spare < 0:
                return w_hi[:, number % RING, :], w_lo[:, number % RING, :]
            cs = slice(spare % 2 * UK * CH, (spare % 2 + 1) * UK * CH)
            return tuple(m[:, :, :].rearrange("p h t -> p (h t)")[:, cs]
                         for m in ((ya_hi, ya_lo), (yb_hi, yb_lo))[spare // 2])

        @block.sync
        def _(sp):
            sp.dma_start(rows[0:96, :], conv_w.rearrange("j (b c) -> (j b) c", c=P)).then_inc(rows_landed, 16)
            sp.dma_start(rows[96:96 + KT, :], norm_gain.rearrange("(k c) -> k c", c=P)).then_inc(rows_landed, 16)

            def iteration(h, first):
                head_col = h * P if first else sp.snap(h * P)
                gate_col = OFF_GATE if first else sp.snap(h * CH + OFF_GATE)
                for j in range(UNITS):
                    slot = j % RING
                    if first:
                        for g in range(max(2 * j - 1, 0), min(2 * j + 1, XU)):
                            cs = slice(g * UK * P, (g + 1) * UK * P)
                            sp.dma_start(x_sb[:, :, cs], x[:, cs].rearrange("(t p) n -> p t n", p=P)
                                         ).then_inc(x_landed[g], 16)
                    used = None if first and j < RING else h * UNITS + j - RING + 1
                    k = (j % (KT // UK)) * UK
                    if used is not None:
                        sp.wait_ge(lo_ready, used)
                    for i in range(UK) if first and j == 0 else reversed(range(UK)):
                        r = slice((k + i) * P, (k + i + 1) * P)
                        dst = w_raw[:, slot, i * CH:(i + 1) * CH]
                        if j < UNITS // 3 * 2:
                            branch = 1 if j < UNITS // 3 else 0
                            dst = dst.rearrange("p (a n) -> p a n", a=4)
                            src = w_in[r, branch * 4 * W:(branch + 1) * 4 * W].rearrange(
                                "p (a w) -> p a w", a=4)[:, :, bass.ds(head_col, P)]
                        else:
                            src = w_in[r, bass.ds(gate_col, CH)]
                        landed = first_landed if first and j == 0 and i == 0 else w_landed[slot]
                        sp.dma_start(dst, src).then_inc(landed, 16)
                    if first and j == RING - 1:
                        sp.dma_start(wba[:, :].rearrange("p (k n) -> p k n", k=KT),
                                     w_in[:, OFF_BETA:OFF_GATE].rearrange("(k p) n -> p k n", p=P)
                                     ).then_inc(wba_landed, 16)
                        sp.dma_start(dn_gain[:, :], dn_norm_gain.rearrange("(a n) -> a n", a=1).to_broadcast([P, P])
                                     ).then_inc(small_landed, 16)
                        sp.dma_start(alog[:, :], a_log.rearrange("(a n) -> a n", a=1).to_broadcast([P, H])
                                     ).then_inc(small_landed, 16)
                        sp.dma_start(dtb[:, :], dt_bias.rearrange("(a n) -> a n", a=1).to_broadcast([P, H])
                                     ).then_inc(small_landed, 16)

            iteration(0, True)
            with sp.Fori(1, H) as h:
                iteration(h, False)

            def chunk(wmat, c, units, first_unit):
                col = c * CH if isinstance(c, int) else sp.snap(c * CH)
                for j in range(units):
                    slot = j % RING
                    sp.wait_ge(lo_ready, c * units + (first_unit + j - RING + 1))
                    for i in reversed(range(UK)):
                        k = UK * j + i
                        sp.dma_start(w_raw[:, slot, i * CH:(i + 1) * CH],
                                     wmat[k * P:(k + 1) * P, bass.ds(col, CH)]).then_inc(w_landed[slot], 16)

            with sp.Fori(0, NC) as c:
                chunk(w_a, c, BU, FIRST_A)
            with sp.Fori(0, NC) as c:
                chunk(w_b, c, BU, FIRST_B)
            for c in range(NC):
                chunk(w_out, c, OU, FIRST_O)
                if c == 0:
                    sp.wait_ge(merged, T * NC)
                    for j in range(NC):
                        sp.dma_start(gate[:, j, :, :], x[:, j * CH:(j + 1) * CH].rearrange("(t p) n -> p t n", p=P)
                                     ).then_inc(x_again[j], 16)
                    sp.wait_ge(mT_done, 2 * NC)
                    sp.dma_start(gate[:, NC:NC + NC // 2, :, :].rearrange("p c t n -> p (c t n)"),
                                 final_gain.rearrange("(a n) -> a n", a=1).to_broadcast([P, D])
                                 ).then_inc(gain_landed, 16)
            n = (NC - 1) * CH
            for t, ready, count, cs in ((0, y_dve, 1, (0, n)), (0, y_dve, 2, (n, D)), (1, y_act, 1, (0, CH)),
                                        (1, y_dve, 3, (CH, n)), (1, y_dve, 4, (n, D))):
                sp.wait_ge(ready, count)
                src = last[:, t:t + 1, :] if cs[0] == n else gate[:, cs[0] // CH:cs[1] // CH, t, :]
                sp.dma_start(out[t * P:(t + 1) * P, cs[0]:cs[1]].rearrange("p (c n) -> p c n", n=CH),
                             src).then_inc(stored, 16)
            sp.wait_ge(stored, 16 * 5)

        @block.gpsimd
        def _(pool):
            pool.memset(ident[:, :], 0.0).then_inc(const_step, 1)
            pool.wait_ge(const_step, 1)
            pool.affine_select(out=ident[:, :], in_=ident[:, :], compare_op=ALU.not_equal, fill=1.0, base=0,
                               pattern=[[-1, P]], channel_multiplier=1).then_inc(ident_made, 1)
            pool.memset(ones[:, :], 1.0).then_inc(const_step, 1)
            pool.memset(half[:, :], -0.5).then_inc(const_step, 1)
            pool.wait_ge(const_step, 3)
            pool.affine_select(out=causal[:, :], in_=ones[:, :], compare_op=ALU.is_ge, fill=0.0, base=0,
                               pattern=[[1, P]], channel_multiplier=-1).then_inc(const_step, 1)
            pool.iota(sm[:, 0:P], pattern=[[1, P]], base=0, channel_multiplier=-1,
                      allow_small_or_imprecise_dtypes=True).then_inc(const_step, 1)
            pool.iota(sm[:, P:3 * P], pattern=[[1, 2 * P]], base=-P, channel_multiplier=-1,
                      allow_small_or_imprecise_dtypes=True).then_inc(const_step, 1)
            pool.wait_ge(const_step, 6)
            pool.affine_select(out=far[:, 0:P], in_=sm[:, 0:P], compare_op=ALU.is_ge, fill=FAR, base=0,
                               pattern=[[-1, P]], channel_multiplier=1).then_inc(const_step, 1)
            pool.affine_select(out=far[:, P:3 * P], in_=sm[:, P:3 * P], compare_op=ALU.is_ge, fill=FAR, base=P,
                               pattern=[[-1, 2 * P]], channel_multiplier=1).then_inc(const_step, 1)
            done = 8
            for n in range(LEVELS + 1):
                s = 1 << n
                m = neg1[:, :] if n == 0 else levels[:, n - 1, :]
                blocks = m.rearrange("p (b e c) -> p b e c", e=2, c=s)
                pool.memset(m, -1.0 if n == 0 else 1.0).then_inc(const_step, 1)
                done += 1
                pool.wait_ge(const_step, done)
                pool.affine_select(out=blocks, in_=blocks, compare_op=ALU.is_ge, fill=0.0, base=-1,
                                   pattern=[[0, P // (2 * s)], [1, 2], [0, s]], channel_multiplier=0).then_inc(const_step, 1)
                pool.wait_ge(const_step, done + 1)
                pool.affine_select(out=blocks, in_=blocks, compare_op=ALU.is_ge, fill=0.0, base=0,
                                   pattern=[[-2 * s, P // (2 * s)], [0, 2], [0, s]], channel_multiplier=1).then_inc(const_step, 1)
                pool.wait_ge(const_step, done + 2)
                pool.affine_select(out=blocks, in_=blocks, compare_op=ALU.is_ge, fill=0.0, base=s - 1,
                                   pattern=[[2 * s, P // (2 * s)], [0, 2], [0, s]], channel_multiplier=-1).then_inc(const_step, 1)
                done += 3
            for h in range(H):
                pool.memset(tabs[:, h, C_SLOPE:C_SLOPE + 1], 2.0 ** (-8.0 * (h + 1) / H) / SCALE).then_inc(tabs_pool, 1)
            pool.wait_ge(const_step, done)
            pool.memset(ysb[:, :, :, :], 0.0).then_inc(const_made, 1)

            def inv_sqrt(dst, src, n):
                return pool.tensor_tensor(dst, src, half[:, 0:n], ALU.pow)

            def output_norm(h):
                pool.wait_ge(o_mean, h + 1)
                inv_sqrt(ro[:, 1, :], ro[:, 0, :], T).then_inc(ro_ready, 1)

            def head(h, first):
                if not first:
                    output_norm(h - 1)
                if not first:
                    pool.wait_ge(conv_step, 12 * h)
                    pool.wait_ge(sm_ready, h)
                    pool.wait_ge(scaled_act, 3 * h)
                    pool.wait_ge(scaled_dve, 3 * h)
                row = tabs[:, bass.ds(h, 1), :]
                pool.tensor_copy(hs[:, 0:C_G], row[:, :, 0:C_G].rearrange("p a c -> p (a c)")).then_inc(taps_ready, 1)
                if first:
                    pool.wait_ge(tabs_ready, 8)
                pool.tensor_copy(hs[:, C_G:C_ALL], row[:, :, C_G:C_ALL].rearrange("p a c -> p (a c)")).then_inc(hs_ready, 1)
                pool.wait_ge(dn_z_ready, h + 1)
                pool.tensor_tensor(dn_z[:, :, :], dn_z[:, :, :],
                                   dn_gain[:, None, :].to_broadcast([P, T, P]), ALU.mult).then_inc(dn_zg_ready, 1)
                pool.wait_ge(norm_eps, h + 1)
                if not first:
                    pool.wait_ge(scaled_dve, 3 * h)
                inv_sqrt(rn[:, 1, :], rn[:, 0, :], 4).then_inc(norm_ready, 1)
                pool.wait_ge(scaled_dve, 3 * h + 1)
                if not first:
                    pool.wait_ge(s1_done, h)
                for dst, t, col in ((kd0, 0, C_DL), (kbg1, 1, C_BEG)):
                    pool.tensor_tensor(dst[:, :], tin[:, t, 0, :], hs[:, col:col + 1].to_broadcast([P, P]),
                                       ALU.mult).then_inc(scaled_pool, 1)
                pool.wait_ge(lt_ready, h + 1)
                for n in range(LEVELS):
                    pool.tensor_tensor(mt[:, n, :, :], lt[:, :, :],
                                       levels[:, n, None, :].to_broadcast([P, T, P]), ALU.mult).then_inc(mt_ready, 1)

            pool.wait_ge(rx_mean, 1)
            inv_sqrt(rx[:, 4:6], rx[:, 2:4], T).then_inc(rx_ready, 1)
            pool.wait_ge(tabs_pool, H)
            pool.wait_ge(tabs_ready, 3)
            pool.wait_ge(small_landed, 48)
            head(0, True)
            with pool.Fori(1, H) as h:
                head(h, False)
            output_norm(H - 1)
            pool.wait_ge(gain_landed, 16)
            fg = gate[:, NC:NC + NC // 2, :, :].rearrange("p c t n -> p (c t n)")
            for c in range(NC - 1):
                for t in range(T):
                    pool.wait_ge(f_squared, T * c + t + 1)
                    g = gate[:, c, t, :]
                    pool.tensor_tensor(g, g, fg[:, c * CH:(c + 1) * CH], ALU.mult).then_inc(f_gained, 1)
            for t in range(T):
                pool.wait_ge(f_mean, t + 1)
                inv_sqrt(fr[:, 2, t:t + 1], fr[:, 1, t:t + 1], 1).then_inc(fr_ready, 1)

        @block.tensor
        def _(pe):
            def keep_busy(n):
                for _ in range(n):
                    pe.transpose(pj[1][:, 1, 0:P], ident[:, :], ident[:, :])

            pe.wait_ge(ident_made, 1)
            keep_busy(10)
            pe.wait_ge(rows_landed, 32)
            pe.transpose(E[:, 0:96 + KT], rows[0:96 + KT, :], ident[0:96 + KT, 0:96 + KT]).then_inc(cols_turned, 1)
            banks = [A, B, C, E]

            def turn_x(g):
                pe.wait_ge(x_landed[g], 16)
                if g == 3:
                    pe.wait_ge(cols_ready, 1)
                if g >= 4:
                    pe.wait_ge(xt_lo_ready, 2 * (g - 3))
                for q in range(4):
                    k, t = 2 * g + q // 2, q % 2
                    mm = pe.transpose(banks[g % 4][:, q * P:(q + 1) * P], x_sb[:, t, k * P:(k + 1) * P], ident[:, :])
                mm.then_inc(x_turned, 1)

            def unit(slot, number, hi, lo, k0, bank, kt_all, free, between=None):
                pe.wait_ge(lo_ready, number + 1)
                for t in range(T):
                    if k0 == 0:
                        free(t)
                    for i in range(UK):
                        k = k0 + i
                        tok = slice(t * P, (t + 1) * P)
                        cs = slice(i * CH, (i + 1) * CH)
                        pe.matmul(bank[:, t, :], hi[:, k, tok], w_hi[:, slot, cs], start=(k == 0), stop=False)
                        pe.matmul(bank[:, t, :], hi[:, k, tok], w_lo[:, slot, cs], start=False, stop=False)
                        mm = pe.matmul(bank[:, t, :], lo[:, k, tok], w_hi[:, slot, cs], start=False,
                                       stop=(k == kt_all - 1))
                    if t == T - 1:
                        mm.then_inc(unit_used, 1)
                    elif k == kt_all - 1:
                        mm.then_inc(tile0_done, 1)
                    if between is not None:
                        between(t)

            def first_unit():
                keep_busy(4)
                turn_x(0)
                keep_busy(10)
                turn_x(1)
                keep_busy(6)
                for k in range(UK):
                    if k == 0:
                        pe.wait_ge(first_lo, 1)
                    else:
                        pe.wait_ge(lo_ready, 1)
                    pe.wait_ge(xt_lo_ready, k + 1)
                    for t in range(T):
                        tok = slice(t * P, (t + 1) * P)
                        cs = slice(k * CH, (k + 1) * CH)
                        pe.matmul(pj[0][:, t, :], xt_hi[:, k, tok], w_hi[:, 0, cs], start=(k == 0), stop=False)
                        pe.matmul(pj[0][:, t, :], xt_hi[:, k, tok], w_lo[:, 0, cs], start=False, stop=False)
                        mm = pe.matmul(pj[0][:, t, :], xt_lo[:, k, tok], w_hi[:, 0, cs], start=False, stop=False)
                mm.then_inc(unit_used, 1)
                turn_x(2)
                turn_x(3)

            def dn_step(s, h, first=False):
                if s == S_TURN:
                    pe.wait_ge(dn_nat_ready, T * h + T)
                    if not first:
                        pe.wait_ge(yb_lo_ready, h)
                    for p in range(3):
                        for t in range(T):
                            mm = pe.transpose(dn_ps[:, (p * T + t) * P:(p * T + t + 1) * P],
                                              dn_nat[:, t, p * P:(p + 1) * P], ident[:, :])
                    mm.then_inc(dn_turned, 1)
                if s == S_DEC:
                    pe.wait_ge(hs_ready, h + 1)
                    if not first:
                        pe.wait_ge(ya_ready, T * h)
                    for t in range(T):
                        mm = pe.matmul(E[:, t * P:(t + 1) * P], hs[:, C_G + t:C_G + t + 1].to_broadcast([P, P]),
                                       causal[:, :], start=True, stop=True)
                    mm.then_inc(dec_done, 1)
                if s == S_NAT:
                    pe.wait_ge(convs_ready, h + 1)
                    for i in range(3 * T):
                        mm = pe.transpose(dn_ps[:, i * P:(i + 1) * P], convs[:, i * P:(i + 1) * P], ident[:, :])
                    mm.then_inc(nat_done, 1)
                if s == S_BACK:
                    pe.wait_ge(scaled_dve, 3 * h + 3)
                    pe.wait_ge(scaled_act, 3 * h + 3)
                    for t in range(T):
                        for p in range(3):
                            i = 3 * t + p
                            pe.transpose(dn_ps[:, i * P:(i + 1) * P], tin[:, t, p, :], ident[:, :])
                    pe.transpose(dn_ps[:, 6 * P:7 * P], qg1[:, :], ident[:, :]).then_inc(back_done, 1)
                if s == S_KK:
                    pe.wait_ge(tT_act, h + 1)
                    pe.wait_ge(tT_dve, h + 1)
                    for t in range(T):
                        o = 3 * P * t
                        mm = pe.matmul(A[:, 2 * P * t:2 * P * (t + 1)], tT[:, o:o + P], tT[:, o + P:o + 3 * P],
                                       start=True, stop=True)
                    mm.then_inc(kk_done, 1)
                if s in S_XT:
                    n = S_XT.index(s)
                    if n == 0:
                        pe.wait_ge(x1_step, 2 * h + 2)
                    else:
                        pe.wait_ge(xsT_ready, LEVELS * h + n)
                    for t in range(T):
                        mm = pe.transpose(B[:, t * P:(t + 1) * P], xs[:, T + t, :], ident[:, :])
                    mm.then_inc(xT_turned, 1)
                if s in S_Y:
                    n = S_Y.index(s)
                    if n == 0:
                        pe.wait_ge(lt_ready, h + 1)
                        pe.wait_ge(intra_ready, h + 1)
                    pe.wait_ge(xs_ready, LEVELS * h + n + 1)
                    pe.wait_ge(mt_ready, LEVELS * h + n + 1)
                    x = halves(xs[:, 0:T, :], n, 0)
                    for t in range(T):
                        mm = pe.matmul(packed(A, 0, n)[:, t], mt[:, n, t, :], x[:, t], start=True, stop=True)
                    mm.then_inc(y_done, 1)
                if s in S_XY:
                    n = S_XY.index(s)
                    pe.wait_ge(y_ready, LEVELS * h + n + 1)
                    xT = halves(xs[:, T:2 * T, :], n, 1)
                    for t in range(T):
                        mm = pe.matmul(packed(B, T, n)[:, t], ysb[:, n, t, :], xT[:, t], start=True, stop=True)
                    mm.then_inc(xy_done, 1)
                if s == S_U:
                    pe.wait_ge(xsT_ready, LEVELS * h + LEVELS)
                    pe.wait_ge(scaled_pool, 2 * h + 2)
                    for t in range(T):
                        pe.matmul(A[:, t * P:(t + 1) * P], xs[:, T + t, :], vb[:, t, :], start=True, stop=True)
                    pe.matmul(B[:, 3 * P:4 * P], kbg1[:, :], xs[:, T + 1, :], start=True, stop=True).then_inc(u_done, 1)
                if s == S_S1:
                    pe.wait_ge(u_ready, h + 1)
                    pe.wait_ge(wT_ready, h + 1)
                    pe.matmul(B[:, P:2 * P], intra[:, 0, :], u[:, 0, :], start=True, stop=True)
                    pe.matmul(B[:, 0:P], kd0[:, :], u[:, 0, :], start=True, stop=True).then_inc(s1_done, 1)
                if s == S_WS:
                    pe.wait_ge(s1_ready, h + 1)
                    pe.matmul(A[:, 3 * P:4 * P], wT[:, :], s1[:, :], start=True, stop=True).then_inc(ws_done, 1)
                if s == S_O1:
                    pe.wait_ge(vnew_ready, h + 1)
                    pe.matmul(B[:, 2 * P:3 * P], tT[:, 6 * P:7 * P], s1[:, :], start=True, stop=False)
                    pe.matmul(B[:, 2 * P:3 * P], intra[:, 1, :], vnew[:, :], start=False, stop=True).then_inc(o_done, 1)
                if s == S_YT:
                    pe.wait_ge(yb_ready, T * h + T)
                    for t in range(T):
                        mm = pe.transpose(A[:, t * P:(t + 1) * P], yb[:, t, :], ident[:, :])
                    mm.then_inc(ybT_done, 1)

            def mo_step(s, h, first=False):
                if s == M_TURN:
                    pe.wait_ge(mo_nat_ready, T * h + T)
                    pe.wait_ge(dsub_ready, T * h + T)
                    if not first:
                        pe.wait_ge(ya_lo_ready, h)
                    for p in range(2):
                        for t in range(T):
                            mm = pe.transpose(C[:, (p * T + t) * P:(p * T + t + 1) * P],
                                              mo_nat[:, t, p * P:(p + 1) * P], ident[:, :])
                    mm.then_inc(mo_turned, 1)
                if s == M_QK:
                    pe.wait_ge(moT_ready, h + 1)
                    pe.matmul(E[:, 0:P], moT[:, 0, 0:P], moT[:, 1, 0:P], start=True, stop=True)
                    pe.matmul(E[:, P:3 * P], moT[:, 0, P:2 * P], moT[:, 1, :], start=True, stop=True).then_inc(qk_done, 1)
                if s == M_PT:
                    pe.wait_ge(prob_ready, T * h + T)
                    for i in range(3):
                        mm = pe.transpose(C[:, i * P:(i + 1) * P], prob[:, i * P:(i + 1) * P], ident[:, :])
                    mm.then_inc(pt_done, 1)
                if s == M_PV:
                    pe.wait_ge(pt_ready, h + 1)
                    v = [mo_nat[:, t, 2 * P:3 * P] for t in range(T)]
                    pe.matmul(E[:, 0:P], probT[:, 0:P], v[0], start=True, stop=True)
                    pe.matmul(E[:, P:2 * P], probT[:, P:2 * P], v[0], start=True, stop=False)
                    pe.matmul(E[:, P:2 * P], probT[:, 2 * P:3 * P], v[1], start=False, stop=True).then_inc(pv_done, 1)
                if s == M_YT:
                    pe.wait_ge(ya_ready, T * h + T)
                    for t in range(T):
                        mm = pe.transpose(C[:, t * P:(t + 1) * P], ya[:, t, :], ident[:, :])
                    mm.then_inc(yaT_done, 1)

            def beta_decay_inputs():
                pe.wait_ge(const_made, 1)
                pe.wait_ge(wba_hi_ready, 1)
                pe.wait_ge(wba_lo_ready, 2)
                n = 2 * H
                for k in range(KT):
                    pe.matmul(E[0:2 * n, 0:SEQ], wba_parts[:, k, :, :].rearrange("p e n -> p (e n)"), xt_hi[:, k, :],
                              start=(k == 0), stop=False)
                    mm = pe.matmul(E[0:n, 0:SEQ], wba_parts[:, k, 0, :], xt_lo[:, k, :], start=False, stop=(k == KT - 1))
                mm.then_inc(ba_done, 1)

            def beta_decay_turned():
                pe.wait_ge(baT_ready, 1)
                n = 2 * H
                for t in range(T):
                    mm = pe.matmul(C[:, t * n:(t + 1) * n], baT[:, t * P:(t + 1) * P], fold[:, :], start=True, stop=True)
                mm.then_inc(ba_turned, 1)

            def cumulate():
                pe.wait_ge(g_ready, 1)
                g = gl[:, :, :].rearrange("p t h -> p (t h)")
                pe.matmul(C[:, 64:64 + T * H], causal[:, :], g, start=True, stop=True)
                pe.matmul(C[:, 128:128 + T * H], ones[:, :], g, start=True, stop=True).then_inc(cum_done, 1)

            def iteration(h, first):
                for j in range(1 if first else 0, UNITS):
                    c = j // (KT // UK)
                    k0 = (j % (KT // UK)) * UK

                    def free(t, c=c):
                        if c == 0:
                            if not first:
                                pe.wait_ge(gate_ready, T * h - T + t + 1)
                        if c == 1 and not first:
                            pe.wait_ge(mo_nat_ready, T * h - T + t + 1)
                        if c == 2:
                            pe.wait_ge(dn_nat_ready, T * h + t + 1)

                    if first and j < XU:
                        pe.wait_ge(xt_lo_ready, UK * j + UK)

                    def between(t, j=j):
                        s = T * j + t
                        if not first:
                            dn_step(s + SLOTS, h - 1)
                        dn_step(s, h, first)
                        mo_step(s, h, first)
                        if first and s == 2 * XU - 2:
                            beta_decay_turned()
                        if first and s == 2 * XU + 1:
                            cumulate()

                    unit(j % RING, h * UNITS + j, xt_hi, xt_lo, k0, pj[c % 2], KT, free, between)
                    if first and j + 3 < XU:
                        turn_x(j + 3)
                    if first and j == XU - 2:
                        beta_decay_inputs()

            first_unit()
            iteration(0, True)
            with pe.Fori(1, H) as h:
                iteration(h, False)

            def branch(c, hi, lo, first_unit, number, dn):
                for j in range(BU):
                    def free(t):
                        if number == 0:
                            pe.wait_ge(gate_ready, T * (H - 1) + t + 1)
                        elif number == 1:
                            pe.wait_ge(mo_nat_ready, T * H)
                        else:
                            pe.wait_ge(a_gated, T * (number - 2) + t + 1)

                    def between(t, j=j):
                        dn_step(dn + T * j + t + SLOTS, H - 1)

                    if c == 0 and j == BU - 1:
                        pe.wait_ge(ya_lo_ready, H)
                    unit(j % RING, first_unit + c * BU + j, hi, lo, UK * j, pj[number % 2], H, free, between)

            for c in range(NC):
                branch(c, ya_hi, ya_lo, FIRST_A, c, 2 * BU * c)

            def turn_merged(c):
                pe.wait_ge(merged, T * c + T)
                ps = [dn_ps, mo_ps][c % 2]
                if c >= 2:
                    pe.wait_ge(mT_lo_ready, 2 * (c - 1))
                for half in range(2):
                    for q in range(4):
                        i, t = 2 * half + q // 2, q % 2
                        mm = pe.transpose(ps[:, (4 * half + q) * P:(4 * half + q + 1) * P],
                                          gate[:, NC + c, t, i * P:(i + 1) * P], ident[:, :])
                    mm.then_inc(mT_done, 1)

            for c in range(NC):
                def free(t, c=c):
                    if c < 2:
                        pe.wait_ge(a_gated, T * (c + 2) + t + 1)
                    else:
                        pe.wait_ge(b_gated, T * (c - 2) + t + 1)
                for j in range(BU):
                    if c == 0 and j == BU - 1:
                        pe.wait_ge(yb_lo_ready, H)
                    unit(j % RING, FIRST_B + c * BU + j, yb_hi, yb_lo, UK * j, pj[c % 2], H, free)
                    if j == 2 and c > 0:
                        turn_merged(c - 1)
            for c in range(NC - 1):
                def free(t, c=c):
                    if c < 2:
                        pe.wait_ge(b_gated, T * (c + 2) + t + 1)
                    else:
                        pe.wait_ge(sum_ready, T * (c - 2) + t + 1)
                for j in range(OU):
                    if c == 0:
                        pe.wait_ge(mT_hi_ready, j + 1)
                        pe.wait_ge(mT_lo_ready, j + 1)
                    unit(j % RING, FIRST_O + c * OU + j, xt_hi, xt_lo, UK * j, pj[c % 2], KT, free)
                    if c == 0 and j == 2:
                        turn_merged(NC - 1)
            c = NC - 1
            for t in range(T):
                pe.wait_ge(sum_ready, T * (c - 2) + t + 1)
                tok = slice(t * P, (t + 1) * P)
                for k in range(KT):
                    number = FIRST_O + OU * c + k // UK
                    if t == 0 and k % UK == 0:
                        pe.wait_ge(lo_ready, number + 1)
                    hi, lo = parts(number)
                    cs = slice(k % UK * CH, (k % UK + 1) * CH)
                    pe.matmul(pj[c % 2][:, t, :], xt_hi[:, k, tok], hi[:, cs], start=(k == 0), stop=False)
                    pe.matmul(pj[c % 2][:, t, :], xt_hi[:, k, tok], lo[:, cs], start=False, stop=False)
                    mm = pe.matmul(pj[c % 2][:, t, :], xt_lo[:, k, tok], hi[:, cs], start=False, stop=(k == KT - 1))
                    if t == T - 1 and k % UK == UK - 1:
                        mm.then_inc(unit_used, 1)
                    elif k == KT - 1:
                        mm.then_inc(tile0_done, 1)

        @block.scalar
        def _(act):
            def split(slot, number, landed, first=False):
                act.wait_ge(w_landed[slot], landed - 16 if slot == 0 else landed)
                if not first:
                    act.wait_ge(unit_used, number - RING + 1)
                act.activation(w_hi[:, slot, :], w_raw[:, slot, :], ACT.Copy).then_inc(hi_ready, 1)

            act.wait_ge(ident_made, 1)
            act.activation(fr[:, 0, 0:1], ident[:, 0:1], ACT.Copy).then_inc(table_loaded, 1)
            act.wait_ge(cols_ready, 1)
            x_banks = [A, B, C, E]
            for g in range(XU):
                act.wait_ge(x_turned, g + 1)
                for k in (2 * g, 2 * g + 1):
                    act.activation(xt_hi[:, k, :], x_banks[g % 4][:, (k % 2) * SEQ:(k % 2 + 1) * SEQ], ACT.Copy,
                                   scale=cols[:, 96 + k:97 + k]).then_inc(xt_hi_ready, 1)
                    if k == 0:
                        act.wait_ge(first_landed, 16)
                        act.activation(w_hi[:, 0, 0:CH], w_raw[:, 0, 0:CH], ACT.Copy).then_inc(first_hi, 1)
                    if k == 1:
                        act.wait_ge(w_landed[0], 16)
                        act.activation(w_hi[:, 0, CH:], w_raw[:, 0, CH:], ACT.Copy).then_inc(hi_ready, 1)
                if g > 0:
                    split(g % RING, g, (g // RING + 1) * 32, g < RING)

            def start_stats():
                act.wait_ge(wba_landed, 16)
                act.activation(wba_parts[:, :, 0, :], wba[:, :].rearrange("p (k n) -> p k n", k=KT),
                               ACT.Copy).then_inc(wba_hi_ready, 1)
                act.activation(gate[:, NC:NC + NC // 2, :, :].rearrange("p c t n -> p (c t n)"), x_sb[:, 0, :], ACT.Square,
                               accum_out=rx[:, 0:1]).then_inc(x_squared_act, 1)

            def tables():
                act.wait_ge(ba_done, 1)
                act.activation(baT[:, :], E[0:4 * H, 0:SEQ], ACT.Copy).then_inc(baT_ready, 1)
                act.wait_ge(rx_ready, 1)
                act.wait_ge(ba_turned, 1)
                for t in range(T):
                    act.activation(ba[:, t, :], C[:, t * 2 * H:(t + 1) * 2 * H], ACT.Copy,
                                   scale=rx[:, 4 + t:5 + t]).then_inc(ba_ready, 1)
                act.wait_ge(ba_ready, T)
                act.activation(ba[:, :, 0:H], ba[:, :, 0:H], ACT.Exp, scale=-1.0).then_inc(beta_exp, 1)
                act.wait_ge(tab_step, 2)
                act.activation(sp[:, 1, :, :], sp[:, 1, :, :], ACT.Exp).then_inc(tab_act, 1)
                act.wait_ge(small_landed, 48)
                act.activation(alog[:, :], alog[:, :], ACT.Exp).then_inc(tab_act, 1)
                act.wait_ge(tab_act, 2)
                act.activation(sp[:, 2, :, :], sp[:, 1, :, :], ACT.Ln, bias=ones[:, 0:1]).then_inc(tab_act, 1)

            def tables_cumulated():
                act.wait_ge(cum_ready, 2)
                act.activation(sp[:, 0:2, :, :], cum[:, :, :, :], ACT.Exp).then_inc(tab_act, 1)

            def dn_step(s, h, first=False):
                if s == S_TURN - 2:
                    if first:
                        act.wait_ge(rx_ready, 1)
                    if not first:
                        act.wait_ge(dn_turned, h)
                        act.wait_ge(dn_z_ready, h)
                    for t in range(T):
                        wait_chunk(act, t, 3 * h, UNITS * h + UNITS // 3 - 1)
                        act.activation(dn_nat[:, t, :], pj[0][:, t, :], ACT.Copy,
                                       scale=rx[:, 4 + t:5 + t]).then_inc(dn_nat_ready, 1)
                if s == S_DEC + 1:
                    act.wait_ge(dsub_ready, T * h + T)
                    act.activation(dsub[:, :, :], dsub[:, :, :], ACT.Exp).then_inc(dexp_ready, 1)
                if s == S_NAT - 1:
                    act.wait_ge(conv_step, 12 * h + 12)
                    if not first:
                        act.wait_ge(nat_done, h)
                    act.activation(convs[:, :], conv[:, :, :].rearrange("p a t -> p (a t)"), ACT.Silu).then_inc(convs_ready, 1)
                    if not first:
                        act.wait_ge(yb_ready, T * h)
                    act.activation(dn_z[:, :, :], dn_nat[:, :, 3 * P:4 * P], ACT.Silu).then_inc(dn_z_ready, 1)
                if s == S_NAT:
                    act.wait_ge(nat_done, h + 1)
                    if not first:
                        act.wait_ge(norm_eps, h)
                    for i in range(2 * T):
                        act.activation(mt[:, i // 2, i % 2, :], dn_ps[:, i * P:(i + 1) * P], ACT.Square,
                                       accum_out=ss[:, i:i + 1]).then_inc(norm_squared, 1)
                if s == S_NAT + 2:
                    if not first:
                        act.wait_ge(back_done, h)
                    act.wait_ge(scaled_dve, 3 * h + 1)
                    for t in range(T):
                        act.activation(tin[:, t, 1, :], tin[:, t, 0, :], ACT.Copy,
                                       scale=hs[:, C_BETA + t:C_BETA + t + 1]).then_inc(scaled_act, 1)
                    act.wait_ge(scaled_dve, 3 * h + 2)
                    act.activation(qg1[:, :], tin[:, 1, 2, :], ACT.Copy,
                                   scale=hs[:, C_EG:C_EG + 1]).then_inc(scaled_act, 1)
                if s == S_BACK:
                    act.wait_ge(back_done, h + 1)
                    act.activation(tT[:, 0:4 * P], dn_ps[:, 0:4 * P], ACT.Copy).then_inc(tT_act, 1)
                if s in S_XT:
                    act.wait_ge(xT_turned, LEVELS * h + S_XT.index(s) + 1)
                    act.activation(xs[:, 0:T, :].rearrange("p t n -> p (t n)"), B[:, 0:T * P], ACT.Copy).then_inc(xs_ready, 1)
                if s in S_Y:
                    n = S_Y.index(s)
                    act.wait_ge(y_done, LEVELS * h + n + 1)
                    act.activation(halves(ysb[:, n, :, :], n, 0), packed(A, 0, n), ACT.Copy).then_inc(y_ready, 1)
                if s == S_U:
                    act.wait_ge(u_done, h + 1)
                    if not first:
                        act.wait_ge(o_done, h)
                    act.activation(u[:, :, :].rearrange("p t n -> p (t n)"), A[:, 0:T * P], ACT.Copy).then_inc(u_ready, 1)
                if s == S_O1:
                    act.wait_ge(o_done, h + 1)
                    if not first:
                        act.wait_ge(o_mean, h)
                    for t in range(T):
                        act.activation(mt[:, 2, t, :], B[:, (1 + t) * P:(2 + t) * P], ACT.Square,
                                       accum_out=so[:, t:t + 1]).then_inc(o_squared, 1)
                if s == S_YT:
                    act.wait_ge(ybT_done, h + 1)
                    act.activation(yb_hi[:, bass.ds(h, 1), :].rearrange("p a n -> p (a n)"), A[:, 0:SEQ],
                                   ACT.Copy).then_inc(yb_hi_ready, 1)

            def mo_step(s, h, first=False):
                if s == M_TURN - 2:
                    if not first:
                        act.wait_ge(pv_done, h)
                        act.wait_ge(mo_z_ready, h)
                    for t in range(T):
                        wait_chunk(act, t, 3 * h + 1, UNITS * h + 2 * UNITS // 3 - 1)
                        act.activation(mo_nat[:, t, :], pj[1][:, t, :], ACT.Copy,
                                       scale=rx[:, 4 + t:5 + t]).then_inc(mo_nat_ready, 1)
                if s == M_TURN:
                    act.wait_ge(mo_turned, h + 1)
                    act.activation(moT[:, :, :].rearrange("p a t -> p (a t)"), C, ACT.Copy).then_inc(moT_ready, 1)
                    if not first:
                        act.wait_ge(ya_ready, T * h)
                    act.activation(mo_z[:, :, :], mo_nat[:, :, 3 * P:4 * P], ACT.Silu).then_inc(mo_z_ready, 1)
                if s == M_EXP:
                    act.wait_ge(mx_ready, h + 1)
                    if not first:
                        act.wait_ge(rsum_ready, h)
                    act.activation(prob[:, 0:P], sm[:, 0:P], ACT.Exp, bias=mx[:, 0:1], scale=SCALE,
                                   accum_out=mx[:, 2:3]).then_inc(prob_ready, 1)
                    act.activation(prob[:, P:3 * P], sm[:, P:3 * P], ACT.Exp, bias=mx[:, 1:2], scale=SCALE,
                                   accum_out=mx[:, 3:4]).then_inc(prob_ready, 1)
                if s == M_PT:
                    act.wait_ge(pt_done, h + 1)
                    act.activation(probT[:, :], C[:, 0:3 * P], ACT.Copy).then_inc(pt_ready, 1)
                if s == M_YT:
                    act.wait_ge(yaT_done, h + 1)
                    act.activation(ya_hi[:, bass.ds(h, 1), :].rearrange("p a n -> p (a n)"), C[:, 0:SEQ],
                                   ACT.Copy).then_inc(ya_hi_ready, 1)

            def gates(h, t):
                wait_chunk(act, t, 3 * h + 2, UNITS * h + UNITS - 1)
                act.activation(gate[:, bass.ds(h, 1), t, :].rearrange("p a n -> p (a n)"), pj[0][:, t, :],
                               ACT.Copy, scale=rx[:, 4 + t:5 + t]).then_inc(gate_ready, 1)

            def iteration(h, first):
                for s in range(SLOTS):
                    if first and s == 2 * XU - 6:
                        start_stats()
                    if first and s == 2 * XU - 1:
                        tables()
                    if not first:
                        dn_step(s + SLOTS, h - 1)
                    dn_step(s, h, first)
                    mo_step(s, h, first)
                    if s == SLOTS - 2:
                        gates(h, 0)
                    if first and s == 2 * XU:
                        tables_cumulated()
                    if s == SLOTS - 1:
                        gates(h, 1)
                    n = s // 2 + LEAD
                    if s % 2 == (1 if s >= SLOTS - 2 else 0) and not (first and n < XU):
                        split(n % RING, h * UNITS + n, (h * (UNITS // RING) + n // RING + 1) * 32)

            iteration(0, True)
            with act.Fori(1, H) as h:
                iteration(h, False)

            def tail_split(n):
                if n < FIRST_O + NC * OU - RING:
                    split(n % RING, n, (n // RING + 1) * 32)
                else:
                    slot = n % RING
                    act.wait_ge(w_landed[slot], (n // RING + 1) * 32 - (16 if slot == 0 else 0))
                    act.activation(parts(n)[0], w_raw[:, slot, :], ACT.Copy).then_inc(hi_ready, 1)

            for c in range(NC):
                for j in range(BU):
                    dn_step(2 * BU * c + 2 * j + SLOTS, H - 1)
                    tail_split(FIRST_A + BU * c + j + LEAD)
                    dn_step(2 * BU * c + 2 * j + 1 + SLOTS, H - 1)
                    n = BU * c + j - 5
                    if 0 <= n < NG:
                        if n == 0:
                            act.wait_ge(gate_ready, T * H)
                        act.activation(gate[:, n, :, :], gate[:, n, :, :], ACT.Sigmoid).then_inc(sig_ready, 1)

            def merged_hi(c):
                ps = [dn_ps, mo_ps][c % 2]
                for half in range(2):
                    act.wait_ge(mT_done, 2 * c + half + 1)
                    act.activation(xt_hi[:, 4 * c + 2 * half:4 * c + 2 * half + 2, :].rearrange("p k t -> p (k t)"),
                                   ps[:, half * CH:(half + 1) * CH], ACT.Copy).then_inc(mT_hi_ready, 1)

            for n in range(NC * BU):
                tail_split(FIRST_B + n + LEAD)
                if n % BU == 2 and n > BU:
                    merged_hi(n // BU - 1)

            def squares(c):
                for t in range(T):
                    act.wait_ge(sum_ready, T * c + t + 1)
                    if T * c + t >= 2:
                        act.wait_ge(f_squared, T * c + t - 1)
                    act.activation(sq[:, t, :], gate[:, c, t, :], ACT.Square,
                                   accum_out=fs[:, t, c:c + 1]).then_inc(f_squared, 1)

            sq = mt[:, 0:4, :, :].rearrange("p (b a) t n -> p b (a t n)", a=2)
            for n in range(NC * OU - LEAD):
                tail_split(FIRST_O + n + LEAD)
                if n == 3:
                    merged_hi(NC - 1)
                if n % OU == 1 and n > OU:
                    squares(n // OU - 1)
            squares(NC - 1)
            act.wait_ge(fr_ready, T)
            act.activation(gate[:, 0, 1, :], gate[:, 0, 1, :], ACT.Copy, scale=fr[:, 2, 1:2]).then_inc(y_act, 1)

        @block.vector
        def _(dve):
            def split(slot, number, first=False):
                dve.wait_ge(hi_ready, number + 1)
                dve.tensor_tensor(w_lo[:, slot, :], w_raw[:, slot, :], w_hi[:, slot, :].bitcast(F32),
                                  ALU.subtract).then_inc(lo_ready, 1)

            dve.wait_ge(cols_turned, 1)
            dve.tensor_copy(cols[:, 0:96 + KT], E[:, 0:96 + KT]).then_inc(cols_ready, 1)
            dve.wait_ge(cols_ready, 1)
            x_banks = [A, B, C, E]
            for g in range(XU):
                dve.wait_ge(xt_hi_ready, 2 * g + 2)
                for k in (2 * g, 2 * g + 1):
                    src = x_banks[g % 4][:, (k % 2) * SEQ:(k % 2 + 1) * SEQ]
                    dve.scalar_tensor_tensor(out=xt_lo[:, k, :], in0=src, scalar=cols[:, 96 + k:97 + k],
                                             in1=xt_hi[:, k, :].bitcast(F32), op0=ALU.mult,
                                             op1=ALU.subtract).then_inc(xt_lo_ready, 1)
                    if k < UK:
                        dve.wait_ge(*((first_hi, 1) if k == 0 else (hi_ready, 1)))
                        cs = slice(k * CH, (k + 1) * CH)
                        dve.tensor_tensor(w_lo[:, 0, cs], w_raw[:, 0, cs], w_hi[:, 0, cs].bitcast(F32),
                                          ALU.subtract).then_inc(first_lo if k == 0 else lo_ready, 1)
                if g > 0:
                    split(g % RING, g)

            def start_stats():
                dve.wait_ge(const_made, 1)
                taps = cols[:, 0:96].rearrange("p (j a h) -> p h a j", j=4, a=3)
                for a in range(3):
                    dve.tensor_copy(tabs[:, :, C_CONV + 4 * a:C_CONV + 4 * a + 4], taps[:, :, a, :]).then_inc(tabs_ready, 1)
                dve.wait_ge(wba_hi_ready, 1)
                dve.tensor_tensor(wba_parts[:, :, 1, :], wba[:, :].rearrange("p (k n) -> p k n", k=KT),
                                  wba_parts[:, :, 0, :].bitcast(F32), ALU.subtract).then_inc(wba_lo_ready, 1)
                n = 2 * H
                dve.tensor_tensor(fold[:, :], ident[0:2 * n, 0:n], ident[0:2 * n, n:2 * n], ALU.add).then_inc(wba_lo_ready, 1)
                dve.tensor_tensor_reduce(gate[:, NC + NC // 2:2 * NC, :, :].rearrange("p c t n -> p (c t n)"),
                                         x_sb[:, 1, :], x_sb[:, 1, :], 1.0, 0.0, ALU.mult,
                                         ALU.add, rx[:, 1:2]).then_inc(x_squared, 1)
                dve.wait_ge(x_squared, 1)
                dve.wait_ge(x_squared_act, 1)
                dve.tensor_scalar(rx[:, 2:4], rx[:, 0:2], 1.0 / D, EPS, ALU.mult, ALU.add).then_inc(rx_mean, 1)

            def tables():
                dve.wait_ge(ba_ready, T)
                dve.wait_ge(small_landed, 48)
                dve.tensor_tensor(sp[:, 0, :, :], ba[:, :, H:2 * H], dtb[:, None, :].to_broadcast([P, T, H]),
                                  ALU.add).then_inc(tab_step, 1)
                dve.wait_ge(tab_step, 1)
                dve.scalar_tensor_tensor(out=sp[:, 1, :, :], in0=sp[:, 0, :, :], scalar=-1.0, in1=sp[:, 0, :, :],
                                         op0=ALU.mult, op1=ALU.min).then_inc(tab_step, 1)
                dve.wait_ge(beta_exp, 1)
                dve.tensor_scalar(ba[:, :, 0:H], ba[:, :, 0:H], 1.0, None, ALU.add).then_inc(beta_ready, 1)
                dve.wait_ge(beta_ready, 1)
                dve.reciprocal(tabs[:, :, C_BETA:C_BETA + T].rearrange("p h t -> p t h"), ba[:, :, 0:H]).then_inc(beta_ready, 1)
                dve.wait_ge(tab_act, 3)
                dve.scalar_tensor_tensor(out=sp[:, 3, :, :], in0=sp[:, 0, :, :], scalar=0.0, in1=sp[:, 2, :, :],
                                         op0=ALU.max, op1=ALU.add).then_inc(tab_step, 1)
                dve.wait_ge(tab_step, 3)
                dve.scalar_tensor_tensor(out=gl[:, :, :], in0=sp[:, 3, :, :], scalar=-1.0,
                                         in1=alog[:, None, :].to_broadcast([P, T, H]), op0=ALU.mult,
                                         op1=ALU.mult).then_inc(g_ready, 1)

            def tables_cumulated():
                dve.wait_ge(cum_done, 1)
                c0 = C[:, 64:64 + T * H].rearrange("p (t h) -> p t h", t=T)
                dve.tensor_copy(cum[:, 0, :, :], c0).then_inc(cum_ready, 1)
                dve.wait_ge(cum_ready, 1)
                dve.tensor_tensor(cum[:, 1, :, :], C[:, 128:128 + T * H].rearrange("p (t h) -> p t h", t=T),
                                  cum[:, 0, :, :], ALU.subtract).then_inc(cum_ready, 1)
                dve.wait_ge(g_ready, 1)
                dve.tensor_copy(tabs[:, :, C_G:C_G + T].rearrange("p h t -> p t h"), gl[:, :, :]).then_inc(tabs_ready, 1)
                dve.tensor_copy(tabs[:, :, C_CUM:C_CUM + T].rearrange("p h t -> p t h"),
                                cum[:, 0, :, :]).then_inc(tabs_ready, 1)
                dve.wait_ge(tab_act, 4)
                dve.wait_ge(beta_ready, 2)
                dve.tensor_copy(tabs[:, :, C_EG], sp[:, 0, 1, :]).then_inc(tabs_ready, 1)
                dve.tensor_copy(tabs[:, :, C_DL], sp[:, 1, 0, :]).then_inc(tabs_ready, 1)
                dve.tensor_tensor(tabs[:, :, C_BEG], sp[:, 0, 1, :], tabs[:, :, C_BETA + 1], ALU.mult).then_inc(tabs_ready, 1)

            def dn_step(s, h, first=False):
                if s in (S_TURN, S_DEC):
                    if s == S_TURN:
                        dve.wait_ge(dn_turned, h + 1)
                        dve.wait_ge(taps_ready, h + 1)
                        if not first:
                            dve.wait_ge(convs_ready, h)
                    for back in ((0, 1) if s == S_TURN else (2, 3)):
                        if back == 2:
                            dve.wait_ge(dec_done, h + 1)
                            if not first:
                                dve.wait_ge(decay_ready, h)
                            for t in range(T):
                                dve.tensor_scalar(dsub[:, t, :], E[:, t * P:(t + 1) * P], hs[:, C_CUM + t:C_CUM + t + 1],
                                                  0.0, ALU.subtract, ALU.min).then_inc(dsub_ready, 1)
                        for p in range(3):
                            tap = hs[:, C_CONV + 4 * p + 3 - back:C_CONV + 4 * p + 4 - back]
                            u_ = dn_ps[:, p * SEQ:(p + 1) * SEQ]
                            if back == 0:
                                dve.tensor_scalar(conv[:, p, :], u_, tap, None, ALU.mult).then_inc(conv_step, 1)
                            else:
                                dve.wait_ge(conv_step, 12 * h + 3 * (back - 1) + p + 1)
                                dve.scalar_tensor_tensor(out=conv[:, p, back:SEQ], in0=u_[:, 0:SEQ - back], scalar=tap,
                                                         in1=conv[:, p, back:SEQ], op0=ALU.mult,
                                                         op1=ALU.add).then_inc(conv_step, 1)
                if s == S_NAT:
                    dve.wait_ge(norm_squared, 2 * T * (h + 1))
                    if not first:
                        dve.wait_ge(norm_ready, h)
                    dve.tensor_scalar(rn[:, 0, :], ss[:, :], EPS, None, ALU.add).then_inc(norm_eps, 1)
                    r = rn[:, 1, :]
                    dve.wait_ge(norm_ready, h + 1)
                    ps = dn_ps[:, 0:6 * P].rearrange("p (a t n) -> p a t n", a=3, t=T)
                    if not first:
                        dve.wait_ge(back_done, h)
                        dve.wait_ge(scaled_pool, 2 * h)
                        dve.wait_ge(u_done, h)
                    dve.tensor_tensor(tin[:, :, 0, :], ps[:, 1], r[:, 2:4, None].to_broadcast([P, T, P]),
                                      ALU.mult).then_inc(scaled_dve, 1)
                    dve.scalar_tensor_tensor(out=tin[:, :, 2, :], in0=ps[:, 0], scalar=SCALE,
                                             in1=r[:, 0:2, None].to_broadcast([P, T, P]), op0=ALU.mult,
                                             op1=ALU.mult).then_inc(scaled_dve, 1)
                    dve.tensor_tensor(vb[:, :, :], ps[:, 2], hs[:, C_BETA:C_BETA + 2, None].to_broadcast([P, T, P]),
                                      ALU.mult).then_inc(scaled_dve, 1)
                if s == S_BACK:
                    dve.wait_ge(back_done, h + 1)
                    if not first:
                        dve.wait_ge(o_done, h)
                    dve.tensor_copy(tT[:, 4 * P:7 * P], dn_ps[:, 4 * P:7 * P]).then_inc(tT_dve, 1)
                    dve.wait_ge(dexp_ready, h + 1)
                    dve.tensor_tensor(decay[:, :, :], dsub[:, :, :], causal[:, None, :].to_broadcast([P, T, P]),
                                      ALU.mult).then_inc(decay_ready, 1)
                if s == S_KK:
                    dve.wait_ge(kk_done, h + 1)
                    dve.wait_ge(decay_ready, h + 1)
                    if not first:
                        dve.wait_ge(mt_ready, LEVELS * h)
                        dve.wait_ge(u_done, h)
                    ps = A.rearrange("p (t a n) -> p t a n", t=T, a=2)
                    dve.tensor_tensor(lt[:, :, :], ps[:, :, 0, :], decay[:, :, :], ALU.mult).then_inc(lt_ready, 1)
                    dve.wait_ge(lt_ready, h + 1)
                    dve.tensor_tensor(u[:, :, :], lt[:, :, :], neg1[:, None, :].to_broadcast([P, T, P]),
                                      ALU.mult).then_inc(x1_step, 1)
                    dve.wait_ge(x1_step, 2 * h + 1)
                    dve.tensor_tensor(xs[:, T:2 * T, :], u[:, :, :], ident[:, None, :].to_broadcast([P, T, P]),
                                      ALU.add).then_inc(x1_step, 1)
                    dve.tensor_tensor(intra[:, :, :], ps[:, :, 1, :], decay[:, :, :], ALU.mult).then_inc(intra_ready, 1)
                if s in S_XY:
                    n = S_XY.index(s)
                    dve.wait_ge(xy_done, LEVELS * h + n + 1)
                    xT = halves(xs[:, T:2 * T, :], n, 1)
                    dve.tensor_tensor(xT, xT, packed(B, T, n), ALU.subtract).then_inc(xsT_ready, 1)
                if s == S_U:
                    dve.wait_ge(u_done, h + 1)
                    dve.tensor_copy(wT[:, :], B[:, 3 * P:4 * P]).then_inc(wT_ready, 1)
                if s == S_S1:
                    dve.wait_ge(s1_done, h + 1)
                    dve.tensor_copy(s1[:, :], B[:, 0:P]).then_inc(s1_ready, 1)
                if s == S_WS:
                    dve.wait_ge(ws_done, h + 1)
                    dve.tensor_tensor(vnew[:, :], u[:, 1, :], A[:, 3 * P:4 * P], ALU.subtract).then_inc(vnew_ready, 1)
                if s == S_O1 + 1:
                    dve.wait_ge(o_squared, T * (h + 1))
                    if not first:
                        dve.wait_ge(ro_ready, h)
                    dve.tensor_scalar(ro[:, 0, :], so[:, :], 1.0 / P, EPS, ALU.mult, ALU.add).then_inc(o_mean, 1)
                    dve.wait_ge(dn_zg_ready, h + 1)
                    dve.wait_ge(ro_ready, h + 1)
                    r = ro[:, 1, :]
                    for t in range(T):
                        dve.scalar_tensor_tensor(out=yb[:, t, :], in0=B[:, (1 + t) * P:(2 + t) * P], scalar=r[:, t:t + 1],
                                                 in1=dn_z[:, t, :], op0=ALU.mult, op1=ALU.mult).then_inc(yb_ready, 1)
                if s == S_YT:
                    dve.wait_ge(yb_hi_ready, h + 1)
                    hd = bass.ds(h, 1)
                    dve.tensor_tensor(yb_lo[:, hd, :], A[:, 0:SEQ].rearrange("p (a n) -> p a n", a=1),
                                      yb_hi[:, hd, :].bitcast(F32), ALU.subtract).then_inc(yb_lo_ready, 1)

            def mo_step(s, h, first=False):
                if s == M_QK:
                    dve.wait_ge(qk_done, h + 1)
                    dve.wait_ge(hs_ready, h + 1)
                    if not first:
                        dve.wait_ge(prob_ready, T * h)
                    dve.scalar_tensor_tensor(out=sm[:, :], in0=far[:, :], scalar=hs[:, C_SLOPE:C_SLOPE + 1],
                                             in1=E[:, 0:3 * P], op0=ALU.mult, op1=ALU.add).then_inc(sm_ready, 1)
                    dve.wait_ge(sm_ready, h + 1)
                    dve.tensor_reduce(mx[:, 4:5], sm[:, 0:P], AX_X, ALU.max).then_inc(max_step, 1)
                    dve.tensor_reduce(mx[:, 5:6], sm[:, P:3 * P], AX_X, ALU.max).then_inc(max_step, 1)
                    dve.wait_ge(max_step, 2 * h + 2)
                    dve.tensor_scalar(mx[:, 0:2], mx[:, 4:6], -SCALE, None, ALU.mult).then_inc(mx_ready, 1)
                if s == M_EXP + 1:
                    dve.wait_ge(prob_ready, T * h + T)
                    dve.reciprocal(mx[:, 6:8], mx[:, 2:4]).then_inc(rsum_ready, 1)
                if s == M_PV:
                    dve.wait_ge(pv_done, h + 1)
                    dve.wait_ge(rsum_ready, h + 1)
                    dve.wait_ge(mo_z_ready, h + 1)
                    if not first:
                        dve.wait_ge(yaT_done, h)
                    for t in range(T):
                        dve.scalar_tensor_tensor(out=ya[:, t, :], in0=E[:, t * P:(t + 1) * P], scalar=mx[:, 6 + t:7 + t],
                                                 in1=mo_z[:, t, :], op0=ALU.mult, op1=ALU.mult).then_inc(ya_ready, 1)
                if s == M_YT:
                    dve.wait_ge(ya_hi_ready, h + 1)
                    hd = bass.ds(h, 1)
                    dve.tensor_tensor(ya_lo[:, hd, :], C[:, 0:SEQ].rearrange("p (a n) -> p a n", a=1),
                                      ya_hi[:, hd, :].bitcast(F32), ALU.subtract).then_inc(ya_lo_ready, 1)

            def iteration(h, first):
                for s in range(SLOTS):
                    if first and s == 2 * XU - 6:
                        start_stats()
                    if first and s == 2 * XU - 1:
                        tables()
                    if first and s == 2 * XU:
                        tables_cumulated()
                    if not first:
                        dn_step(s + SLOTS, h - 1)
                    dn_step(s, h, first)
                    mo_step(s, h, first)
                    n = s // 2 + LEAD
                    if s % 2 == 0 and not (first and n < XU):
                        split(n % RING, h * UNITS + n)

            iteration(0, True)
            with dve.Fori(1, H) as h:
                iteration(h, False)

            def tail_split(n):
                if n < FIRST_O + NC * OU - RING:
                    split(n % RING, n)
                else:
                    dve.wait_ge(hi_ready, n + 1)
                    hi, lo = parts(n)
                    dve.tensor_tensor(lo, w_raw[:, n % RING, :], hi.bitcast(F32), ALU.subtract).then_inc(lo_ready, 1)

            def gate_a(c):
                for t in range(T):
                    wait_chunk(dve, t, 3 * H + c, FIRST_A + BU * c + BU - 1)
                    dve.wait_ge(sig_ready, c + 1)
                    dve.tensor_tensor(gate[:, c, t, :], gate[:, c, t, :], pj[c % 2][:, t, :], ALU.mult).then_inc(a_gated, 1)

            def gate_b(c):
                for t in range(T):
                    wait_chunk(dve, t, 3 * H + NC + c, FIRST_B + BU * c + BU - 1)
                    g = gate[:, NC + c, t, :]
                    dve.tensor_tensor(g, g, pj[c % 2][:, t, :], ALU.mult).then_inc(b_gated, 1)
                    dve.wait_ge(b_gated, T * c + t + 1)
                    dve.tensor_tensor(g, g, gate[:, c, t, :], ALU.add).then_inc(merged, 1)

            for c in range(NC):
                for j in range(BU):
                    dn_step(2 * BU * c + 2 * j + SLOTS, H - 1)
                    tail_split(FIRST_A + BU * c + j + LEAD)
                    dn_step(2 * BU * c + 2 * j + 1 + SLOTS, H - 1)
                    if c > 0 and j == 1:
                        gate_a(c - 1)

            def merged_lo(c):
                ps = [dn_ps, mo_ps][c % 2]
                for half in range(2):
                    dve.wait_ge(mT_hi_ready, 2 * c + half + 1)
                    ks = slice(4 * c + 2 * half, 4 * c + 2 * half + 2)
                    dve.tensor_tensor(xt_lo[:, ks, :].rearrange("p k t -> p (k t)"), ps[:, half * CH:(half + 1) * CH],
                                      xt_hi[:, ks, :].rearrange("p k t -> p (k t)").bitcast(F32),
                                      ALU.subtract).then_inc(mT_lo_ready, 1)

            for n in range(NC * BU):
                tail_split(FIRST_B + n + LEAD)
                if n == 0:
                    gate_a(NC - 1)
                if n % BU == 0 and n > 0:
                    gate_b(n // BU - 1)
                if n % BU == 2 and n > BU:
                    merged_lo(n // BU - 1)

            def residual(c, t):
                dve.wait_ge(x_again[c], 16)
                wait_chunk(dve, t, 3 * H + 2 * NC + c, FIRST_O + OU * c + OU - 1)
                g = gate[:, c, t, :]
                dve.tensor_tensor(g, g, pj[c % 2][:, t, :], ALU.add).then_inc(sum_ready, 1)

            fg = gate[:, NC:NC + NC // 2, :, :].rearrange("p c t n -> p (c t n)")
            for n in range(NC * OU - LEAD):
                tail_split(FIRST_O + n + LEAD)
                if n == 0:
                    gate_b(NC - 1)
                if n == 3:
                    merged_lo(NC - 1)
                if n % OU == 0 and n > 0:
                    residual(n // OU - 1, 0)
                    residual(n // OU - 1, 1)
            c = NC - 1
            for t in range(T):
                residual(c, t)
                dve.wait_ge(gain_landed, 16)
                dve.wait_ge(sum_ready, T * c + t + 1)
                dve.tensor_tensor(last[:, t, :], gate[:, c, t, :], fg[:, c * CH:D], ALU.mult).then_inc(last_gained, 1)
                dve.wait_ge(f_squared, T * c + t + 1)
                dve.tensor_reduce(fr[:, 0, t:t + 1], fs[:, t, :], AX_X, ALU.add).then_inc(f_total, 1)
                dve.wait_ge(f_total, t + 1)
                dve.tensor_scalar(fr[:, 1, t:t + 1], fr[:, 0, t:t + 1], 1.0 / D, EPS, ALU.mult, ALU.add).then_inc(f_mean, 1)
                dve.wait_ge(fr_ready, t + 1)
                dve.wait_ge(f_gained, T * (NC - 1))
                g = gate[:, t:NC - 1, t, :]
                dve.tensor_scalar(g, g, fr[:, 2, t:t + 1], None, ALU.mult).then_inc(y_dve, 1)
                dve.wait_ge(last_gained, t + 1)
                dve.tensor_scalar(last[:, t, :], last[:, t, :], fr[:, 2, t:t + 1], None, ALU.mult).then_inc(y_dve, 1)


_INS = ['x', 'norm_gain', 'w_in', 'conv_w', 'a_log', 'dt_bias', 'dn_norm_gain', 'w_branch_a', 'w_branch_b',
        'w_out', 'final_norm_gain']


def kernel(**inputs):
    import numpy as _np
    import concourse.bacc as _bacc
    from concourse import mybir as _mybir
    from concourse.bass_utils import run_bass_kernel_spmd as _run

    nc = _bacc.Bacc("TRN2", target_bir_lowering=False, num_devices=1)
    arrays, args = {}, []
    for name in _INS:
        a = _np.ascontiguousarray(inputs[name])
        if name != 'final_norm_gain':
            a = a[0]
        arrays[f"in_{name}_dram"] = a
        args.append(nc.dram_tensor(f"in_{name}_dram", a.shape, _mybir.dt.from_np(a.dtype), kind="ExternalInput").ap())
    o = nc.dram_tensor("out_dram", (SEQ, D), F32, kind="ExternalOutput").ap()
    build(nc, *args, o)
    r = _run(nc, [arrays], core_ids=[0])
    return r.results[0]["out_dram"].reshape(1, SEQ, D)
```
